# Optimizing a Trainium2 kernel written in Bass

```python
import jax, jax.numpy as jnp
from jax import lax
import numpy as np

D_MODEL = 1024
BATCH = 1
SEQ = 256
DEPTH = 2

CHUNK = 64
N_A_LAYERS = DEPTH // 2
N_B_LAYERS = DEPTH - N_A_LAYERS
A_HEADS = 8
A_KEY_DIM = 128
A_VAL_DIM = D_MODEL // A_HEADS
A_FORGET_DIM = A_HEADS * A_KEY_DIM
A_IN_DIM = 2 * A_FORGET_DIM + 2 * D_MODEL
B_HEADS = 16
B_HEAD_DIM = D_MODEL // B_HEADS
B_DIM = B_HEADS * B_HEAD_DIM
B_PAST_CHUNKS = 8
B_BAND = (B_PAST_CHUNKS + 1) * CHUNK
REL_CLIP = 256
N_REL = REL_CLIP + CHUNK
FFN_DIM = -(-8 * D_MODEL // (3 * 256)) * 256
NORM_EPS = 1e-6
N_MOD = 6
MASK_VALUE = -1e30
MIN_FORGET = 1e-30


def rms_norm(x, gain):
    xf = x.astype(jnp.float32)
    y = xf * lax.rsqrt(jnp.mean(xf * xf, axis=-1, keepdims=True) + NORM_EPS)
    return (y * gain.astype(jnp.float32)).astype(x.dtype)

def modulate(x, shift, scale):
    return x * (1 + scale[:, None, :]) + shift[:, None, :]

def swiglu(u, w_in, w_out):
    gate, up = jnp.split(u @ w_in, 2, axis=-1)
    return (jax.nn.silu(gate) * up) @ w_out

def hgrn2_mixer(u, w_in, w_out, lb, o_gain):
    bsz, seq, _ = u.shape
    n_chunks = seq // CHUNK
    q, z_f, v, g = jnp.split(u @ w_in, [A_FORGET_DIM, 2 * A_FORGET_DIM, 2 * A_FORGET_DIM + D_MODEL], axis=-1)
    q = jax.nn.silu(q)
    zf = z_f.astype(jnp.float32)
    lbf = lb.astype(jnp.float32)
    sig = jax.nn.sigmoid(zf)
    f = lbf + (1 - lbf) * sig
    log_f = jnp.log(jnp.maximum(f, MIN_FORGET))
    k = (1 - lbf) * (1 - sig)

    def to_chunks(t, d):
        return t.astype(jnp.float32).reshape(bsz, n_chunks, CHUNK, A_HEADS, d).transpose(1, 0, 2, 3, 4)

    xs = (to_chunks(q, A_KEY_DIM), to_chunks(k, A_KEY_DIM), to_chunks(v, A_VAL_DIM), to_chunks(log_f, A_KEY_DIM))
    causal = jnp.tril(jnp.ones((CHUNK, CHUNK), dtype=bool))

    def step(state, chunk):
        qc, kc, vc, lfc = chunk
        b = jnp.cumsum(lfc, axis=1)
        diff = b[:, :, None] - b[:, None, :]
        decay = jnp.exp(jnp.where(causal[None, :, :, None, None], diff, MASK_VALUE))
        attn = jnp.einsum('bthd,btshd,bshd->bhts', qc, decay, kc)
        o = (jnp.einsum('bhts,bshv->bthv', attn, vc)
             + jnp.einsum('bthd,bhdv->bthv', qc * jnp.exp(b), state))
        b_last = b[:, -1]
        state = (jnp.exp(b_last)[..., None] * state
                 + jnp.einsum('bshd,bshv->bhdv', kc * jnp.exp(b_last[:, None] - b), vc))
        return state, o

    state0 = jnp.zeros((bsz, A_HEADS, A_KEY_DIM, A_VAL_DIM), jnp.float32)
    _, o = lax.scan(step, state0, xs)
    o = o.transpose(1, 0, 2, 3, 4).reshape(bsz, seq, A_HEADS, A_VAL_DIM)
    o = o * lax.rsqrt(jnp.mean(o * o, axis=-1, keepdims=True) + NORM_EPS) * o_gain.astype(jnp.float32)
    o = o * jax.nn.silu(g.astype(jnp.float32)).reshape(bsz, seq, A_HEADS, A_VAL_DIM)
    return o.reshape(bsz, seq, D_MODEL).astype(u.dtype) @ w_out

def shared_kv(h, c_act, gain, mod_w, mod_b, w_kv):
    bsz, seq, _ = h.shape
    shift, scale = jnp.split(c_act @ mod_w + mod_b, 2, axis=-1)
    u = modulate(rms_norm(h, gain), shift, scale)
    k, v = jnp.split(u @ w_kv, 2, axis=-1)
    pad = ((0, 0), (B_PAST_CHUNKS * CHUNK, 0), (0, 0), (0, 0))
    k = jnp.pad(k.reshape(bsz, seq, B_HEADS, B_HEAD_DIM), pad)
    v = jnp.pad(v.reshape(bsz, seq, B_HEADS, B_HEAD_DIM), pad)
    return k, v

def chunk_band_attention(u, k_pad, v_pad, w_q, w_o, rel_bias):
    bsz, seq, _ = u.shape
    n_chunks = seq // CHUNK
    q = (u @ w_q).reshape(bsz, n_chunks, CHUNK, B_HEADS, B_HEAD_DIM).transpose(1, 0, 2, 3, 4)
    q_pos = jnp.arange(CHUNK)[:, None] + B_PAST_CHUNKS * CHUNK
    k_pos = jnp.arange(B_BAND)
    rel = jnp.clip(k_pos[None, :] - q_pos, -REL_CLIP, CHUNK - 1) + REL_CLIP
    bias = rel_bias.astype(jnp.float32)[rel].transpose(2, 0, 1)
    scale = B_HEAD_DIM ** -0.5

    def one_chunk(args):
        qc, idx = args
        kb = lax.dynamic_slice_in_dim(k_pad, idx * CHUNK, B_BAND, axis=1)
        vb = lax.dynamic_slice_in_dim(v_pad, idx * CHUNK, B_BAND, axis=1)
        s = jnp.einsum('bqhd,bkhd->bhqk', qc, kb).astype(jnp.float32) * scale + bias
        valid = k_pos >= (B_PAST_CHUNKS - idx) * CHUNK
        s = jnp.where(valid, s, MASK_VALUE)
        p = jax.nn.softmax(s, axis=-1).astype(vb.dtype)
        return jnp.einsum('bhqk,bkhd->bqhd', p, vb)

    o = lax.map(one_chunk, (q, jnp.arange(n_chunks)))
    o = o.transpose(1, 0, 2, 3, 4).reshape(bsz, seq, B_DIM)
    return o @ w_o

def first_inputs(seed: int = 0) -> dict:
    key = jax.random.key(seed)
    ks = jax.random.split(key, 24)
    f32 = jnp.float32
    nrm = lambda k, shape, s: jax.random.normal(k, shape, f32) * s
    D = D_MODEL
    return {
        "x": nrm(ks[0], (BATCH, SEQ, D), 1.0),
        "c": nrm(ks[1], (BATCH, D), 1.0),
        "mod_w": nrm(ks[2], (DEPTH, D, N_MOD * D), 0.5 * D ** -0.5),
        "mod_b": nrm(ks[3], (DEPTH, N_MOD * D), 0.02),
        "norm_mix": 1.0 + nrm(ks[4], (DEPTH, D), 0.02),
        "norm_ffn": 1.0 + nrm(ks[5], (DEPTH, D), 0.02),
        "ffn_w_in": nrm(ks[6], (DEPTH, D, 2 * FFN_DIM), D ** -0.5),
        "ffn_w_out": nrm(ks[7], (DEPTH, FFN_DIM, D), FFN_DIM ** -0.5),
        "a_w_in": nrm(ks[8], (N_A_LAYERS, D, A_IN_DIM), D ** -0.5),
        "a_w_out": nrm(ks[9], (N_A_LAYERS, D, D), D ** -0.5),
        "a_lb": nrm(ks[10], (N_A_LAYERS, A_FORGET_DIM), 1.0),
        "a_out_norm": 1.0 + nrm(ks[11], (N_A_LAYERS, A_VAL_DIM), 0.02),
        "kv_norm": 1.0 + nrm(ks[12], (D,), 0.02),
        "kv_mod_w": nrm(ks[13], (D, 2 * D), 0.5 * D ** -0.5),
        "kv_mod_b": nrm(ks[14], (2 * D,), 0.02),
        "kv_w": nrm(ks[15], (D, 2 * B_DIM), D ** -0.5),
        "b_w_q": nrm(ks[16], (N_B_LAYERS, D, B_DIM), D ** -0.5),
        "b_w_o": nrm(ks[17], (N_B_LAYERS, B_DIM, D), B_DIM ** -0.5),
        "b_rel_bias": nrm(ks[18], (N_B_LAYERS, N_REL, B_HEADS), 0.5),
        "final_norm": 1.0 + nrm(ks[19], (D,), 0.02),
    }

def first_block(x, c, mod_w, mod_b, norm_mix, norm_ffn, ffn_w_in, ffn_w_out,
              a_w_in, a_w_out, a_lb, a_out_norm,
              kv_norm, kv_mod_w, kv_mod_b, kv_w,
              b_w_q, b_w_o, b_rel_bias, final_norm):
    c_act = jax.nn.silu(c)
    sm = jax.nn.softmax(a_lb.astype(jnp.float32), axis=0)
    lower_bounds = jnp.cumsum(sm, axis=0) - sm[0]
    h = x
    k_pad = None
    v_pad = None
    for layer in range(DEPTH):
        mod = c_act @ mod_w[layer] + mod_b[layer]
        sh1, sc1, g1, sh2, sc2, g2 = jnp.split(mod, N_MOD, axis=-1)
        u = modulate(rms_norm(h, norm_mix[layer]), sh1, sc1)
        if layer < N_A_LAYERS:
            mix = hgrn2_mixer(u, a_w_in[layer], a_w_out[layer], lower_bounds[layer], a_out_norm[layer])
        else:
            j = layer - N_A_LAYERS
            mix = chunk_band_attention(u, k_pad, v_pad, b_w_q[j], b_w_o[j], b_rel_bias[j])
        h = h + g1[:, None, :] * mix
        u = modulate(rms_norm(h, norm_ffn[layer]), sh2, sc2)
        h = h + g2[:, None, :] * swiglu(u, ffn_w_in[layer], ffn_w_out[layer])
        if layer == N_A_LAYERS - 1:
            k_pad, v_pad = shared_kv(h, c_act, kv_norm, kv_mod_w, kv_mod_b, kv_w)
    return rms_norm(h, final_norm)


DEPTH_2 = 1

MEM_LEN = 256
EPS = 1e-6
HEAD_DIM = 64
ATTN_WIDTH = D_MODEL // 2
ATTN_Q_HEADS = ATTN_WIDTH // HEAD_DIM
ATTN_KV_HEADS = 2
ATTN_REP = ATTN_Q_HEADS // ATTN_KV_HEADS
KV_WIDTH = ATTN_KV_HEADS * HEAD_DIM
WINDOW = 128
ATTN_BLOCK = 128
SGU_WIDTH = D_MODEL - ATTN_WIDTH
SGU_GROUP_DIM = 64
SGU_GROUPS = SGU_WIDTH // SGU_GROUP_DIM
SGU_CHUNK = 128
IN_WIDTH = ATTN_WIDTH + 2 * KV_WIDTH + 2 * SGU_WIDTH
X_HEADS = 4
X_HEAD_DIM = D_MODEL // X_HEADS
N_GROUPS = 4
EXPERTS_PER_GROUP = 8
N_EXPERTS = N_GROUPS * EXPERTS_PER_GROUP
TOP_K = 2
D_EXPERT = D_MODEL // 2
MOE_BLOCK = 256


def rms_norm_2(x, gain):
    xf = x.astype(jnp.float32)
    y = xf * lax.rsqrt(jnp.mean(xf * xf, axis=-1, keepdims=True) + EPS)
    return (y * gain.astype(jnp.float32)).astype(x.dtype)

def sliding_window_attention(q, k, v, sinks):
    B, S = q.shape[:2]
    nb = S // ATTN_BLOCK
    qb = q.reshape(B, nb, ATTN_BLOCK, ATTN_KV_HEADS, ATTN_REP, HEAD_DIM).astype(jnp.float32)
    kb = k.reshape(B, nb, ATTN_BLOCK, ATTN_KV_HEADS, HEAD_DIM)
    vb = v.reshape(B, nb, ATTN_BLOCK, ATTN_KV_HEADS, HEAD_DIM)
    pad = ((0, 0), (1, 0), (0, 0), (0, 0), (0, 0))
    kwin = jnp.concatenate([jnp.pad(kb, pad)[:, :-1], kb], axis=2).astype(jnp.float32)
    vwin = jnp.concatenate([jnp.pad(vb, pad)[:, :-1], vb], axis=2).astype(jnp.float32)
    scores = jnp.einsum('bnqhrd,bnkhd->bnhrqk', qb, kwin) * (HEAD_DIM ** -0.5)
    qi = jnp.arange(ATTN_BLOCK)[:, None]
    kj = jnp.arange(2 * ATTN_BLOCK)[None, :]
    dist = qi + ATTN_BLOCK - kj
    band = (dist >= 0) & (dist < WINDOW)
    key_pos = jnp.arange(nb)[:, None, None] * ATTN_BLOCK + kj[None] - ATTN_BLOCK
    mask = band[None] & (key_pos >= 0)
    scores = jnp.where(mask[None, :, None, None], scores, jnp.finfo(jnp.float32).min)
    sink = sinks.astype(jnp.float32).reshape(ATTN_KV_HEADS, ATTN_REP)[None, None, :, :, None, None]
    m = jnp.maximum(jnp.max(scores, axis=-1, keepdims=True), sink)
    p = jnp.exp(scores - m)
    denom = jnp.sum(p, axis=-1, keepdims=True) + jnp.exp(sink - m)
    out = jnp.einsum('bnhrqk,bnkhd->bnqhrd', p / denom, vwin)
    return out.reshape(B, S, ATTN_WIDTH).astype(q.dtype)

def spatial_gating(u, v, sgu_norm, sgu_w, sgu_b):
    B, S = u.shape[:2]
    nc = S // SGU_CHUNK
    vc = rms_norm_2(v, sgu_norm).reshape(B, nc, SGU_CHUNK, SGU_GROUPS, SGU_GROUP_DIM)
    causal = jnp.tril(jnp.ones((SGU_CHUNK, SGU_CHUNK), dtype=bool))
    w = jnp.where(causal[None], sgu_w, jnp.zeros((), sgu_w.dtype))
    s = jnp.einsum('gij,bcjgd->bcigd', w, vc) + sgu_b.T[None, None, :, :, None]
    return u * s.reshape(B, S, SGU_WIDTH)

def memory_cross_attention(h, mem_n, w_cq, w_ck, w_cv, cq_norm, ck_norm, w_co):
    B, S = h.shape[:2]
    M = mem_n.shape[1]
    q = rms_norm_2((h @ w_cq).reshape(B, S, X_HEADS, X_HEAD_DIM), cq_norm)
    k = rms_norm_2((mem_n @ w_ck).reshape(B, M, X_HEADS, X_HEAD_DIM), ck_norm)
    v = (mem_n @ w_cv).reshape(B, M, X_HEADS, X_HEAD_DIM)
    scores = jnp.einsum('bshd,bmhd->bhsm', q.astype(jnp.float32), k.astype(jnp.float32)) * (X_HEAD_DIM ** -0.5)
    p = jax.nn.softmax(scores, axis=-1)
    out = jnp.einsum('bhsm,bmhd->bshd', p, v.astype(jnp.float32)).astype(h.dtype)
    return out.reshape(B, S, D_MODEL) @ w_co

def hierarchical_moe(h, w_router_group, w_router_expert, w1, w3, w2):
    B, S, D = h.shape
    T = B * S
    xt = h.reshape(T, D)
    xf = xt.astype(jnp.float32)
    p_group = jax.nn.softmax(xf @ w_router_group.astype(jnp.float32), axis=-1)
    g_idx = jnp.argmax(p_group, axis=-1)
    g_w = jnp.take_along_axis(p_group, g_idx[:, None], axis=1)[:, 0]
    local = jnp.einsum('td,gde->tge', xf, w_router_expert.astype(jnp.float32))
    local = jnp.take_along_axis(local, g_idx[:, None, None], axis=1)[:, 0]
    top_logit, top_idx = lax.top_k(local, TOP_K)
    gate = jax.nn.softmax(top_logit, axis=-1) * g_w[:, None]
    flat_e = (g_idx[:, None] * EXPERTS_PER_GROUP + top_idx).reshape(-1).astype(jnp.int32)
    flat_w = gate.reshape(-1)
    A = T * TOP_K
    order = jnp.argsort(flat_e)
    sorted_e = flat_e[order]
    counts = jnp.zeros((N_EXPERTS,), jnp.int32).at[flat_e].add(1)
    starts = jnp.cumsum(counts) - counts
    padded = (counts + MOE_BLOCK - 1) // MOE_BLOCK * MOE_BLOCK
    pad_end = jnp.cumsum(padded)
    pad_start = pad_end - padded
    dest = pad_start[sorted_e] + jnp.arange(A, dtype=jnp.int32) - starts[sorted_e]
    nb = -(-A // MOE_BLOCK) + N_EXPERTS
    P = nb * MOE_BLOCK
    slot_tok = jnp.full((P,), T, jnp.int32).at[dest].set((order // TOP_K).astype(jnp.int32))
    slot_w = jnp.zeros((P,), jnp.float32).at[dest].set(flat_w[order])
    block_e = jnp.minimum(jnp.searchsorted(pad_end, jnp.arange(nb, dtype=jnp.int32) * MOE_BLOCK, side='right'), N_EXPERTS - 1)
    x_pad = jnp.concatenate([xt, jnp.zeros((1, D), xt.dtype)], axis=0)
    xb = x_pad[slot_tok].reshape(nb, MOE_BLOCK, D)

    def run_block(args):
        xblk, e = args
        hid = jax.nn.silu(xblk @ w1[e]) * (xblk @ w3[e])
        return hid @ w2[e]

    yb = lax.map(run_block, (xb, block_e)).reshape(P, D)
    y = jnp.zeros((T + 1, D), jnp.float32).at[slot_tok].add(yb.astype(jnp.float32) * slot_w[:, None])[:T]
    return y.astype(h.dtype).reshape(B, S, D)

def second_inputs(seed: int = 0) -> dict:
    key = jax.random.key(seed)
    ks = jax.random.split(key, 32)
    f32 = jnp.float32
    nrm = lambda k, shape, s: jax.random.normal(k, shape, f32) * s
    gain = lambda k, n: 1.0 + 0.02 * jax.random.normal(k, (n,), f32)
    return {
        "x": nrm(ks[0], (BATCH, SEQ, D_MODEL), 1.0),
        "mem": nrm(ks[1], (BATCH, MEM_LEN, D_MODEL), 1.0),
        "norm_mix": gain(ks[2], D_MODEL),
        "w_in": nrm(ks[3], (D_MODEL, IN_WIDTH), D_MODEL ** -0.5),
        "q_norm": gain(ks[4], HEAD_DIM),
        "k_norm": gain(ks[5], HEAD_DIM),
        "attn_sinks": nrm(ks[6], (ATTN_Q_HEADS,), 0.5),
        "sgu_norm": gain(ks[7], SGU_WIDTH),
        "sgu_w": nrm(ks[8], (SGU_GROUPS, SGU_CHUNK, SGU_CHUNK), SGU_CHUNK ** -0.5),
        "sgu_b": 1.0 + nrm(ks[9], (SGU_GROUPS, SGU_CHUNK), 0.1),
        "out_norm_attn": gain(ks[10], ATTN_WIDTH),
        "out_norm_sgu": gain(ks[11], SGU_WIDTH),
        "w_out": nrm(ks[12], (D_MODEL, D_MODEL), D_MODEL ** -0.5),
        "norm_cross": gain(ks[13], D_MODEL),
        "norm_mem": gain(ks[14], D_MODEL),
        "w_cq": nrm(ks[15], (D_MODEL, D_MODEL), D_MODEL ** -0.5),
        "w_ck": nrm(ks[16], (D_MODEL, D_MODEL), D_MODEL ** -0.5),
        "w_cv": nrm(ks[17], (D_MODEL, D_MODEL), D_MODEL ** -0.5),
        "cq_norm": gain(ks[18], X_HEAD_DIM),
        "ck_norm": gain(ks[19], X_HEAD_DIM),
        "w_co": nrm(ks[20], (D_MODEL, D_MODEL), D_MODEL ** -0.5),
        "norm_ffn": gain(ks[21], D_MODEL),
        "w_router_group": nrm(ks[22], (D_MODEL, N_GROUPS), D_MODEL ** -0.5),
        "w_router_expert": nrm(ks[23], (N_GROUPS, D_MODEL, EXPERTS_PER_GROUP), D_MODEL ** -0.5),
        "w1": nrm(ks[24], (N_EXPERTS, D_MODEL, D_EXPERT), D_MODEL ** -0.5),
        "w3": nrm(ks[25], (N_EXPERTS, D_MODEL, D_EXPERT), D_MODEL ** -0.5),
        "w2": nrm(ks[26], (N_EXPERTS, D_EXPERT, D_MODEL), D_EXPERT ** -0.5),
    }

def second_block(x, mem, norm_mix, w_in, q_norm, k_norm, attn_sinks, sgu_norm, sgu_w, sgu_b,
              out_norm_attn, out_norm_sgu, w_out, norm_cross, norm_mem, w_cq, w_ck, w_cv,
              cq_norm, ck_norm, w_co, norm_ffn, w_router_group, w_router_expert, w1, w3, w2):
    B, S = x.shape[:2]
    mem_n = rms_norm_2(mem, norm_mem)
    for _ in range(DEPTH_2):
        h = rms_norm_2(x, norm_mix)
        proj = h @ w_in
        c0 = ATTN_WIDTH
        c1 = c0 + KV_WIDTH
        c2 = c1 + KV_WIDTH
        c3 = c2 + SGU_WIDTH
        q = rms_norm_2(proj[..., :c0].reshape(B, S, ATTN_Q_HEADS, HEAD_DIM), q_norm)
        k = rms_norm_2(proj[..., c0:c1].reshape(B, S, ATTN_KV_HEADS, HEAD_DIM), k_norm)
        v = proj[..., c1:c2].reshape(B, S, ATTN_KV_HEADS, HEAD_DIM)
        u = jax.nn.gelu(proj[..., c2:c3])
        g = jax.nn.gelu(proj[..., c3:])
        attn = sliding_window_attention(q, k, v, attn_sinks)
        sg = spatial_gating(u, g, sgu_norm, sgu_w, sgu_b)
        mixed = jnp.concatenate([rms_norm_2(attn, out_norm_attn), rms_norm_2(sg, out_norm_sgu)], axis=-1)
        x = x + mixed @ w_out
        x = x + memory_cross_attention(rms_norm_2(x, norm_cross), mem_n, w_cq, w_ck, w_cv, cq_norm, ck_norm, w_co)
        x = x + hierarchical_moe(rms_norm_2(x, norm_ffn), w_router_group, w_router_expert, w1, w3, w2)
    return x


def setup_inputs(seed=0):
    out = dict(first_inputs(seed))
    for name, value in second_inputs(seed + 1).items():
        if name != "x":
            out[name + "_2"] = value
    return out


def reference(
    x, c, mod_w, mod_b, norm_mix, norm_ffn, ffn_w_in, ffn_w_out, a_w_in, a_w_out, a_lb,
    a_out_norm, kv_norm, kv_mod_w, kv_mod_b, kv_w, b_w_q, b_w_o, b_rel_bias, final_norm, mem_2,
    norm_mix_2, w_in_2, q_norm_2, k_norm_2, attn_sinks_2, sgu_norm_2, sgu_w_2, sgu_b_2,
    out_norm_attn_2, out_norm_sgu_2, w_out_2, norm_cross_2, norm_mem_2, w_cq_2, w_ck_2, w_cv_2,
    cq_norm_2, ck_norm_2, w_co_2, norm_ffn_2, w_router_group_2, w_router_expert_2, w1_2, w3_2,
    w2_2,
):
    x = first_block(
        x, c, mod_w, mod_b, norm_mix, norm_ffn, ffn_w_in, ffn_w_out, a_w_in, a_w_out, a_lb,
        a_out_norm, kv_norm, kv_mod_w, kv_mod_b, kv_w, b_w_q, b_w_o, b_rel_bias, final_norm,
    )
    return second_block(
        x, mem_2, norm_mix_2, w_in_2, q_norm_2, k_norm_2, attn_sinks_2, sgu_norm_2, sgu_w_2,
        sgu_b_2, out_norm_attn_2, out_norm_sgu_2, w_out_2, norm_cross_2, norm_mem_2, w_cq_2,
        w_ck_2, w_cv_2, cq_norm_2, ck_norm_2, w_co_2, norm_ffn_2, w_router_group_2,
        w_router_expert_2, w1_2, w3_2, w2_2,
    )


_drawn_inputs = setup_inputs


def setup_inputs(seed=0):
    import zlib

    import numpy as np

    out = dict(_drawn_inputs(seed))
    spreads = {}
    factors = {'norm_mix': 2.833,
     'a_out_norm': 3.177,
     'kv_norm': 8.0,
     'q_norm_2': 2.971,
     'attn_sinks_2': 3.686,
     'sgu_norm_2': 5.084,
     'norm_cross_2': 8.0,
     'norm_mem_2': 6.437,
     'cq_norm_2': 8.0,
     'ck_norm_2': 8.0,
     'norm_ffn_2': 8.0}
    for name, (base, spread) in spreads.items():
        noise = np.random.default_rng([zlib.crc32(name.encode()), seed]).standard_normal(out[name].shape)
        drawn = base * np.exp(spread * noise) if base else spread * noise
        out[name] = __import__('jax').numpy.asarray(drawn.astype(out[name].dtype))
    for name, factor in factors.items():
        out[name] = (out[name] * factor).astype(out[name].dtype)
    return out
```

```python
from contextlib import ExitStack

import concourse.bass as bass
from concourse import mybir

P = 128
ALU = mybir.AluOpType
ACT = mybir.ActivationFunctionType
F32 = mybir.dt.float32
F32R = mybir.dt.float32r
I32 = mybir.dt.int32
U8 = mybir.dt.uint8
AX = mybir.AxisListType.X

D = 1024
DC = D // P
T = 256
TB = T // P
FFN = 2816
FFI = FFN // 256
HA = 8
HB = 16
NREL = 320
HW = 8
HX = 4
NE = 32
NGROUP = 4
PER = NE // NGROUP
DE = 512
CAP = 64
EPS = 1e-6
MIN_FORGET = 1e-30
MASKED = -1e30

RING = 6
SLOT = 2048
NBUF = 4
LOOKAHEAD = NBUF - 1

MOD0, MODKV, MOD1 = 0, 48, 64
VEC = {}


def table2():
    at = 0
    for name, rows in (("norm_mix", 16), ("norm_ffn", 16), ("a_lb", 8), ("kv_norm", 8), ("final_norm", 8),
                       ("norm_mix_2", 8), ("norm_cross_2", 8), ("norm_mem_2", 8), ("norm_ffn_2", 8),
                       ("a_out_norm", 1), ("out_norm_attn_2", 4), ("out_norm_sgu_2", 4), ("cq_norm_2", 2),
                       ("ck_norm_2", 2), ("c", 8)):
        VEC[name] = at
        at += rows
    VEC["q_norm_2"], VEC["k_norm_2"] = at, at + 1
    return at + 2


ROWS2 = table2()


def plan():
    slots, pieces, jobs = [], [], {}
    turn = {"act": 0, "dve": 0}
    outs = []

    def slot(kind, matrix, at):
        slots.append({"kind": kind, "matrix": matrix, "at": at, "n": len(slots)})
        return slots[-1]

    def gemv(name, matrix, n):
        jobs[name] = [slot("gemv", matrix, 256 * i) for i in range(n)]

    def piece(s, half, job, engine=None):
        p = {"w": len(pieces), "slot": s["n"], "half": half, "engine": engine}
        if engine:
            if half == 0:
                outs.append(engine)
                turn[engine] += 1
            n = len(outs) - 1
            p["out"], p["turn"] = n, turn[engine]
            p["engine_before"] = outs[n - 2] if n >= 2 else None
            p["turn_before"] = outs[:n - 1].count(outs[n - 2]) if n >= 2 else 0
        s.setdefault("pieces", []).append(p["w"])
        pieces.append(p)
        jobs.setdefault(job, []).append(p)
        return p

    def linear(job, matrix, first, n, engine):
        for i in range(n):
            s = slot("lin", matrix, first + 256 * i)
            for half in range(2):
                piece(s, half, job, engine)

    def ffn(layer, with_gemv):
        for i in range(FFI + 1):
            if i < FFI:
                for part, engine in (("gate", "act"), ("up", "dve")):
                    s = slot("lin", f"ffn_in{layer}", 256 * i + (FFN if part == "up" else 0))
                    for half in range(2):
                        piece(s, half, f"{part}{layer}_{i}", engine)
            if i > 0:
                s = slot("out", f"ffn_out{layer}", 256 * (i - 1))
                for half in range(2):
                    piece(s, half, f"down{layer}_{i - 1}")
            if with_gemv:
                gemv(f"gemv_ffn{i}", "mod1", 2)
                for k, s in enumerate(jobs[f"gemv_ffn{i}"]):
                    s["at"] = 256 * (2 * i + k)

    gemv("gemv_first", "mod0", 8)
    linear("zf", "a_in", D, 4, "act")
    linear("q", "a_in", 0, 4, "act")
    for r in range(8):
        part, first = ("v", 2 * D) if r < 4 else ("g", 3 * D)
        linear(part + str(r), "a_in", first + 256 * (r % 4), 1, "act")
        gemv(f"gemv_round{r}", "mod0", 2)
        for k, s in enumerate(jobs[f"gemv_round{r}"]):
            s["at"] = 2048 + 256 * (2 * r + k)
    linear("a_out", "a_out", 0, 4, "dve")
    gemv("gemv_kv", "modkv", 8)
    ffn(0, True)
    linear("kv_k", "kv", 0, 4, "act")
    linear("kv_v", "kv", D, 4, "act")
    linear("b_q", "b_q", 0, 4, "act")
    linear("b_o", "b_o", 0, 4, "dve")
    ffn(1, False)
    linear("in2", "in2", 0, 7, "act")
    linear("out2", "out2", 0, 4, "dve")
    linear("ck", "ck", 0, 4, "act")
    linear("cv", "cv", 0, 4, "act")
    linear("cq", "cq", 0, 4, "act")
    linear("co", "co", 0, 4, "dve")
    return slots, pieces, jobs


def two_blocks(nc, x, c, mod_w, mod_b, norm_mix, norm_ffn, ffn_w_in, ffn_w_out, a_w_in, a_w_out, a_lb,
               a_out_norm, kv_norm, kv_mod_w, kv_mod_b, kv_w, b_w_q, b_w_o, b_rel_bias, final_norm, mem_2,
               norm_mix_2, w_in_2, q_norm_2, k_norm_2, attn_sinks_2, sgu_norm_2, sgu_w_2, sgu_b_2,
               out_norm_attn_2, out_norm_sgu_2, w_out_2, norm_cross_2, norm_mem_2, w_cq_2, w_ck_2, w_cv_2,
               cq_norm_2, ck_norm_2, w_co_2, norm_ffn_2, w_router_group_2, w_router_expert_2, w1_2, w3_2,
               w2_2, out):
    slots, pieces, jobs = plan()
    matrices = {"mod0": mod_w[0], "mod1": mod_w[1], "modkv": kv_mod_w, "a_in": a_w_in[0], "a_out": a_w_out[0],
                "ffn_in0": ffn_w_in[0], "ffn_in1": ffn_w_in[1], "ffn_out0": ffn_w_out[0],
                "ffn_out1": ffn_w_out[1], "kv": kv_w, "b_q": b_w_q[0], "b_o": b_w_o[0], "in2": w_in_2,
                "out2": w_out_2, "ck": w_ck_2, "cv": w_cv_2, "cq": w_cq_2, "co": w_co_2}
    gemv_of = {}
    for s in slots:
        if s["kind"] == "gemv":
            gemv_of[s["n"]] = len(gemv_of)
    NG = len(gemv_of)

    with ExitStack() as ctx:
        def sb(name, shape, dt=F32):
            return ctx.enter_context(nc.sbuf_tensor(name, shape, dt))

        def sem(name):
            return ctx.enter_context(nc.semaphore(name))

        ARENA = RING * SLOT + 19456
        arena = sb("arena", [P, ARENA])

        def part(at, *shape, base=RING * SLOT, rows=P):
            n = 1
            for k in shape:
                n *= k
            assert base + at + n <= ARENA
            flat = arena[0:rows, base + at:base + at + n]
            if len(shape) == 1:
                return flat
            names = "abcd"[:len(shape)]
            return flat.rearrange(f"p ({' '.join(names)}) -> p {' '.join(names)}",
                                  **{k: v for k, v in zip(names, shape)})

        ring = [arena[:, SLOT * n:SLOT * (n + 1)] for n in range(RING)]
        wsplit = sb("wsplit", [P, NBUF, 2, 1024], F32R)
        u = sb("u", [P, 2, DC, T], F32R)
        hid = sb("hid", [P, 2, 2, 2, T], F32R)
        h = sb("h", [P, DC, T])
        sq = sb("sq", [P, DC, T])
        vec1 = sb("vec1", [P, 112])
        vec2 = sb("vec2", [P, ROWS2])
        ident = sb("ident", [P, P])
        ones = sb("ones", [P, P])
        mod = sb("mod", [P, 112])
        gain = sb("gain", [P, 5, DC])
        lbs = sb("lbs", [P, 4, HA])
        gsb = sb("gsb", [P, 2, 256])
        cact = sb("cact", [P, DC, 32])
        stat = sb("stat", [P, 64])
        diag = sb("diag", [P, 4, P])
        small = sb("small", [P, 3, 64])

        def vec(name, i=0):
            return vec2[:, VEC[name] + i:VEC[name] + i + 1]

        FP, GS, qA, kA, qd, kd = (part(2048 * i, HA, T) for i in range(6))
        vA = part(12288, TB, D)
        gA = part(14336, HA, T)
        attA = part(16384, HA, 3, P)
        silu_g = part(0, 2, 2, T)
        hidden = part(1024, 2, 2, T)
        qB, kB = part(0, DC, T), part(2048, DC, T)
        vB = part(4096, TB, D)
        biasB = part(6144, HB, 3 * P)
        sc_sb, pr_sb, pt_sb = (part(12288 + 1024 * i, 2, 512) for i in range(3))
        rel_rows = part(15360, 3, HB)
        relT = part(15488, 384)
        q_raw = part(0, 5, T)
        qW = part(1280, 4, T)
        kW = part(2304, T)
        vW = part(2560, TB, P)
        uW = part(2816, 4, T)
        gW = part(3840, TB, 512)
        gn = part(4864, TB, 512)
        wT = part(5888, 8, P)
        wRow = part(6912, 8, P)
        mix = part(7936, DC, T)
        gain_bc = part(9984, 512)
        sgb = part(10496, 1024, rows=1)
        winmask = part(11520, 3, P)
        causal_f = part(11904, P)
        sinks = part(12032, HW)
        memT = part(0, DC, T)
        kX, qX = part(2048, DC, T), part(4096, DC, T)
        vX = part(6144, TB, D)
        raw = part(8192, DC, T)
        x_tok = part(0, TB, D)
        rows1, rows2 = part(2048, P), part(2176, P)
        mem_tok = part(10240, TB, D)

        ps = ctx.enter_context(nc.psum_tensor("ps", [P, 8, 512], F32))
        lin = [ps[:, n, :].rearrange("p (c t) -> p c t", c=2) for n in range(2)]
        acc = ps[:, 2:6, :].rearrange("p b (c t) -> p (b c) t", t=T)
        gps = ps[:, 6, 0:256]
        modps = ps[:, 6, 256:368]
        rbc = ps[:, 7, 0:256]
        stps = ps[:, 7, 256:320]

        slot_in = [sem(f"slot_in{n}") for n in range(RING)]
        hi_done = sem("hi_done")
        lo_done = sem("lo_done")
        piece_done = sem("piece_done")
        lin_out = {"act": sem("lin_out_act"), "dve": sem("lin_out_dve")}
        gemv_mm = sem("gemv_mm")
        gemv_sb = sem("gemv_sb")
        gemv_col = sem("gemv_col")
        mod_done = sem("mod_done")
        ld_x, ld_vec, ld_mem = sem("ld_x"), sem("ld_vec"), sem("ld_mem")
        const_done = sem("const_done")
        setup_t = sem("setup_t")
        setup_c = sem("setup_c")
        act_order = sem("act_order")
        sq_done = sem("sq_done")
        sum_done = sem("sum_done")
        var_done = sem("var_done")
        std_done = sem("std_done")
        rstd_done = sem("rstd_done")
        diag_done = sem("diag_done")
        bc_done = sem("bc_done")
        scaled = sem("scaled")
        u_hi, u_lo = sem("u_hi"), sem("u_lo")

        block = ctx.enter_context(nc.Block())

        def slot_use(n):
            return 16 * (n // RING + 1)

        def slot_src(s):
            w = matrices[s["matrix"]]
            if s["kind"] == "out":
                return w[s["at"]:s["at"] + 256, :].rearrange("(k p) n -> p k n", p=P)
            return w.rearrange("(k p) n -> p k n", p=P)[:, :, s["at"]:s["at"] + 256]

        def slot_dst(s):
            return ring[s["n"] % RING].rearrange("p (k n) -> p k n", k=2 if s["kind"] == "out" else DC)

        def piece_src(p):
            s = slots[p["slot"]]
            if s["kind"] == "out":
                return slot_dst(s)[:, :, 512 * p["half"]:512 * (p["half"] + 1)]
            return slot_dst(s)[:, :, P * p["half"]:P * (p["half"] + 1)]

        def piece_buf(p, lo):
            b = wsplit[:, p["w"] % NBUF, lo, :]
            return b.rearrange("p (k n) -> p k n", k=2 if slots[p["slot"]]["kind"] == "out" else DC)

        def wait_out(eng, p):
            eng.wait_ge(lin_out[p["engine"]], p["turn"])

        STATS = {name: i for i, name in enumerate(
            ("mix0", "ffn0", "kv", "ffn1", "final", "mix_2", "mem", "cross", "moe"))}
        OPERANDS = {name: i for i, name in enumerate(
            ("mix0", "ffn0", "kv", "mix1", "ffn1", "mix_2", "mixed", "mem", "cross"))}
        SCALED_BEFORE = {"ffn0": 1, "kv": 2, "ffn1": 4, "final": 5, "mix_2": 5, "mem": 7, "cross": 8, "moe": 9}
        SQ_FREE = {"mix0": [], "ffn0": [], "kv": [(u_lo, 16)], "ffn1": [(u_lo, 32)], "final": [(u_lo, 40)],
                   "mix_2": [(sum_done, STATS["final"] + 1)], "mem": [(u_lo, 56)], "cross": [(u_lo, 64)],
                   "moe": [(u_lo, 72)]}


        f_hi, f_lo = sem("f_hi"), sem("f_lo")
        acc_done = sem("acc_done")
        res_done = sem("res_done")
        a_prep = sem("a_prep")
        a_init = sem("a_init")
        a_dec = sem("a_dec")
        a_fg = sem("a_fg")
        a_mm = sem("a_mm")
        a_cp = sem("a_cp")
        a_x = sem("a_x")
        a_o = sem("a_o")
        a_sq = sem("a_sq")
        a_ss = sem("a_ss")
        a_var, a_std, a_rs = sem("a_var"), sem("a_std"), sem("a_rs")
        a_diag = sem("a_diag")
        a_bc = sem("a_bc")
        a_t = sem("a_t")
        a_og = sem("a_og")
        a_g = sem("a_g")
        a_hi, a_lo = sem("a_hi"), sem("a_lo")
        out_done = sem("out_done")

        LAST = {job: ps_[-1]["w"] for job, ps_ in jobs.items() if "w" in ps_[-1]}
        masks = sb("masks", [P, 8, P], U8)
        xor_i = part(12288, 3, P)

        def pairs(job):
            return [jobs[job][n:n + 2] for n in range(0, len(jobs[job]), 2)]

        def bank(pair):
            return lin[pair[0]["out"] % 2]

        LEVELS = [1, 2, 4, 8, 16, 32, 64]

        def halves(m, H, upper):
            v = m.rearrange("p h (b two j) -> p (h b) two j", two=2, j=H)
            return v[:, :, 1 if upper else 0, :]

        HEADS = [("B", n) for n in range(HB)] + [("W", n) for n in range(HW)] + [("X", n) for n in range(HX)]
        FIRST = {"B": 0, "W": HB, "X": HB + HW}
        COUNT = {"B": HB, "W": HW, "X": HX}
        SCALE = {"B": 1.0, "W": 0.125, "X": 0.0625}
        at_s = sem("at_s")
        at_b = sem("at_b")
        at_e = sem("at_e")
        at_p = sem("at_p")
        at_t = sem("at_t")
        at_pt = sem("at_pt")
        at_o = sem("at_o")
        at_hi = sem("at_hi")
        at_lo = sem("at_lo")

        def before_b(a):
            return 3 * a + min(max(a - FIRST["W"], 0), HW)

        def runs(kind):
            if kind == "X":
                return slice(0, 256), slice(256, 512), slice(0, 512)
            if kind == "W":
                return slice(0, 129), slice(129, 386), slice(1, 385)
            return slice(0, 128), slice(128, 384), slice(0, 384)

        def blocks(kind):
            if kind == "X":
                return [(0, 0), (128, 2), (256, 1), (384, 3)]
            off = 1 if kind == "W" else 0
            return [(off, 0), (off + 128, 1), (off + 256, 2)]

        def drains(kind, i):
            if kind == "X":
                return 12 + i
            return {"B": 0, "W": 8}[kind] + i // 2 if i % 2 == 1 else None

        def o_bank(kind, i):
            k = 12 + i if kind == "X" else {"B": 0, "W": 8}[kind] + i // 2
            return k, ps[:, 6 + k % 2, :]

        def lo_before(k):
            return k if k <= 8 else 8 + max(k - 12, 0)

        b_rel = sem("b_rel")
        b_relt = sem("b_relt")
        b_zero = sem("b_zero")
        b_bias = sem("b_bias")
        scratch = nc.dram_tensor("rel_by_head", [HB, 3 * P], F32).ap()
        w_ld = sem("w_ld")
        w_ms = sem("w_ms")
        w_tp = sem("w_tp")
        w_tc = sem("w_tc")
        w_sq = sem("w_sq")
        w_ss = sem("w_ss")
        w_std = sem("w_std")
        w_rs = sem("w_rs")
        w_n = sem("w_n")
        w_dup = sem("w_dup")
        w_dc = sem("w_dc")
        w_s = sem("w_s")
        w_sg = sem("w_sg")
        x_tp, x_tc = sem("x_tp"), sem("x_tc")
        x_sq, x_ss, x_std, x_rs, x_n = (sem("x_" + n) for n in ("sq", "ss", "std", "rs", "n"))
        flip = sb("flip", [P, P])
        pair_ones = sb("pair_ones", [P, P])
        kdup = part(15360, 2, T)
        gst = part(15872, 8)
        qk_std = part(12288, 5, T)
        half_std = part(12288, 2, T)
        x_rstd = part(12288, 8, T)
        mem_tok = part(17024, TB, D)
        m_hn = sem("m_hn")
        m_tok = sem("m_tok")
        m_tokc = sem("m_tokc")
        m_const = sem("m_const")
        m_wr = sem("m_wr")
        m_log = sem("m_log")
        m_acc = sem("m_acc")
        route = sem("route")
        route_e = sem("route_e")
        m_rank = sem("m_rank")
        m_flag = sem("m_flag")
        w13_in = [sem("w13_in0"), sem("w13_in1")]
        w2_in = [sem("w2_in0"), sem("w2_in1")]
        m_s = sem("m_s")
        m_g = sem("m_g")
        m_x = sem("m_x")
        m_h = sem("m_h")
        m_si = sem("m_si")
        m_hd = sem("m_hd")
        m_t = sem("m_t")
        m_tc = sem("m_tc")
        m_y = sem("m_y")
        m_yc = sem("m_yc")
        m_all = sem("m_all")
        m_out = sem("m_out")
        wbuf = [arena[:, RING * SLOT:2 * RING * SLOT], arena[:, 0:RING * SLOT]]
        w13 = [b_[:, 0:8192].rearrange("p (m k n) -> p m k n", m=2, k=DC) for b_ in wbuf]
        w2b = [b_[:, 8192:12288].rearrange("p (k n) -> p k n", k=4) for b_ in wbuf]
        hn_tok = part(12288, TB, D)
        xe = part(14336, DC, CAP)
        tt = part(14848, 512)
        y_sb = part(15360, 512)
        silu_e = part(15872, 256)
        hid_e = part(16128, 256)
        sel = part(16384, 2, TB, CAP)
        gate_sel = part(16640, 2, TB, 2 * CAP)
        slot_no = part(17152, 4, 2 * CAP)
        wr = part(17664, DC, NGROUP + NE)
        logits = part(17952, TB, NGROUP + NE)
        tri = part(18048, P)
        M1, M2, R, G = (part(18176 + 64 * i, TB, NE) for i in range(4))
        prod = part(18432, TB, NE)
        og, og_t = part(18496, TB, NGROUP), part(18504, TB, NGROUP)
        o1, o2, loc, loc2, eq8, eq_t = (part(18512 + 16 * i, TB, PER) for i in range(6))
        rs = part(18608, 16, TB)
        flag = part(18640, 4)
        slot_i = part(18688, 4 * 2 * CAP)
        CROSS_DONE = jobs["co"][-1]["turn"]

        def w_expert(w, n):
            return w[bass.ds(n, 1)].rearrange("o (k p) n -> p (o k) n", p=P)
        ROUTED = 39
        @block.sync
        def _(sp):
            sp.dma_start(x_tok, x[0].rearrange("(b p) d -> p b d", p=P)).then_inc(ld_x, 16)
            for s in slots:
                n = s["n"]
                if n >= RING:
                    old = slots[n - RING]
                    if old["kind"] == "gemv":
                        sp.wait_ge(gemv_mm, gemv_of[old["n"]] + 1)
                    else:
                        sp.wait_ge(lo_done, old["pieces"][-1] + 1)
                sp.dma_start(slot_dst(s), slot_src(s)).then_inc(slot_in[n % RING], 16)
            sp.wait_ge(at_lo, 12)
            for n in range(2):
                if n == 1:
                    sp.wait_ge(lo_done, LAST["co"] + 1)
                sp.dma_start(w13[n][:, 0], w_expert(w1_2, n)).then_inc(w13_in[n], 16)
                sp.dma_start(w13[n][:, 1], w_expert(w3_2, n)).then_inc(w13_in[n], 16)
                sp.dma_start(w2b[n], w_expert(w2_2, n)).then_inc(w2_in[n], 16)
            with sp.Fori(0, NE // 2 - 1) as i:
                for b in range(2):
                    sp.wait_ge(m_h, 2 * i + b + 1)
                    sp.dma_start(w13[b][:, 0], w_expert(w1_2, 2 * i + 2 + b)).then_inc(w13_in[b], 16)
                    sp.dma_start(w13[b][:, 1], w_expert(w3_2, 2 * i + 2 + b)).then_inc(w13_in[b], 16)
                    sp.wait_ge(m_y, 2 * i + b + 1)
                    sp.dma_start(w2b[b], w_expert(w2_2, 2 * i + 2 + b)).then_inc(w2_in[b], 16)
            sp.wait_ge(m_flag, 1)
            more = sp.value_load(flag[0:1, 1:2].bitcast(I32), min_val=0, max_val=1)
            with sp.If(more > 0):
                sp.wait_ge(m_y, NE)
                with sp.Fori(0, NE) as e:
                    sp.wait_ge(m_y, 3 * e + NE)
                    sp.dma_start(w13[0][:, 0], w_expert(w1_2, e)).then_inc(w13_in[0], 16)
                    sp.dma_start(w13[0][:, 1], w_expert(w3_2, e)).then_inc(w13_in[0], 16)
                    sp.dma_start(w2b[0], w_expert(w2_2, e)).then_inc(w2_in[0], 16)
            for b in range(TB):
                sp.wait_ge(m_out, 2 * b + 2)
                sp.dma_start(out[0][P * b:P * (b + 1), :], hn_tok[:, b, :]).then_inc(out_done, 16)
            sp.wait_ge(out_done, 32)

        @block.gpsimd
        def _(pool):
            pool.memset(ones[:], 1.0).then_inc(const_done, 1)
            pool.memset(ident[:], 0.0).then_inc(const_done, 1)
            pool.memset(cact[:], 0.0).then_inc(const_done, 1)
            pool.wait_ge(const_done, 3)
            pool.affine_select(out=ident[:], in_=ident[:], compare_op=ALU.not_equal, fill=1.0, base=0,
                               pattern=[[-1, P]], channel_multiplier=1).then_inc(const_done, 1)
            pool.iota(xor_i[:, 0, :].bitcast(I32), pattern=[[0, P]], base=0, channel_multiplier=1).then_inc(const_done, 1)
            pool.iota(xor_i[:, 1, :].bitcast(I32), pattern=[[1, P]], base=0, channel_multiplier=0).then_inc(const_done, 1)
            pool.wait_ge(setup_c, 4)
            pool.memset(GS, 1.0).then_inc(a_init, 1)
            pool.memset(qd, 0.0).then_inc(a_init, 1)
            pool.memset(attA, 0.0).then_inc(a_init, 1)
            pool.memset(pair_ones[:], 0.0).then_inc(w_ms, 1)
            pool.memset(flip[:], 0.0).then_inc(b_zero, 1)
            pool.wait_ge(w_ms, 1)
            pool.wait_ge(b_zero, 1)
            pool.affine_select(out=flip[:], in_=flip[:], compare_op=ALU.not_equal, fill=1.0, base=1 - P,
                               pattern=[[1, P]], channel_multiplier=1).then_inc(b_zero, 1)
            pool.wait_ge(b_zero, 2)
            pool.memset(pair_ones[0:64, 0:64], 1.0).then_inc(w_ms, 1)
            pool.memset(pair_ones[64:128, 64:128], 1.0).then_inc(w_ms, 1)
            pool.wait_ge(a_lo, 2)
            for r, n in enumerate((P, P, NREL - 2 * P)):
                pool.dma_start(rel_rows[0:n, r, :], b_rel_bias[0][P * r:P * r + n, :]).then_inc(b_rel, 16)
            pool.memset(relT[0:HB, :], 0.0).then_inc(b_zero, 1)
            pool.wait_ge(b_relt, 2)
            pool.dma_start(scratch, relT[0:HB, :]).then_inc(b_rel, 16)
            pool.wait_ge(b_rel, 64)
            pool.dma_start(biasB[:, :, 0:P], bass.AP(scratch.tensor, 129, [[1, P], [3 * P, HB], [1, P]]))\
                .then_inc(b_rel, 16)
            pool.dma_start(biasB[:, :, P:3 * P], bass.AP(scratch.tensor, 1, [[1, P], [3 * P, HB], [1, 2 * P]]))\
                .then_inc(b_rel, 16)
            pool.wait_ge(b_rel, 96)
            pool.memset(biasB[64:128, :, 64:128], MASKED).then_inc(b_bias, 1)
            pool.memset(biasB[64:128, :, P + 192:3 * P], MASKED).then_inc(b_bias, 1)
            pool.wait_ge(at_lo, HB // 2)
            pool.dma_start(wRow, sgu_w_2.rearrange("g i j -> i g j")).then_inc(w_ld, 16)
            pool.dma_start(gain_bc, bass.AP(sgu_norm_2.tensor, 0, [[0, P], [1, 512]])).then_inc(w_ld, 16)
            pool.dma_start(sinks, bass.AP(attn_sinks_2.tensor, 0, [[0, P], [1, HW]])).then_inc(w_ld, 16)
            pool.dma_start(sgb, bass.AP(sgu_b_2.tensor, 0, [[0, 1], [1, 8 * P]])).then_inc(w_ld, 16)
            pool.dma_start(mem_tok, mem_2[0].rearrange("(b p) d -> p b d", p=P)).then_inc(ld_mem, 16)
            pool.memset(winmask, 0.0).then_inc(w_ms, 1)
            pool.wait_ge(w_ms, 4)
            for n, sign in ((0, 1), (1, -1), (2, 1)):
                pool.affine_select(out=winmask[:, n, :], in_=winmask[:, n, :],
                                   compare_op=ALU.is_ge if sign > 0 else ALU.is_ge, fill=MASKED,
                                   base=0 if sign > 0 else -1, pattern=[[-sign, P]],
                                   channel_multiplier=sign).then_inc(w_ms, 1)
            pool.wait_ge(w_ld, 64)
            pool.affine_select(out=wRow, in_=wRow, compare_op=ALU.is_ge, fill=0.0, base=0,
                               pattern=[[0, 8], [-1, P]], channel_multiplier=1).then_inc(w_ms, 1)
            pool.wait_ge(x_tc, 2)
            pool.wait_ge(at_lo, 12)
            pool.iota(slot_i.bitcast(I32).rearrange("p (a b c) -> p a b c", a=4, b=2),
                      pattern=[[CAP, 4], [0, 2], [1, CAP]], base=0, channel_multiplier=0).then_inc(m_const, 1)
            pool.memset(tri, 1.0).then_inc(m_const, 1)
            pool.wait_ge(m_const, 2)
            pool.affine_select(out=tri, in_=tri, compare_op=ALU.is_gt, fill=0.0, base=0, pattern=[[1, P]],
                               channel_multiplier=-1).then_inc(m_const, 1)
            pool.dma_start(wr[:, :, 0:NGROUP], w_router_group_2.rearrange("(k p) g -> p k g", p=P)).then_inc(m_wr, 16)
            for g in range(NGROUP):
                pool.dma_start(wr[:, :, NGROUP + PER * g:NGROUP + PER * (g + 1)],
                               w_router_expert_2[g].rearrange("(k p) e -> p k e", p=P)).then_inc(m_wr, 16)

        @block.scalar
        def _(act):
            split = [0]
            fence = [LAST["a_out"]]

            def hi_upto(w):
                while split[0] <= min(w, fence[0]):
                    p = pieces[split[0]]
                    act.wait_ge(slot_in[p["slot"] % RING], slot_use(p["slot"]))
                    if p["w"] >= NBUF:
                        act.wait_ge(piece_done, p["w"] - NBUF + 1)
                    act.activation(piece_buf(p, 0), piece_src(p), ACT.Copy).then_inc(hi_done, 1)
                    split[0] += 1

            def result(pair):
                for p in pair:
                    hi_upto(p["w"] + LOOKAHEAD)
                act.wait_ge(piece_done, pair[1]["w"] + 1)

            def gemv_rows(s):
                g = gemv_of[s["n"]]
                act.wait_ge(gemv_mm, g + 1)
                act.activation(gsb[:, g % 2, :], gps, ACT.Copy).then_inc(gemv_sb, 1)

            def root(name):
                act.wait_ge(var_done, STATS[name] + 1)
                act.activation(stat[:, 2:4], stat[:, 0:2], ACT.Sqrt).then_inc(std_done, 1)

            def squares(name, src, last_write):
                act.wait_ge(*last_write)
                for w in SQ_FREE[name]:
                    act.wait_ge(*w)
                act.activation(sq[:], src, ACT.Square).then_inc(sq_done, 1)

            def operand_hi(name, shift, after):
                i = OPERANDS[name]
                if after is not None:
                    act.wait_ge(piece_done, after + 1)
                for c_ in range(DC):
                    act.wait_ge(scaled, 8 * i + c_ + 1)
                    bias = shift(c_) if shift else 0.0
                    act.activation(u[:, 0, c_, :], sq[:, c_, :], ACT.Identity, bias=bias).then_inc(u_hi, 1)

            for i, (row, n, src) in enumerate(((0, 48, mod_b[0]), (48, 16, kv_mod_b), (64, 48, mod_b[1]))):
                act.dma_start(rows1[row:row + n, :], src.rearrange("(r p) -> r p", p=P)).then_inc(ld_vec, 16)
            for name, src in (("norm_mix", norm_mix.rearrange("l (r p) -> (l r) p", p=P)),
                              ("norm_ffn", norm_ffn.rearrange("l (r p) -> (l r) p", p=P)),
                              ("a_lb", a_lb[0].rearrange("(r p) -> r p", p=P)),
                              ("kv_norm", kv_norm.rearrange("(r p) -> r p", p=P)),
                              ("final_norm", final_norm.rearrange("(r p) -> r p", p=P)),
                              ("norm_mix_2", norm_mix_2.rearrange("(r p) -> r p", p=P)),
                              ("norm_cross_2", norm_cross_2.rearrange("(r p) -> r p", p=P)),
                              ("norm_mem_2", norm_mem_2.rearrange("(r p) -> r p", p=P)),
                              ("norm_ffn_2", norm_ffn_2.rearrange("(r p) -> r p", p=P)),
                              ("a_out_norm", a_out_norm),
                              ("out_norm_attn_2", out_norm_attn_2.rearrange("(r p) -> r p", p=P)),
                              ("out_norm_sgu_2", out_norm_sgu_2.rearrange("(r p) -> r p", p=P)),
                              ("cq_norm_2", cq_norm_2.rearrange("(r p) -> r p", p=P)),
                              ("ck_norm_2", ck_norm_2.rearrange("(r p) -> r p", p=P)),
                              ("c", c[0].rearrange("(r p) -> r p", p=P))):
                r0 = VEC[name]
                act.dma_start(rows2[r0:r0 + src.shape[0], :], src).then_inc(ld_vec, 16)
            for name, src in (("q_norm_2", q_norm_2), ("k_norm_2", k_norm_2)):
                r0 = VEC[name]
                for twice in range(2):
                    act.dma_start(rows2[r0:r0 + 1, 64 * twice:64 * twice + 64],
                                  src.rearrange("(r p) -> r p", r=1)).then_inc(ld_vec, 16)
            act.wait_ge(setup_c, 2)
            act.wait_ge(const_done, 3)
            act.activation(cact[:, :, 0:1], vec2[:, VEC["c"]:VEC["c"] + DC].rearrange("p (c o) -> p c o", o=1),
                           ACT.Silu).then_inc(act_order, 1)
            act.wait_ge(setup_c, 5)
            act.activation(lbs[:, 3, :], lbs[:, 0, :], ACT.Exp).then_inc(act_order, 1)
            squares("mix0", h[:], (setup_c, 4))
            for s in jobs["gemv_first"]:
                gemv_rows(s)
            root("mix0")
            hi_upto(LOOKAHEAD)
            operand_hi("mix0", lambda c_: mod[:, c_:c_ + 1], None)
            for n, pair in enumerate(pairs("zf")):
                result(pair)
                act.activation(kd[:, 2 * n:2 * n + 2, :], bank(pair), ACT.Sigmoid).then_inc(lin_out["act"], 1)
            for n, pair in enumerate(pairs("q")):
                result(pair)
                act.activation(qA[:, 2 * n:2 * n + 2, :], bank(pair), ACT.Silu).then_inc(lin_out["act"], 1)
            for r in range(8):
                pair = jobs[("v" if r < 4 else "g") + str(r)]
                n = r % 4
                gemv_rows(jobs[f"gemv_round{r}"][0])
                result(pair)
                if r < 4:
                    act.activation(vA[:, :, 256 * n:256 * (n + 1)].rearrange("p b (c n) -> p c b n", c=2),
                                   bank(pair).rearrange("p c (b n) -> p c b n", b=TB),
                                   ACT.Copy).then_inc(lin_out["act"], 1)
                else:
                    act.activation(gA[:, 2 * n:2 * n + 2, :], bank(pair), ACT.Silu).then_inc(lin_out["act"], 1)
                gemv_rows(jobs[f"gemv_round{r}"][1])
            for b in range(2):
                act.wait_ge(a_mm, 4 * 8 + b + 1)
                act.activation(attA[:, 4 * b:4 * b + 4, 1, :],
                               ps[:, 2 + b, :].rearrange("p (h t) -> p h t", h=4), ACT.Copy).then_inc(a_x, 1)
            act.wait_ge(u_lo, 8)
            for n in range(4):
                act.wait_ge(a_o, 2 * n + 2)
                act.activation(sq[:, 2 * n:2 * n + 2, :], acc[:, 2 * n:2 * n + 2, :], ACT.Square).then_inc(a_sq, 1)
            for n in range(2):
                act.activation(qA[:, 4 * n:4 * n + 4, :], acc[:, 4 * n:4 * n + 4, :], ACT.Copy,
                               scale=vec("a_out_norm")).then_inc(a_og, 1)
            act.wait_ge(a_var, 1)
            act.activation(stat[:, 16:32], stat[:, 0:16], ACT.Sqrt).then_inc(a_std, 1)
            for b in range(2):
                act.wait_ge(a_g, b + 1)
                act.activation(u[:, 0, 4 * b:4 * b + 4, :], sq[:, 4 * b:4 * b + 4, :], ACT.Copy).then_inc(a_hi, 1)
            hi_upto(jobs["a_out"][0]["w"] + LOOKAHEAD)
            for p in jobs["a_out"]:
                hi_upto(p["w"] + LOOKAHEAD)

            def ffn_act(layer, name, shift, before, last_write):
                squares(name, h[:], last_write)
                if layer == 0:
                    for s in jobs["gemv_kv"]:
                        gemv_rows(s)
                    fence[0] = len(pieces) - 1
                    hi_upto(LAST["a_out"] + 1 + LOOKAHEAD)
                root(name)
                operand_hi(name, shift, before)
                for i in range(FFI):
                    fi = layer * FFI + i
                    pair = jobs[f"gate{layer}_{i}"]
                    result(pair)
                    if i >= 2:
                        wait_out(act, jobs[f"up{layer}_{i - 2}"][1])
                    act.activation(silu_g[:, i % 2, :, :], bank(pair), ACT.Silu).then_inc(lin_out["act"], 1)
                    for p in jobs[f"up{layer}_{i}"]:
                        hi_upto(p["w"] + LOOKAHEAD)
                    if i > 0:
                        for p in jobs[f"down{layer}_{i - 1}"]:
                            hi_upto(p["w"] + LOOKAHEAD - 1)
                    wait_out(act, jobs[f"up{layer}_{i}"][1])
                    if fi >= 2:
                        act.wait_ge(piece_done, jobs[f"down{(fi - 2) // FFI}_{(fi - 2) % FFI}"][1]["w"] + 1)
                    act.activation(hid[:, fi % 2, 0, :, :], hidden[:, i % 2, :, :], ACT.Copy).then_inc(f_hi, 1)
                    if layer == 0:
                        for s in jobs[f"gemv_ffn{i}"]:
                            gemv_rows(s)
                for p in jobs[f"down{layer}_{FFI - 1}"]:
                    hi_upto(p["w"] + LOOKAHEAD)
                if layer == 0:
                    for s in jobs[f"gemv_ffn{FFI}"]:
                        gemv_rows(s)

            ffn_act(0, "ffn0", lambda c_: mod[:, 24 + c_:25 + c_], LAST["a_out"],
                    (lin_out["dve"], jobs["a_out"][-1]["turn"]))
            def attention_act(kind, hi_out):
                first, n = FIRST[kind], COUNT[kind]
                r0, r1, every = runs(kind)

                def exps(i):
                    a = first + i
                    act.wait_ge(at_b, before_b(a + 1))
                    if i >= 2:
                        act.wait_ge(at_t, a - 1)
                    for m, r in enumerate((r0, r1)):
                        act.activation(pr_sb[:, i % 2, r], sc_sb[:, i % 2, r], ACT.Exp,
                                       bias=small[:, 0, 2 * a + m:2 * a + m + 1],
                                       accum_out=small[:, 1, 2 * a + m:2 * a + m + 1]).then_inc(at_e, 1)

                def copy(i):
                    a = first + i
                    act.wait_ge(at_t, a + 1)
                    if i >= 2:
                        act.wait_ge(at_o, a - 1)
                    w = 128 * len(blocks(kind))
                    act.activation(pt_sb[:, i % 2, 0:w], ps[:, 4 + i % 2, 0:w], ACT.Copy).then_inc(at_pt, 1)

                def drain(i):
                    if drains(kind, i) is not None:
                        act.wait_ge(at_o, first + i + 1)
                        k, bank_ = o_bank(kind, i)
                        hi_out(i, bank_).then_inc(at_hi, 1)

                for i in range(n + 2):
                    if i < n:
                        exps(i)
                    if 1 <= i <= n:
                        copy(i - 1)
                    if i >= 2:
                        drain(i - 2)

            def kv_act():
                squares("kv", h[:], (acc_done, 8))
                root("kv")
                operand_hi("kv", lambda c_: mod[:, 48 + c_:49 + c_], LAST["up0_10"])
                for n, pair in enumerate(pairs("kv_k")):
                    result(pair)
                    act.activation(kB[:, 2 * n:2 * n + 2, :], bank(pair), ACT.Copy).then_inc(lin_out["act"], 1)
                for n, pair in enumerate(pairs("kv_v")):
                    result(pair)
                    act.activation(vB[:, :, 256 * n:256 * (n + 1)].rearrange("p b (c n) -> p c b n", c=2),
                                   bank(pair).rearrange("p c (b n) -> p c b n", b=TB),
                                   ACT.Copy).then_inc(lin_out["act"], 1)

            kv_act()
            operand_hi("mix1", lambda c_: mod[:, 64 + c_:65 + c_], LAST["kv_v"])
            for n, pair in enumerate(pairs("b_q")):
                result(pair)
                act.activation(qB[:, 2 * n:2 * n + 2, :], bank(pair), ACT.Copy, scale=0.125).then_inc(lin_out["act"], 1)
            act.wait_ge(piece_done, LAST["b_q"] + 1)
            attention_act("B", lambda i, o: act.activation(
                u[:, 0, i // 2, :], o[:, 0:T], ACT.Copy))
            hi_upto(LAST["b_o"] + LOOKAHEAD)
            ffn_act(1, "ffn1", lambda c_: mod[:, 88 + c_:89 + c_], LAST["b_o"],
                    (lin_out["dve"], jobs["b_o"][-1]["turn"]))

            squares("final", h[:], (acc_done, 16))
            root("final")
            squares("mix_2", h[:], (res_done, 8))
            root("mix_2")
            operand_hi("mix_2", None, LAST["up1_10"])
            def in2_act():
                for n, pair in enumerate(pairs("in2")):
                    result(pair)
                    if n < 2:
                        act.activation(q_raw[:, 2 * n:2 * n + 2, :], bank(pair), ACT.Copy).then_inc(lin_out["act"], 1)
                    elif n == 2:
                        act.activation(q_raw[:, 4, :], bank(pair)[:, 0, :], ACT.Copy)
                        act.activation(vW, bank(pair)[:, 1, :].rearrange("p (b n) -> p b n", b=TB),
                                       ACT.Copy).then_inc(lin_out["act"], 1)
                    elif n < 5:
                        act.activation(uW[:, 2 * n - 6:2 * n - 4, :], bank(pair), ACT.Gelu_apprx_tanh)\
                            .then_inc(lin_out["act"], 1)
                    else:
                        m = n - 5
                        act.activation(gW[:, :, 256 * m:256 * (m + 1)].rearrange("p b (c n) -> p c b n", c=2),
                                       bank(pair).rearrange("p c (b n) -> p c b n", b=TB),
                                       ACT.Gelu_apprx_tanh).then_inc(lin_out["act"], 1)

            in2_act()
            wait_out(act, jobs["in2"][-1])
            act.wait_ge(u_lo, 48)
            act.activation(sq[:, 0:5, :], q_raw, ACT.Square).then_inc(w_sq, 1)
            for b in range(TB):
                act.activation(gn[:, b, :], gW[:, b, :], ACT.Square, accum_out=gst[:, b:b + 1]).then_inc(w_sq, 1)
            act.wait_ge(w_ss, 1)
            act.wait_ge(at_lo, HB // 2)
            act.activation(qk_std, acc[:, 0:5, :], ACT.Sqrt, scale=1.0 / 64, bias=EPS).then_inc(w_std, 1)
            act.wait_ge(w_sq, 3)
            act.activation(gst[:, 2:4], gst[:, 0:2], ACT.Sqrt, scale=1.0 / 512, bias=EPS).then_inc(w_std, 1)
            act.wait_ge(w_dup, 1)
            act.activation(kdup, acc[:, 0:2, :], ACT.Copy).then_inc(w_dc, 1)
            attention_act("W", lambda i, o: act.activation(mix[:, i // 2, :], o[:, 0:T], ACT.Copy))
            act.wait_ge(w_sg, 2)
            act.wait_ge(at_hi, 12)
            act.wait_ge(w_ss, 1)
            act.activation(sq[:], mix, ACT.Square).then_inc(w_sq, 1)
            act.wait_ge(w_ss, 2)
            act.activation(half_std, ps[:, 6, :].rearrange("p (c t) -> p c t", c=2), ACT.Sqrt, scale=1.0 / 512,
                           bias=EPS).then_inc(w_std, 1)
            operand_hi("mixed", None, LAST["in2"])
            hi_upto(LAST["out2"] + LOOKAHEAD)

            act.wait_ge(x_tc, 1)
            squares("mem", memT, (x_tc, 2))
            root("mem")
            operand_hi("mem", None, LAST["out2"])
            for n, pair in enumerate(pairs("ck")):
                result(pair)
                act.activation(kX[:, 2 * n:2 * n + 2, :], bank(pair), ACT.Copy).then_inc(lin_out["act"], 1)
            for n, pair in enumerate(pairs("cv")):
                result(pair)
                act.activation(vX[:, :, 256 * n:256 * (n + 1)].rearrange("p b (c n) -> p c b n", c=2),
                               bank(pair).rearrange("p c (b n) -> p c b n", b=TB),
                               ACT.Copy).then_inc(lin_out["act"], 1)
            squares("cross", h[:], (lin_out["dve"], jobs["out2"][-1]["turn"]))
            root("cross")
            operand_hi("cross", None, LAST["cv"])
            for n, pair in enumerate(pairs("cq")):
                result(pair)
                act.activation(qX[:, 2 * n:2 * n + 2, :], bank(pair), ACT.Copy).then_inc(lin_out["act"], 1)
            wait_out(act, jobs["cq"][-1])
            act.activation(raw, kX, ACT.Square).then_inc(x_sq, 1)
            act.wait_ge(u_lo, 72)
            act.activation(sq[:], qX, ACT.Square).then_inc(x_sq, 1)
            act.wait_ge(x_ss, 1)
            act.activation(x_rstd, acc[:], ACT.Sqrt, scale=1.0 / 256, bias=EPS).then_inc(x_std, 1)
            act.wait_ge(piece_done, LAST["cq"] + 1)
            act.wait_ge(x_rs, 1)
            act.wait_ge(x_n, 4)
            attention_act("X", lambda i, o: act.activation(
                u[:, 0, 2 * i:2 * i + 2, :], o.rearrange("p (c t) -> p c t", c=2), ACT.Copy))
            hi_upto(LAST["co"])
            squares("moe", h[:], (lin_out["dve"], CROSS_DONE))
            root("moe")
            act.wait_ge(route, 2)
            for b in range(TB):
                act.activation(og_t[:, b, :], logits[:, b, 0:NGROUP], ACT.Exp, bias=rs[:, 0, b:b + 1],
                               accum_out=rs[:, 1, b:b + 1]).then_inc(route_e, 1)
            act.wait_ge(route, 20)
            act.activation(rs[:, 8, :], rs[:, 7, :], ACT.Exp).then_inc(route_e, 1)

            def expert_act(n):
                act.wait_ge(m_h, n + 1)
                act.activation(silu_e, ps[:, 0, 0:256], ACT.Silu).then_inc(m_si, 1)
                act.wait_ge(m_t, n + 1)
                act.activation(tt, ps[:, 1, :], ACT.Copy).then_inc(m_tc, 1)
                act.wait_ge(m_y, n + 1)
                act.activation(y_sb, ps[:, 6, :], ACT.Copy).then_inc(m_yc, 1)

            with act.Fori(0, NE // 2) as i:
                for b in range(2):
                    expert_act(2 * i + b)
            act.wait_ge(m_flag, 1)
            more = act.value_load(flag[0:1, 1:2].bitcast(I32), min_val=0, max_val=1)
            with act.If(more > 0):
                with act.Fori(0, NE) as e:
                    for p_ in range(3):
                        expert_act(3 * e + NE + p_)
                act.wait_ge(m_all, 1 + 3 * NE)
            act.wait_ge(m_all, 1)
            act.activation(hn_tok[:, 0, 0:512], ps[:, 2, :], ACT.Copy).then_inc(m_out, 1)
            act.wait_ge(m_out, 2)
            act.activation(hn_tok[:, 1, 0:512], ps[:, 4, :], ACT.Copy).then_inc(m_out, 1)

        @block.vector
        def _(dve):
            split = [0]
            fence = [LAST["a_out"]]

            def lo_upto(w):
                while split[0] <= min(w, fence[0]):
                    p = pieces[split[0]]
                    dve.wait_ge(hi_done, p["w"] + 1)
                    dve.tensor_tensor(piece_buf(p, 1), piece_src(p), piece_buf(p, 0).bitcast(F32),
                                      ALU.subtract).then_inc(lo_done, 1)
                    split[0] += 1

            def result(pair):
                for p in pair:
                    lo_upto(p["w"] + LOOKAHEAD)
                dve.wait_ge(piece_done, pair[1]["w"] + 1)

            def norm_rstd(name, width):
                i = STATS[name]
                dve.wait_ge(sum_done, i + 1)
                dve.tensor_scalar(stat[:, 0:2], stps[:, 0:2], 1.0 / width, EPS, ALU.mult, ALU.add)\
                   .then_inc(var_done, 1)
                dve.wait_ge(std_done, i + 1)
                dve.reciprocal(stat[:, 4:6], stat[:, 2:4]).then_inc(rstd_done, 1)
                dve.wait_ge(rstd_done, i + 1)
                if i > 0:
                    dve.wait_ge(bc_done, i)
                for b in range(TB):
                    dve.tensor_scalar(diag[:, b, :], ident[:], stat[:, 4 + b:5 + b], None, ALU.mult)\
                       .then_inc(diag_done, 1)
                dve.wait_ge(bc_done, i + 1)

            def operand(name, src, gains, shift, by=lambda c_: rbc):
                i = OPERANDS[name]
                if i > 0:
                    dve.wait_ge(u_lo, 8 * i)
                for c_ in range(DC):
                    dve.scalar_tensor_tensor(out=sq[:, c_, :], in0=src[:, c_, :], scalar=gains(c_), in1=by(c_),
                                             op0=ALU.mult, op1=ALU.mult).then_inc(scaled, 1)
                for c_ in range(DC):
                    dve.wait_ge(u_hi, 8 * i + c_ + 1)
                    s_ = shift(c_) if shift else 0.0
                    dve.scalar_tensor_tensor(out=u[:, 1, c_, :], in0=sq[:, c_, :], scalar=s_,
                                             in1=u[:, 0, c_, :].bitcast(F32), op0=ALU.add, op1=ALU.subtract)\
                       .then_inc(u_lo, 1)

            def add_gated(job, gate):
                for n, pair in enumerate(pairs(job)):
                    result(pair)
                    for m in range(2):
                        c_ = 2 * n + m
                        ins = dve.scalar_tensor_tensor(out=h[:, c_, :], in0=bank(pair)[:, m, :],
                                                       scalar=gate(c_) if gate else 1.0, in1=h[:, c_, :],
                                                       op0=ALU.mult, op1=ALU.add)
                    ins.then_inc(lin_out["dve"], 1)

            dve.wait_ge(setup_t, 1)
            dve.tensor_copy(vec1[:], ps[:, 0, 0:112]).then_inc(setup_c, 1)
            dve.wait_ge(setup_t, 2)
            dve.tensor_copy(vec2[:], ps[:, 1, 0:ROWS2]).then_inc(setup_c, 1)
            for b in range(2):
                dve.wait_ge(setup_t, 3 + b)
                dve.tensor_copy(h[:, 4 * b:4 * b + 4, :], acc[:, 4 * b:4 * b + 4, :]).then_inc(setup_c, 1)
            lb_col = vec2[:, VEC["a_lb"]:VEC["a_lb"] + HA]
            dve.wait_ge(setup_c, 4)
            dve.tensor_tensor(lbs[:, 0, :], lb_col, lb_col, ALU.subtract).then_inc(setup_c, 1)
            dve.wait_ge(act_order, 2)
            dve.reciprocal(lbs[:, 1, :], lbs[:, 3, :]).then_inc(setup_c, 1)
            dve.wait_ge(setup_c, 6)
            dve.tensor_tensor(lbs[:, 2, :], lbs[:, 3, :], lbs[:, 1, :], ALU.mult).then_inc(setup_c, 1)
            dve.wait_ge(setup_c, 7)
            dve.tensor_tensor(lbs[:, 0, :], lbs[:, 2, :], lbs[:, 2, :], ALU.subtract).then_inc(setup_c, 1)
            dve.wait_ge(setup_c, 8)
            dve.tensor_scalar(lbs[:, 1, :], lbs[:, 0, :], -1.0, 1.0, ALU.mult, ALU.add).then_inc(setup_c, 1)
            dve.tensor_scalar(lbs[:, 2, :], lbs[:, 0, :], 1.0, -1.0, ALU.mult, ALU.add).then_inc(setup_c, 1)
            dve.wait_ge(const_done, 6)
            si, ti, xi = (xor_i[:, n, :] for n in range(3))
            dve.tensor_tensor(xi.bitcast(I32), si.bitcast(I32), ti.bitcast(I32), ALU.bitwise_xor).then_inc(setup_c, 1)
            dve.tensor_tensor(si, ti.bitcast(I32), si.bitcast(I32), ALU.is_lt).then_inc(setup_c, 1)
            dve.wait_ge(setup_c, 12)
            dve.tensor_copy(ti, xi.bitcast(I32)).then_inc(setup_c, 1)
            dve.wait_ge(setup_c, 13)
            dve.scalar_tensor_tensor(out=xi, in0=si, scalar=1000.0, in1=ti, op0=ALU.mult, op1=ALU.add).then_inc(setup_c, 1)
            dve.wait_ge(setup_c, 14)
            dve.tensor_scalar(masks[:, 0, :], xi, 0.0, None, ALU.is_equal).then_inc(setup_c, 1)
            for n, H in enumerate(LEVELS):
                dve.wait_ge(setup_c, 15 + 2 * n)
                dve.tensor_scalar(ti, xi, float(H), None, ALU.is_ge).then_inc(setup_c, 1)
                dve.wait_ge(setup_c, 16 + 2 * n)
                dve.scalar_tensor_tensor(out=masks[:, n + 1, :], in0=xi, scalar=float(2 * H), in1=ti,
                                         op0=ALU.is_lt, op1=ALU.mult).then_inc(setup_c, 1)
            dve.wait_ge(gemv_col, 8)
            dve.tensor_tensor(mod[:, 0:16], modps[:, 0:16], vec1[:, 0:16], ALU.add).then_inc(mod_done, 1)
            dve.wait_ge(mod_done, 1)
            dve.scalar_tensor_tensor(out=gain[:, 0, :], in0=mod[:, 8:16], scalar=1.0,
                                     in1=vec2[:, VEC["norm_mix"]:VEC["norm_mix"] + DC],
                                     op0=ALU.add, op1=ALU.mult).then_inc(mod_done, 1)
            dve.wait_ge(mod_done, 2)
            norm_rstd("mix0", D)
            lo_upto(LOOKAHEAD)
            operand("mix0", h, lambda c_: gain[:, 0, c_:c_ + 1], lambda c_: mod[:, c_:c_ + 1])
            for n, p in enumerate(jobs["zf"]):
                lo_upto(p["w"] + LOOKAHEAD)
                wait_out(dve, p)
                dve.tensor_scalar(FP[:, n, :], kd[:, n, :], lbs[:, 1, n:n + 1], lbs[:, 0, n:n + 1],
                                  ALU.mult, ALU.add).then_inc(a_prep, 1)
                dve.tensor_scalar(kA[:, n, :], kd[:, n, :], lbs[:, 2, n:n + 1], lbs[:, 1, n:n + 1],
                                  ALU.mult, ALU.add).then_inc(a_prep, 1)
            dve.wait_ge(a_prep, 16)
            dve.tensor_scalar(FP, FP, MIN_FORGET, None, ALU.max).then_inc(a_prep, 1)
            for p in jobs["q"]:
                lo_upto(p["w"] + LOOKAHEAD)
            wait_out(dve, jobs["q"][-1])
            dve.wait_ge(a_prep, 17)
            dve.wait_ge(a_init, 3)

            def decayed(n):
                H = (LEVELS + [128])[n]
                if n > 0:
                    dve.wait_ge(a_mm, 4 * (n + 1))
                    dve.wait_ge(a_fg, 2 * n)
                dve.tensor_tensor(halves(qd, H, True), halves(qA, H, True), halves(FP, H, True), ALU.mult)\
                   .then_inc(a_dec, 1)
                dve.tensor_tensor(halves(kd, H, False), halves(kA, H, False), halves(GS, H, False), ALU.mult)\
                   .then_inc(a_dec, 1)

            def products(n):
                H = LEVELS[n]
                last = lambda upper: halves(FP, H, upper)[:, :, H - 1:H].to_broadcast([P, HA * T // (2 * H), H])
                dve.wait_ge(a_dec, 2 * n + 2)
                dve.tensor_tensor(halves(GS, H, False), halves(GS, H, False), last(True), ALU.mult)\
                   .then_inc(a_fg, 1)
                dve.wait_ge(a_fg, 2 * n + 1)
                dve.tensor_tensor(halves(FP, H, True), halves(FP, H, True), last(False), ALU.mult)\
                   .then_inc(a_fg, 1)

            def select(r):
                m = masks[:, r, :].rearrange("p (o t) -> p o t", o=1).to_broadcast([P, 4, P])
                for b in range(4):
                    dve.wait_ge(a_mm, 4 * r + b + 1)
                    dve.copy_predicated(out=attA[:, 2 * b:2 * b + 2, 0:3:2, :],
                                        mask=m.rearrange("p (h b) t -> p h b t", h=2),
                                        data=ps[:, 2 + b, :].rearrange("p (h b t) -> p h b t", h=2, b=2))\
                       .then_inc(a_cp, 1)

            decayed(0)
            products(0)
            for r in range(8):
                for p in jobs[("v" if r < 4 else "g") + str(r)]:
                    lo_upto(p["w"] + LOOKAHEAD)
                select(r)
                if r < 7:
                    decayed(r + 1)
                    if r + 1 < 7:
                        products(r + 1)
            dve.wait_ge(a_ss, 1)
            dve.tensor_scalar(stat[:, 0:16], stps[:, 0:16], 1.0 / P, EPS, ALU.mult, ALU.add).then_inc(a_var, 1)
            dve.wait_ge(a_std, 1)
            dve.reciprocal(stat[:, 32:48], stat[:, 16:32]).then_inc(a_rs, 1)
            dve.wait_ge(a_rs, 1)
            for n in range(16):
                if n >= 4:
                    dve.wait_ge(a_bc, n - 3)
                else:
                    dve.wait_ge(bc_done, 1)
                dve.tensor_scalar(diag[:, n % 4, :], ident[:], stat[:, 32 + n:33 + n], None, ALU.mult)\
                   .then_inc(a_diag, 1)
                if n % 8 == 7:
                    b = n // 8
                    four = slice(4 * b, 4 * b + 4)
                    dve.wait_ge(a_og, b + 1)
                    wait_out(dve, jobs["g7"][-1])
                    dve.tensor_tensor(qA[:, four, :], qA[:, four, :], gA[:, four, :], ALU.mult).then_inc(a_t, 1)
                    dve.wait_ge(a_t, b + 1)
                    dve.wait_ge(a_bc, n + 1)
                    dve.tensor_tensor(sq[:, four, :], qA[:, four, :],
                                      ps[:, 0:2, :].rearrange("p b (c t) -> p (b c) t", t=T), ALU.mult)\
                       .then_inc(a_g, 1)
            for b in range(2):
                dve.wait_ge(a_hi, b + 1)
                dve.tensor_tensor(u[:, 1, 4 * b:4 * b + 4, :], sq[:, 4 * b:4 * b + 4, :],
                                  u[:, 0, 4 * b:4 * b + 4, :].bitcast(F32), ALU.subtract).then_inc(a_lo, 1)
            dve.wait_ge(gemv_col, 24)
            dve.tensor_tensor(mod[:, 16:48], modps[:, 16:48], vec1[:, 16:48], ALU.add).then_inc(mod_done, 1)
            dve.wait_ge(mod_done, 3)
            dve.scalar_tensor_tensor(out=gain[:, 1, :], in0=mod[:, 32:40], scalar=1.0,
                                     in1=vec2[:, VEC["norm_ffn"]:VEC["norm_ffn"] + DC],
                                     op0=ALU.add, op1=ALU.mult).then_inc(mod_done, 1)
            add_gated("a_out", lambda c_: mod[:, 16 + c_:17 + c_])

            def ffn_dve(layer, name, gains, shift, gate):
                norm_rstd(name, D)
                fence[0] = len(pieces) - 1
                lo_upto(jobs[f"gate{layer}_0"][0]["w"] + LOOKAHEAD - 1)
                operand(name, h, gains, shift)
                for i in range(FFI):
                    fi = layer * FFI + i
                    for p in jobs[f"gate{layer}_{i}"]:
                        lo_upto(p["w"] + LOOKAHEAD)
                    pair = jobs[f"up{layer}_{i}"]
                    result(pair)
                    wait_out(dve, jobs[f"gate{layer}_{i}"][0])
                    if fi >= 2:
                        dve.wait_ge(f_lo, fi - 1)
                    dve.tensor_tensor(hidden[:, i % 2, :, :], silu_g[:, i % 2, :, :], bank(pair),
                                      ALU.mult).then_inc(lin_out["dve"], 1)
                    if i > 0:
                        for p in jobs[f"down{layer}_{i - 1}"]:
                            lo_upto(p["w"] + LOOKAHEAD - 1)
                    dve.wait_ge(f_hi, fi + 1)
                    dve.tensor_tensor(hid[:, fi % 2, 1, :, :], hidden[:, i % 2, :, :],
                                      hid[:, fi % 2, 0, :, :].bitcast(F32), ALU.subtract).then_inc(f_lo, 1)
                for p in jobs[f"down{layer}_{FFI - 1}"]:
                    lo_upto(p["w"] + LOOKAHEAD)
                dve.wait_ge(piece_done, jobs[f"down{layer}_{FFI - 1}"][1]["w"] + 1)
                for c_ in range(DC):
                    dve.scalar_tensor_tensor(out=h[:, c_, :], in0=acc[:, c_, :], scalar=gate(c_), in1=h[:, c_, :],
                                             op0=ALU.mult, op1=ALU.add).then_inc(acc_done, 1)

            dve.wait_ge(mod_done, 4)
            ffn_dve(0, "ffn0", lambda c_: gain[:, 1, c_:c_ + 1], lambda c_: mod[:, 24 + c_:25 + c_],
                    lambda c_: mod[:, 40 + c_:41 + c_])
            def attention_dve(kind, bias, lo_out):
                first, n = FIRST[kind], COUNT[kind]
                r0, r1, every = runs(kind)

                def scores(i):
                    a, at = first + i, before_b(first + i)
                    if i >= 2:
                        dve.wait_ge(at_e, 2 * (a - 1))
                    if kind == "W":
                        dve.tensor_copy(sc_sb[:, i % 2, 0:386:385],
                                        sinks[:, i:i + 1].to_broadcast([P, 2])).then_inc(at_b, 1)
                        at += 1
                    dve.wait_ge(at_s, a + 1)
                    src = ps[:, 2 + i % 2, 0:every.stop - every.start]
                    if bias is None:
                        dve.tensor_scalar(sc_sb[:, i % 2, every], src, SCALE[kind], None, ALU.mult)\
                            .then_inc(at_b, 1)
                    else:
                        dve.scalar_tensor_tensor(out=sc_sb[:, i % 2, every], in0=src, scalar=SCALE[kind],
                                                 in1=bias(i), op0=ALU.mult, op1=ALU.add).then_inc(at_b, 1)
                    dve.wait_ge(at_b, at + 1)
                    for m, r in enumerate((r0, r1)):
                        dve.tensor_reduce(out=small[:, 0, 2 * a + m:2 * a + m + 1], in_=sc_sb[:, i % 2, r],
                                          axis=AX, op=ALU.max, negate=True).then_inc(at_b, 1)

                def probs(i):
                    a = first + i
                    dve.wait_ge(at_e, 2 * a + 2)
                    dve.reciprocal(small[:, 2, 2 * a:2 * a + 2], small[:, 1, 2 * a:2 * a + 2]).then_inc(at_p, 1)
                    dve.wait_ge(at_p, 3 * a + 1)
                    for m, r in enumerate((r0, r1)):
                        dve.tensor_scalar(pr_sb[:, i % 2, r], pr_sb[:, i % 2, r],
                                          small[:, 2, 2 * a + m:2 * a + m + 1], None, ALU.mult).then_inc(at_p, 1)

                def drain(i):
                    if lo_out and drains(kind, i) is not None:
                        k, bank_ = o_bank(kind, i)
                        dve.wait_ge(at_hi, k + 1)
                        lo_out(i, bank_).then_inc(at_lo, 1)

                scores(0)
                for i in range(n + 3):
                    if i + 1 < n:
                        scores(i + 1)
                    if i < n:
                        probs(i)
                    if i >= 3:
                        drain(i - 3)

            def new_gains():
                dve.wait_ge(gemv_col, NG)
                dve.tensor_tensor(mod[:, 48:112], modps[:, 48:112], vec1[:, 48:112], ALU.add).then_inc(mod_done, 1)
                dve.wait_ge(mod_done, 5)
                for g, at, gain_of in ((2, 56, vec2[:, VEC["kv_norm"]:VEC["kv_norm"] + DC]),
                                       (3, 72, vec2[:, VEC["norm_mix"] + DC:VEC["norm_mix"] + 2 * DC]),
                                       (4, 96, vec2[:, VEC["norm_ffn"] + DC:VEC["norm_ffn"] + 2 * DC])):
                    dve.scalar_tensor_tensor(out=gain[:, g, :], in0=mod[:, at:at + DC], scalar=1.0, in1=gain_of,
                                             op0=ALU.add, op1=ALU.mult).then_inc(mod_done, 1)
                dve.wait_ge(mod_done, 8)

            new_gains()
            norm_rstd("kv", D)
            lo_upto(jobs["kv_k"][0]["w"] + LOOKAHEAD - 1)
            operand("kv", h, lambda c_: gain[:, 2, c_:c_ + 1], lambda c_: mod[:, 48 + c_:49 + c_])
            lo_upto(LAST["kv_k"])
            dve.wait_ge(b_relt, 1)
            dve.wait_ge(b_zero, 3)
            dve.tensor_copy(relT[0:HB, 0:NREL], ps[0:HB, 2, 0:NREL]).then_inc(b_relt, 1)
            lo_upto(LAST["kv_v"] + LOOKAHEAD)
            operand("mix1", h, lambda c_: gain[:, 3, c_:c_ + 1], lambda c_: mod[:, 64 + c_:65 + c_])
            lo_upto(LAST["b_q"] + LOOKAHEAD)
            attention_dve("B", None, lambda i, o: dve.tensor_tensor(
                u[:, 1, i // 2, :], o[:, 0:T], u[:, 0, i // 2, :].bitcast(F32), ALU.subtract))
            add_gated("b_o", lambda c_: mod[:, 80 + c_:81 + c_])
            ffn_dve(1, "ffn1", lambda c_: gain[:, 4, c_:c_ + 1], lambda c_: mod[:, 88 + c_:89 + c_],
                    lambda c_: mod[:, 104 + c_:105 + c_])

            norm_rstd("final", D)
            for c_ in range(DC):
                dve.scalar_tensor_tensor(out=h[:, c_, :], in0=h[:, c_, :], scalar=vec("final_norm", c_), in1=rbc,
                                         op0=ALU.mult, op1=ALU.mult).then_inc(res_done, 1)
            norm_rstd("mix_2", D)
            lo_upto(jobs["in2"][0]["w"] + LOOKAHEAD - 1)
            dve.wait_ge(res_done, 8)
            operand("mix_2", h, lambda c_: vec("norm_mix_2", c_), None)
            lo_upto(jobs["in2"][7]["w"])
            for b in range(2):
                dve.wait_ge(w_tp, b + 1)
                dve.tensor_copy(wT[:, 4 * b:4 * b + 4, :], ps[:, 2 + b, :].rearrange("p (g i) -> p g i", g=4))\
                    .then_inc(w_tc, 1)
            lo_upto(LAST["in2"] + LOOKAHEAD)
            dve.wait_ge(w_std, 1)
            dve.reciprocal(qk_std, qk_std).then_inc(w_rs, 1)
            wait_out(dve, jobs["in2"][-1])
            dve.wait_ge(w_rs, 1)
            dve.scalar_tensor_tensor(out=kW, in0=q_raw[:, 4, :], scalar=vec("k_norm_2"), in1=qk_std[:, 4, :],
                                     op0=ALU.mult, op1=ALU.mult).then_inc(w_n, 1)
            dve.scalar_tensor_tensor(out=qW, in0=q_raw[:, 0:4, :], scalar=vec("q_norm_2"), in1=qk_std[:, 0:4, :],
                                     op0=ALU.mult, op1=ALU.mult).then_inc(w_n, 1)
            dve.wait_ge(w_std, 2)
            dve.reciprocal(gst[:, 4:6], gst[:, 2:4]).then_inc(w_rs, 1)
            dve.wait_ge(w_rs, 2)
            dve.wait_ge(w_ld, 64)
            for b in range(TB):
                dve.scalar_tensor_tensor(out=gn[:, b, :], in0=gW[:, b, :], scalar=gst[:, 4 + b:5 + b], in1=gain_bc,
                                         op0=ALU.mult, op1=ALU.mult).then_inc(w_n, 1)
            for b in range(2):
                dve.wait_ge(w_s, b + 1)
                dve.tensor_tensor(mix[:, 4 + 2 * b:6 + 2 * b, :], acc[:, 4 + 2 * b:6 + 2 * b, :],
                                  uW[:, 2 * b:2 * b + 2, :], ALU.mult).then_inc(w_sg, 1)
            dve.wait_ge(w_ms, 8)
            dve.wait_ge(w_n, 2)
            attention_dve("W", lambda i: winmask.rearrange("p b k -> p (b k)"), None)
            dve.wait_ge(w_std, 3)
            dve.reciprocal(half_std, half_std).then_inc(w_rs, 1)
            dve.wait_ge(w_rs, 3)
            dve.wait_ge(at_hi, 12)
            operand("mixed", mix, lambda c_: vec("out_norm_attn_2", c_) if c_ < 4 else vec("out_norm_sgu_2", c_ - 4),
                    None, lambda c_: half_std[:, c_ // 4, :])
            add_gated("out2", None)

            for b in range(2):
                dve.wait_ge(x_tp, b + 1)
                dve.tensor_copy(memT[:, 4 * b:4 * b + 4, :], acc[:, 4 * b:4 * b + 4, :]).then_inc(x_tc, 1)
            norm_rstd("mem", D)
            lo_upto(jobs["ck"][0]["w"] + LOOKAHEAD - 1)
            dve.wait_ge(x_tc, 2)
            operand("mem", memT, lambda c_: vec("norm_mem_2", c_), None)
            lo_upto(LAST["cv"] + LOOKAHEAD)
            norm_rstd("cross", D)
            operand("cross", h, lambda c_: vec("norm_cross_2", c_), None)
            lo_upto(LAST["cq"] + LOOKAHEAD)
            dve.wait_ge(x_std, 1)
            dve.reciprocal(x_rstd, x_rstd).then_inc(x_rs, 1)
            dve.wait_ge(x_rs, 1)
            wait_out(dve, jobs["cq"][-1])
            for m in range(2):
                dve.scalar_tensor_tensor(out=qX[:, m::2, :], in0=qX[:, m::2, :], scalar=vec("cq_norm_2", m),
                                         in1=x_rstd[:, 0:4, :], op0=ALU.mult, op1=ALU.mult).then_inc(x_n, 1)
                dve.scalar_tensor_tensor(out=kX[:, m::2, :], in0=kX[:, m::2, :], scalar=vec("ck_norm_2", m),
                                         in1=x_rstd[:, 4:8, :], op0=ALU.mult, op1=ALU.mult).then_inc(x_n, 1)
            dve.wait_ge(x_n, 4)
            attention_dve("X", None, lambda i, o: dve.tensor_tensor(
                u[:, 1, 2 * i:2 * i + 2, :], o.rearrange("p (c t) -> p c t", c=2),
                u[:, 0, 2 * i:2 * i + 2, :].bitcast(F32), ALU.subtract))
            add_gated("co", None)
            norm_rstd("moe", D)
            for c_ in range(DC):
                dve.scalar_tensor_tensor(out=sq[:, c_, :], in0=h[:, c_, :], scalar=vec("norm_ffn_2", c_), in1=rbc,
                                         op0=ALU.mult, op1=ALU.mult).then_inc(m_hn, 1)
            steps = [0]

            def step(ins):
                ins.then_inc(route, 1)
                steps[0] += 1
                dve.wait_ge(route, steps[0])

            def first_max(values, width, one_hot, t_, at):
                wide = lambda a: a.rearrange("p (b o) -> p b o", o=1).to_broadcast([P, TB, width])
                numbers = slot_no[:, 0:1, 0:width].to_broadcast([P, TB, width])
                step(dve.tensor_reduce(out=rs[:, at, :], in_=values, axis=AX, op=ALU.max))
                step(dve.tensor_tensor(t_, values, wide(rs[:, at, :]), ALU.is_equal))
                step(dve.scalar_tensor_tensor(out=t_, in0=numbers, scalar=-100.0, in1=t_, op0=ALU.add, op1=ALU.mult))
                step(dve.tensor_reduce(out=rs[:, at + 1, :], in_=t_, axis=AX, op=ALU.min))
                step(dve.tensor_scalar(rs[:, at + 1, :], rs[:, at + 1, :], 100.0, None, ALU.add))
                step(dve.tensor_tensor(one_hot, numbers, wide(rs[:, at + 1, :]), ALU.is_equal))

            dve.wait_ge(m_const, 3)
            dve.wait_ge(m_tok, 2)
            dve.tensor_copy(hn_tok, ps[:, 2:6, :].rearrange("p (b j) n -> p b (j n)", b=TB)).then_inc(m_tokc, 1)
            dve.wait_ge(m_log, 1)
            step(dve.tensor_copy(logits, ps[:, 6, 0:72].rearrange("p (b e) -> p b e", b=TB)))
            step(dve.tensor_reduce(out=rs[:, 0, :], in_=logits[:, :, 0:NGROUP], axis=AX, op=ALU.max, negate=True))
            step(dve.tensor_copy(slot_no.rearrange("p a b -> p (a b)"), slot_i.bitcast(I32)))
            dve.wait_ge(route_e, 2)
            first_max(logits[:, :, 0:NGROUP], NGROUP, og, og_t, 2)
            step(dve.tensor_tensor(prod.rearrange("p b (g e) -> p b g e", g=NGROUP),
                                   logits[:, :, NGROUP:].rearrange("p b (g e) -> p b g e", g=NGROUP),
                                   og.rearrange("p b (g o) -> p b g o", o=1).to_broadcast([P, TB, NGROUP, PER]),
                                   ALU.mult))
            step(dve.tensor_reduce(out=loc, in_=prod.rearrange("p b (g e) -> p b e g", g=NGROUP), axis=AX,
                                   op=ALU.add))
            first_max(loc, PER, o1, eq8, 4)
            step(dve.scalar_tensor_tensor(out=loc2, in0=o1, scalar=-3e38, in1=loc, op0=ALU.mult, op1=ALU.add))
            assert steps[0] == 18
            step(dve.tensor_reduce(out=rs[:, 6, :], in_=loc2, axis=AX, op=ALU.max))
            step(dve.tensor_tensor(rs[:, 7, :], rs[:, 6, :], rs[:, 4, :], ALU.subtract))
            first_max(loc2, PER, o2, eq8, 9)
            dve.wait_ge(route_e, 3)
            step(dve.tensor_scalar(rs[:, 11, :], rs[:, 8, :], 1.0, None, ALU.add))
            step(dve.tensor_tensor(rs[:, 11, :], rs[:, 11, :], rs[:, 1, :], ALU.mult))
            step(dve.reciprocal(rs[:, 12, :], rs[:, 11, :]))
            step(dve.tensor_tensor(rs[:, 13, :], rs[:, 12, :], rs[:, 8, :], ALU.mult))
            four = lambda a: a.rearrange("p b (g e) -> p b g e", g=NGROUP)
            for o_, m_ in ((o1, M1), (o2, M2)):
                for b in range(TB):
                    step(dve.tensor_tensor(
                        m_[:, b, :].rearrange("p (g e) -> p g e", g=NGROUP),
                        o_[:, b:b + 1, :].to_broadcast([P, NGROUP, PER]),
                        og[:, b, :].rearrange("p (g o) -> p g o", o=1).to_broadcast([P, NGROUP, PER]), ALU.mult))
            for b in range(TB):
                step(dve.tensor_scalar(G[:, b, :], M2[:, b, :], rs[:, 13, b:b + 1], None, ALU.mult))
                step(dve.scalar_tensor_tensor(out=G[:, b, :], in0=M1[:, b, :], scalar=rs[:, 12, b:b + 1],
                                              in1=G[:, b, :], op0=ALU.mult, op1=ALU.add))
            step(dve.tensor_tensor(M1, M1, M2, ALU.add))
            assert steps[0] == ROUTED
            dve.wait_ge(m_rank, 1)
            step(dve.scalar_tensor_tensor(out=R, in0=ps[:, 6, 128:192].rearrange("p (b e) -> p b e", b=TB),
                                          scalar=1.0, in1=M1, op0=ALU.add, op1=ALU.mult))
            step(dve.tensor_scalar(R, R, -1.0, None, ALU.add))
            step(dve.tensor_reduce(out=rs[:, 14, 0:1], in_=ps[:, 6, 192:224], axis=AX, op=ALU.max))
            step(dve.tensor_scalar(flag[:, 0:1], rs[:, 14, 0:1], float(CAP), None, ALU.is_gt))
            dve.tensor_copy(flag[:, 1:2].bitcast(I32), flag[:, 0:1]).then_inc(m_flag, 1)

            def select_e(e, k, pass_=0):
                for b in range(TB):
                    r_ = R[:, b, bass.ds(e, 1)]
                    dve.tensor_scalar(sel[:, k, b, :], slot_no[:, pass_, 0:CAP], r_, None, ALU.is_equal)\
                        .then_inc(m_s, 1)
                    dve.tensor_scalar(gate_sel[:, k, b, :], slot_no[:, pass_, :], r_, G[:, b, bass.ds(e, 1)],
                                      ALU.is_equal, ALU.mult).then_inc(m_s, 1)

            def tokens(n):
                dve.wait_ge(m_g, n + 1)
                dve.tensor_copy(xe.rearrange("p k s -> p (k s)"), ps[:, 7, :]).then_inc(m_x, 1)

            def hidden_e(n):
                dve.wait_ge(m_si, n + 1)
                dve.tensor_tensor(hid_e, silu_e, ps[:, 0, 256:512], ALU.mult).then_inc(m_hd, 1)

            select_e(0, 0)
            select_e(1, 1)
            tokens(0)
            with dve.Fori(0, NE // 2 - 1) as i:
                for b in range(2):
                    hidden_e(2 * i + b)
                    dve.wait_ge(m_t, 2 * i + b + 1)
                    select_e(2 * i + b + 2, b)
                    tokens(2 * i + b + 1)
            hidden_e(NE - 2)
            tokens(NE - 1)
            hidden_e(NE - 1)
            dve.wait_ge(m_flag, 1)
            more = dve.value_load(flag[0:1, 1:2].bitcast(I32), min_val=0, max_val=1)
            with dve.If(more > 0):
                with dve.Fori(0, NE) as e:
                    for p_ in range(3):
                        dve.wait_ge(m_t, 3 * e + NE + p_)
                        select_e(e, 0, p_ + 1)
                        tokens(3 * e + NE + p_)
                        hidden_e(3 * e + NE + p_)
                dve.wait_ge(m_all, 1 + 3 * NE)
            dve.wait_ge(m_all, 1)
            dve.wait_ge(m_out, 1)
            dve.tensor_copy(hn_tok[:, 0, 512:1024], ps[:, 3, :]).then_inc(m_out, 1)
            dve.wait_ge(m_out, 3)
            dve.tensor_copy(hn_tok[:, 1, 512:1024], ps[:, 5, :]).then_inc(m_out, 1)

        @block.tensor
        def _(pe):
            col = [0]

            def linear(p, by_token=False, rhs=u):
                pe.wait_ge(lo_done, p["w"] + 1)
                if p["half"] == 0 and p["engine_before"]:
                    pe.wait_ge(lin_out[p["engine_before"]], p["turn_before"])
                o, hi, lo = lin[p["out"] % 2][:, p["half"], :], piece_buf(p, 0), piece_buf(p, 1)
                blocks = range(TB) if by_token else range(1)
                for b in blocks:
                    for k in range(DC):
                        for n, (w_, x_) in enumerate(((hi, 0), (hi, 1), (lo, 0))):
                            first, last = k == 0 and n == 0, k == DC - 1 and n == 2
                            if by_token:
                                mm = pe.matmul(o[:, P * b:P * (b + 1)], rhs[:, x_, k, P * b:P * (b + 1)],
                                               w_[:, k, :], start=first, stop=last)
                            else:
                                mm = pe.matmul(o, w_[:, k, :], rhs[:, x_, k, :], start=first, stop=last)
                mm.then_inc(piece_done, 1)

            def column(g):
                assert col[0] == g
                pe.wait_ge(gemv_sb, g + 1)
                for m in range(2):
                    mm = pe.matmul(modps[:, 2 * g + m:2 * g + m + 1], gsb[:, g % 2, P * m:P * (m + 1)],
                                   ones[:, 0:1], start=True, stop=True)
                mm.then_inc(gemv_col, 1)
                col[0] += 1

            def gemv(some):
                for s in some:
                    g = gemv_of[s["n"]]
                    if col[0] < g:
                        column(g - 1)
                    elif g in (8, 24):
                        pe.wait_ge(mod_done, {8: 1, 24: 3}[g])
                    pe.wait_ge(slot_in[s["n"] % RING], slot_use(s["n"]))
                    w_ = slot_dst(s)
                    for k in range(DC):
                        j = k % 4
                        mm = pe.matmul(gps[32 * j:32 * j + 32, :], cact[:, k, :], w_[:, k, :],
                                       start=(k < 4), stop=(k >= 4))
                    mm.then_inc(gemv_mm, 1)

            def sums(name):
                pe.wait_ge(sq_done, STATS[name] + 1)
                if STATS[name] > 0:
                    pe.wait_ge(var_done, STATS[name])
                for b in range(TB):
                    for k in range(DC):
                        mm = pe.matmul(stps[:, b:b + 1], sq[:, k, P * b:P * (b + 1)], ones[:, 0:1],
                                       start=(k == 0), stop=(k == DC - 1))
                mm.then_inc(sum_done, 1)

            def spread(name):
                i = STATS[name]
                pe.wait_ge(diag_done, 2 * i + 2)
                if i > 0:
                    pe.wait_ge(scaled, 8 * SCALED_BEFORE[name])
                if name == "mix_2":
                    pe.wait_ge(res_done, 8)
                for b in range(TB):
                    mm = pe.matmul(rbc[:, P * b:P * (b + 1)], ones[:], diag[:, b, :], start=True, stop=True)
                mm.then_inc(bc_done, 1)

            pe.wait_ge(const_done, 4)
            pe.wait_ge(ld_vec, 16 * 22)
            pe.transpose(ps[:, 0, 0:112], rows1[0:112, :], ident[0:112, 0:112]).then_inc(setup_t, 1)
            pe.transpose(ps[:, 1, 0:ROWS2], rows2[0:ROWS2, :], ident[0:ROWS2, 0:ROWS2]).then_inc(setup_t, 1)
            pe.wait_ge(ld_x, 16)
            for c_ in range(DC):
                for b in range(TB):
                    mm = pe.transpose(acc[:, c_, P * b:P * (b + 1)], x_tok[:, b, P * c_:P * (c_ + 1)], ident[:])
                if c_ % 4 == 3:
                    mm.then_inc(setup_t, 1)
            pe.wait_ge(act_order, 1)
            gemv(jobs["gemv_first"])
            column(7)
            sums("mix0")
            spread("mix0")
            pe.wait_ge(setup_c, 2)
            pe.wait_ge(u_lo, 8)
            for p in jobs["zf"] + jobs["q"]:
                linear(p)

            def round_(r):
                q_, k_ = (qA, kA) if r == 0 else (qd, kd)
                if r == 0:
                    pe.wait_ge(a_prep, 17)
                    wait_out(pe, jobs["q"][-1])
                    pe.wait_ge(setup_c, 4)
                else:
                    pe.wait_ge(a_dec, 2 * r)
                for b in range(4):
                    if r > 0:
                        pe.wait_ge(a_cp, 4 * (r - 1) + b + 1)
                    for n in range(4):
                        hh, tb = 2 * b + n // 2, n % 2
                        mm = pe.matmul(ps[:, 2 + b, P * n:P * (n + 1)], k_[:, hh, P * tb:P * (tb + 1)],
                                       q_[:, hh, P * tb:P * (tb + 1)], start=True, stop=True)
                    mm.then_inc(a_mm, 1)

            for r in range(8):
                for n, p in enumerate(jobs[("v" if r < 4 else "g") + str(r)]):
                    gemv(jobs[f"gemv_round{r}"][n:n + 1])
                    linear(p, by_token=r < 4)
                round_(r)
            column(23)
            pe.wait_ge(a_dec, 16)
            for b in range(2):
                pe.wait_ge(a_cp, 28 + b + 1)
                for n in range(4):
                    mm = pe.matmul(ps[:, 2 + b, P * n:P * (n + 1)], kd[:, 4 * b + n, 0:P], qd[:, 4 * b + n, P:T],
                                   start=True, stop=True)
                mm.then_inc(a_mm, 1)
            pe.wait_ge(a_x, 2)
            pe.wait_ge(a_cp, 32)
            for hh in range(HA):
                pe.matmul(acc[:, hh, :], vA[:, 0, P * hh:P * (hh + 1)], attA[:, hh, 0:2, :], start=True, stop=False)
                pe.matmul(acc[:, hh, P:T], vA[:, 1, P * hh:P * (hh + 1)], attA[:, hh, 2, :], start=False,
                          stop=True).then_inc(a_o, 1)
            for hh in range(HA):
                pe.wait_ge(a_sq, hh // 2 + 1)
                for b in range(TB):
                    mm = pe.matmul(stps[:, 2 * hh + b:2 * hh + b + 1], sq[:, hh, P * b:P * (b + 1)], ones[:, 0:1],
                                   start=True, stop=True)
            mm.then_inc(a_ss, 1)
            wait_out(pe, jobs["g7"][-1])
            for hh in range(HA):
                if hh >= 4:
                    pe.wait_ge(a_g, 1)
                for b in range(TB):
                    pe.wait_ge(a_diag, 2 * hh + b + 1)
                    pe.matmul(lin[hh % 4 // 2][:, hh % 2, P * b:P * (b + 1)], ones[:], diag[:, (2 * hh + b) % 4, :],
                              start=True, stop=True).then_inc(a_bc, 1)
            pe.wait_ge(a_g, 2)
            pe.wait_ge(a_lo, 2)
            for p in jobs["a_out"]:
                linear(p)

            def ffn_pe(layer, name):
                sums(name)
                if layer == 0:
                    gemv(jobs["gemv_kv"])
                spread(name)
                pe.wait_ge(u_lo, 8 * (OPERANDS[name] + 1))
                for i in range(FFI + 1):
                    if i < FFI:
                        for p in jobs[f"gate{layer}_{i}"] + jobs[f"up{layer}_{i}"]:
                            linear(p)
                    if i > 0:
                        fi = layer * FFI + i - 1
                        pe.wait_ge(f_lo, fi + 1)
                        for p in jobs[f"down{layer}_{i - 1}"]:
                            pe.wait_ge(lo_done, p["w"] + 1)
                            for jj in range(4):
                                c_ = 4 * p["half"] + jj
                                for k in range(2):
                                    for n, (lo, x_) in enumerate(((0, 0), (0, 1), (1, 0))):
                                        mm = pe.matmul(acc[:, c_, :], piece_buf(p, lo)[:, k, P * jj:P * (jj + 1)],
                                                       hid[:, fi % 2, x_, k, :],
                                                       start=(i == 1 and c_ % 2 == 0 and k == 0 and n == 0),
                                                       stop=(i == FFI and k == 1 and n == 2),
                                                       skip_group_check=True)
                            mm.then_inc(piece_done, 1)
                    if layer == 0:
                        gemv(jobs[f"gemv_ffn{i}"])

            ffn_pe(0, "ffn0")
            column(NG - 1)
            def attention_pe(kind, keys, queries, values, chunks, bias=None):
                first, n = FIRST[kind], COUNT[kind]

                def scores(i):
                    a = first + i
                    if i >= 2:
                        pe.wait_ge(at_b, before_b(a - 1))
                    o = ps[:, 2 + i % 2, :]
                    if bias:
                        pe.matmul(o[:, 0:3 * P], flip[:], bias(i), start=True, stop=False)
                    for block_ in range(TB):
                        at, w = ((0, 256), (256, 256))[block_] if kind == "X" else ((0, 128), (128, 256))[block_]
                        for k in range(chunks):
                            mm = pe.matmul(o[:, at:at + w], queries(i, k)[:, P * block_:P * (block_ + 1)],
                                           keys(i, k)[:, 0:w], start=(k == 0 and not bias),
                                           stop=(k == chunks - 1 and not (bias and block_ == 0)))
                    mm.then_inc(at_s, 1)

                def turn_(i):
                    a = first + i
                    pe.wait_ge(at_p, 3 * a + 3)
                    if i >= 2:
                        pe.wait_ge(at_pt, a - 1)
                    for at, place in blocks(kind):
                        mm = pe.transpose(ps[:, 4 + i % 2, P * place:P * (place + 1)],
                                          pr_sb[:, i % 2, at:at + P], ident[:])
                    mm.then_inc(at_t, 1)

                def outputs(i):
                    a = first + i
                    k, bank_ = o_bank(kind, i)
                    pe.wait_ge(at_pt, a + 1)
                    if k - {"B": 0, "W": 8, "X": 12}[kind] >= 2:
                        pe.wait_ge(at_hi, k - 1)
                        if kind != "W":
                            pe.wait_ge(at_lo, lo_before(k - 1))
                    pt = pt_sb[:, i % 2, :]
                    if kind == "X":
                        for m in range(2):
                            for b in range(TB):
                                mm = pe.matmul(bank_[:, T * m:T * (m + 1)], values(i, b, m), pt[:, T * b:T * (b + 1)],
                                               start=(b == 0), stop=(b == 1))
                    else:
                        rows = slice(64 * (i % 2), 64 * (i % 2) + 64)
                        pe.matmul(bank_[rows, 0:T], values(i, 0, 0), pt[:, 0:T], start=True, stop=False)
                        mm = pe.matmul(bank_[rows, P:T], values(i, 1, 0), pt[:, T:T + P], start=False, stop=True)
                    mm.then_inc(at_o, 1)

                scores(0)
                scores(1)
                for i in range(n + 1):
                    if i < n:
                        turn_(i)
                    if i + 2 < n:
                        scores(i + 2)
                    if i >= 1:
                        outputs(i - 1)

            sums("kv")
            pe.wait_ge(b_rel, 48)
            pe.wait_ge(acc_done, 8)
            for r, n in enumerate((P, P, NREL - 2 * P)):
                mm = pe.transpose(ps[0:HB, 2, P * r:P * r + n], rel_rows[0:n, r, :], ident[0:n, 0:n])
            mm.then_inc(b_relt, 1)
            spread("kv")
            pe.wait_ge(u_lo, 24)
            for p in jobs["kv_k"]:
                linear(p)
            for p in jobs["kv_v"]:
                linear(p, by_token=True)
            pe.wait_ge(u_lo, 32)
            for p in jobs["b_q"]:
                linear(p)
            wait_out(pe, jobs["b_q"][-1])
            pe.wait_ge(b_rel, 96)
            pe.wait_ge(b_bias, 2)
            half = lambda t_, i: t_[64 * (i % 2):64 * (i % 2) + 64, i // 2, :]
            attention_pe("B", lambda i, k: half(kB, i), lambda i, k: half(qB, i),
                         lambda i, b, m: vB[:, b, 64 * i:64 * i + 64], 1, lambda i: biasB[:, i, :])
            pe.wait_ge(at_lo, HB // 2)
            for p in jobs["b_o"]:
                linear(p)
            ffn_pe(1, "ffn1")

            sums("final")
            spread("final")
            sums("mix_2")
            pe.wait_ge(w_ms, 8)
            pe.wait_ge(acc_done, 16)
            for g in range(8):
                mm = pe.transpose(ps[:, 2 + g // 4, P * (g % 4):P * (g % 4 + 1)], wRow[:, g, :], ident[:])
                if g % 4 == 3:
                    mm.then_inc(w_tp, 1)
            spread("mix_2")
            pe.wait_ge(u_lo, 48)
            for n, p in enumerate(jobs["in2"]):
                linear(p, by_token=(n == 5 or n >= 10))
            pe.wait_ge(w_sq, 1)
            pe.wait_ge(w_tc, 2)
            for n in range(5):
                mm = pe.matmul(acc[:, n, :], pair_ones[:], sq[:, n, :], start=True, stop=True)
            mm.then_inc(w_ss, 1)
            pe.wait_ge(w_std, 1)
            pe.wait_ge(w_n, 1)
            for kv in range(2):
                for hf in range(2):
                    mm = pe.matmul(acc[64 * hf:64 * hf + 64, kv, :], ident[:, 64 * kv:64 * kv + 64], kW,
                                   start=True, stop=True)
            mm.then_inc(w_dup, 1)
            pe.wait_ge(w_n, 4)
            for g in range(8):
                for b in range(TB):
                    o = acc[64 * (g % 2):64 * (g % 2) + 64, 4 + g // 2, P * b:P * (b + 1)]
                    pe.matmul(o, gn[:, b, 64 * g:64 * g + 64], wT[:, g, :], start=True, stop=False)
                    mm = pe.matmul(o, ones[0:1, 0:64], sgb[:, P * g:P * (g + 1)], start=False, stop=True)
                if g % 4 == 3:
                    mm.then_inc(w_s, 1)
            pe.wait_ge(w_dc, 1)
            pe.wait_ge(w_sg, 2)
            attention_pe("W", lambda i, k: kdup[64 * (i % 2):64 * (i % 2) + 64, i // 4, :],
                         lambda i, k: half(qW, i), lambda i, b, m: vW[:, b, 64 * (i // 4):64 * (i // 4) + 64], 1)
            pe.wait_ge(w_sq, 4)
            for b in range(2):
                for k in range(4):
                    mm = pe.matmul(ps[:, 6, T * b:T * (b + 1)], ones[:], sq[:, 4 * b + k, :], start=(k == 0),
                                   stop=(k == 3))
            mm.then_inc(w_ss, 1)
            pe.wait_ge(u_lo, 56)
            for p in jobs["out2"]:
                linear(p)

            pe.wait_ge(ld_mem, 16)
            for c_ in range(DC):
                for b in range(TB):
                    mm = pe.transpose(acc[:, c_, P * b:P * (b + 1)], mem_tok[:, b, P * c_:P * (c_ + 1)], ident[:])
                if c_ % 4 == 3:
                    mm.then_inc(x_tp, 1)
            sums("mem")
            spread("mem")
            pe.wait_ge(u_lo, 64)
            for p in jobs["ck"]:
                linear(p)
            for p in jobs["cv"]:
                linear(p, by_token=True)
            sums("cross")
            spread("cross")
            pe.wait_ge(u_lo, 72)
            for p in jobs["cq"]:
                linear(p)
            pe.wait_ge(x_sq, 2)
            pe.wait_ge(x_tc, 2)
            for n, src in enumerate((sq, raw)):
                for hh in range(HX):
                    for k in range(2):
                        mm = pe.matmul(acc[:, 4 * n + hh, :], ones[:], src[:, 2 * hh + k, :], start=(k == 0),
                                       stop=(k == 1))
            mm.then_inc(x_ss, 1)
            pe.wait_ge(x_n, 4)
            wait_out(pe, jobs["cv"][-1])
            attention_pe("X", lambda i, k: kX[:, 2 * i + k, :], lambda i, k: qX[:, 2 * i + k, :],
                         lambda i, b, m: vX[:, b, T * i + P * m:T * i + P * (m + 1)], 2)
            pe.wait_ge(at_lo, 12)
            for p in jobs["co"]:
                linear(p)
            sums("moe")
            spread("moe")
            pe.wait_ge(m_hn, 8)
            for b in range(TB):
                for c_ in range(DC):
                    mm = pe.transpose(ps[:, 2 + 2 * b + c_ // 4, P * (c_ % 4):P * (c_ % 4 + 1)],
                                      sq[:, c_, P * b:P * (b + 1)], ident[:])
                mm.then_inc(m_tok, 1)
            pe.wait_ge(m_wr, 80)
            for b in range(TB):
                for k in range(DC):
                    mm = pe.matmul(ps[:, 6, 36 * b:36 * (b + 1)], sq[:, k, P * b:P * (b + 1)], wr[:, k, :],
                                   start=(k == 0), stop=(k == DC - 1))
            mm.then_inc(m_log, 1)
            pe.wait_ge(m_tokc, 1)
            for b in range(TB):
                for c_ in range(DC):
                    pe.matmul(ps[:, 2 + 2 * b + c_ // 4, P * (c_ % 4):P * (c_ % 4 + 1)],
                              h[:, c_, P * b:P * (b + 1)], ident[:], start=(c_ % 4 == 0), stop=False,
                              skip_group_check=True)
            pe.wait_ge(route, ROUTED)
            pe.matmul(ps[:, 6, 128:160], tri, M1[:, 0, :], start=True, stop=True)
            pe.matmul(ps[:, 6, 160:192], tri, M1[:, 1, :], start=True, stop=False)
            pe.matmul(ps[:, 6, 160:192], ones[:], M1[:, 0, :], start=False, stop=True)
            pe.matmul(ps[:, 6, 192:224], ones[:], M1[:, 0, :], start=True, stop=False)
            pe.matmul(ps[:, 6, 192:224], ones[:], M1[:, 1, :], start=False, stop=True).then_inc(m_rank, 1)

            def gather(n, k):
                pe.wait_ge(m_s, 4 * n + 4)
                for c_ in range(DC):
                    for b in range(TB):
                        mm = pe.matmul(ps[:, 7, CAP * c_:CAP * (c_ + 1)], hn_tok[:, b, P * c_:P * (c_ + 1)],
                                       sel[:, k, b, :], start=(b == 0), stop=(b == TB - 1))
                mm.then_inc(m_g, 1)

            def up(n, k, loaded):
                pe.wait_ge(m_x, n + 1)
                pe.wait_ge(w13_in[k], loaded)
                for m in range(2):
                    for c_ in range(DC):
                        for j in range(2):
                            mm = pe.matmul(ps[64 * j:64 * j + 64, 0, 256 * m:256 * (m + 1)], xe[:, c_, :],
                                           w13[k][:, m, c_, 256 * j:256 * (j + 1)], start=(c_ == 0),
                                           stop=(c_ == DC - 1))
                mm.then_inc(m_h, 1)

            def turn_e(n, k):
                pe.wait_ge(m_hd, n + 1)
                for m in range(2):
                    pe.transpose(ps[:, 1, P * m:P * (m + 1)], hid_e[:, P * m:P * (m + 1)], ident[:])
                for b in range(TB):
                    mm = pe.transpose(ps[:, 1, 256 + P * b:256 + P * (b + 1)], gate_sel[:, k, b, :], ident[:])
                mm.then_inc(m_t, 1)

            def down(n, k, loaded):
                pe.wait_ge(m_tc, n + 1)
                pe.wait_ge(w2_in[k], loaded)
                for m in range(2):
                    for jk in range(2):
                        for j in range(2):
                            mm = pe.matmul(ps[64 * j:64 * j + 64, 6, :], tt[:, P * m + 64 * jk:P * m + 64 * jk + 64],
                                           w2b[k][:, 2 * jk + m, 512 * j:512 * (j + 1)],
                                           start=(m == 0 and jk == 0), stop=(m == 1 and jk == 1))
                mm.then_inc(m_y, 1)

            def scatter(n):
                pe.wait_ge(m_yc, n)
                for b in range(TB):
                    for j in range(2):
                        mm = pe.matmul(ps[:, 2 + 2 * b + j, :], tt[64 * j:64 * j + 64, 256 + P * b:256 + P * (b + 1)],
                                       y_sb[64 * j:64 * j + 64, :], start=False, stop=False, skip_group_check=True)
                return mm

            def middle(n, k, loaded, last=False):
                up(n, k, loaded)
                scatter(n)
                turn_e(n, k)
                if not last:
                    gather(n + 1, 1 - k)
                down(n, k, loaded // 2)

            pe.wait_ge(route, ROUTED + 4)
            pe.wait_ge(m_tokc, 1)
            gather(0, 0)
            up(0, 0, 32)
            turn_e(0, 0)
            gather(1, 1)
            down(0, 0, 16)
            with pe.Fori(0, NE // 2 - 1) as i:
                middle(2 * i + 1, 1, 32 * i + 32)
                middle(2 * i + 2, 0, 32 * i + 64)
            middle(NE - 1, 1, 16 * NE, last=True)
            scatter(NE).then_inc(m_all, 1)
            pe.wait_ge(m_flag, 1)
            more = pe.value_load(flag[0:1, 1:2].bitcast(I32), min_val=0, max_val=1)
            with pe.If(more > 0):
                with pe.Fori(0, NE) as e:
                    for p_ in range(3):
                        n = 3 * e + NE + p_
                        gather(n, 0)
                        up(n, 0, 32 * e + 16 * NE + 32)
                        turn_e(n, 0)
                        down(n, 0, 16 * e + 8 * NE + 16)
                        scatter(n + 1).then_inc(m_all, 1)


_INPUTS = ["x", "c", "mod_w", "mod_b", "norm_mix", "norm_ffn", "ffn_w_in", "ffn_w_out", "a_w_in", "a_w_out",
           "a_lb", "a_out_norm", "kv_norm", "kv_mod_w", "kv_mod_b", "kv_w", "b_w_q", "b_w_o", "b_rel_bias",
           "final_norm", "mem_2", "norm_mix_2", "w_in_2", "q_norm_2", "k_norm_2", "attn_sinks_2",
           "sgu_norm_2", "sgu_w_2", "sgu_b_2", "out_norm_attn_2", "out_norm_sgu_2", "w_out_2",
           "norm_cross_2", "norm_mem_2", "w_cq_2", "w_ck_2", "w_cv_2", "cq_norm_2", "ck_norm_2", "w_co_2",
           "norm_ffn_2", "w_router_group_2", "w_router_expert_2", "w1_2", "w3_2", "w2_2"]


def kernel(**inputs):
    import numpy as np
    from concourse import bacc
    from concourse.bass_utils import run_bass_kernel_spmd

    nc = bacc.Bacc("TRN2", target_bir_lowering=False, num_devices=1)
    arrays, args = {}, []
    for name in _INPUTS:
        array = np.ascontiguousarray(inputs[name])
        arrays[f"in_{name}"] = array
        args.append(nc.dram_tensor(f"in_{name}", array.shape, mybir.dt.from_np(array.dtype),
                                   kind="ExternalInput").ap())
    out = nc.dram_tensor("out_0", (1, T, D), F32, kind="ExternalOutput")
    two_blocks(nc, *args, out.ap())
    result = run_bass_kernel_spmd(nc, [arrays], core_ids=[0])
    return result.results[0]["out_0"]
```

```python
from contextlib import ExitStack

import concourse.bass as bass
from concourse import mybir

P = 128
ALU = mybir.AluOpType
ACT = mybir.ActivationFunctionType
F32 = mybir.dt.float32
F32R = mybir.dt.float32r
I32 = mybir.dt.int32
U8 = mybir.dt.uint8
AX = mybir.AxisListType.X

D = 1024
DC = D // P
T = 256
TB = T // P
FFN = 2816
FFI = FFN // 256
HA = 8
HB = 16
NREL = 320
HW = 8
HX = 4
NE = 32
NGROUP = 4
PER = NE // NGROUP
DE = 512
CAP = 64
EPS = 1e-6
MIN_FORGET = 1e-30
MASKED = -1e30

RING = 6
SLOT = 2048
NBUF = 4
LOOKAHEAD = NBUF - 1

MOD0, MODKV, MOD1 = 0, 48, 64
VEC = {}


def table2():
    at = 0
    for name, rows in (("norm_mix", 16), ("norm_ffn", 16), ("a_lb", 8), ("kv_norm", 8), ("final_norm", 8),
                       ("norm_mix_2", 8), ("norm_cross_2", 8), ("norm_mem_2", 8), ("norm_ffn_2", 8),
                       ("a_out_norm", 1), ("out_norm_attn_2", 4), ("out_norm_sgu_2", 4), ("cq_norm_2", 2),
                       ("ck_norm_2", 2)):
        VEC[name] = at
        at += rows
    VEC["q_norm_2"], VEC["k_norm_2"] = at, at + 1
    return at + 2


ROWS2 = table2()


def plan():
    slots, pieces, jobs = [], [], {}
    turn = {"act": 0, "dve": 0}
    outs = []

    def slot(kind, matrix, at):
        slots.append({"kind": kind, "matrix": matrix, "at": at, "n": len(slots)})
        return slots[-1]

    def gemv(name, matrix, n):
        jobs[name] = [slot("gemv", matrix, 256 * i) for i in range(n)]

    def piece(s, half, job, engine=None):
        p = {"w": len(pieces), "slot": s["n"], "half": half, "engine": engine}
        if engine:
            if half == 0:
                outs.append(engine)
                turn[engine] += 1
            n = len(outs) - 1
            p["out"], p["turn"] = n, turn[engine]
            p["engine_before"] = outs[n - 2] if n >= 2 else None
            p["turn_before"] = outs[:n - 1].count(outs[n - 2]) if n >= 2 else 0
        s.setdefault("pieces", []).append(p["w"])
        pieces.append(p)
        jobs.setdefault(job, []).append(p)
        return p

    def linear(job, matrix, first, n, engine):
        for i in range(n):
            s = slot("lin", matrix, first + 256 * i)
            for half in range(2):
                piece(s, half, job, engine)

    done = [0]

    def ffn(layer, with_gemv):
        for i in range(FFI + 1):
            if i < FFI:
                for part, engine in (("gate", "act"), ("up", "dve")):
                    s = slot("lin", f"ffn_in{layer}", 256 * i + (FFN if part == "up" else 0))
                    for half in range(2):
                        piece(s, half, f"{part}{layer}_{i}", engine)
            if i > 0:
                s = slot("out", f"ffn_out{layer}", 256 * (i - 1))
                for half in range(2):
                    piece(s, half, f"down{layer}_{i - 1}")
            if with_gemv:
                jobs[f"gemv_ffn{i}"] = []
                for _ in range(3 if i < 8 else 2):
                    matrix, at = ("modkv", 256 * done[0]) if done[0] < 8 else ("mod1", 256 * (done[0] - 8))
                    jobs[f"gemv_ffn{i}"].append(slot("gemv", matrix, at))
                    done[0] += 1

    gemv("gemv_first", "mod0", 8)
    linear("zf", "a_in", D, 4, "act")
    linear("q", "a_in", 0, 4, "act")
    for r in range(8):
        part, first = ("v", 2 * D) if r < 4 else ("g", 3 * D)
        linear(part + str(r), "a_in", first + 256 * (r % 4), 1, "act")
        gemv(f"gemv_round{r}", "mod0", 2)
        for k, s in enumerate(jobs[f"gemv_round{r}"]):
            s["at"] = 2048 + 256 * (2 * r + k)
    linear("a_out", "a_out", 0, 4, "dve")
    ffn(0, True)
    linear("kv_k", "kv", 0, 4, "act")
    linear("kv_v", "kv", D, 4, "act")
    linear("b_q", "b_q", 0, 4, "act")
    linear("b_o", "b_o", 0, 4, "dve")
    ffn(1, False)
    linear("in2", "in2", 0, 7, "act")
    linear("out2", "out2", 0, 4, "dve")
    linear("ck", "ck", 0, 4, "act")
    linear("cv", "cv", 0, 4, "act")
    linear("cq", "cq", 0, 4, "act")
    linear("co", "co", 0, 4, "dve")
    return slots, pieces, jobs


def two_blocks(nc, x, c, mod_w, mod_b, norm_mix, norm_ffn, ffn_w_in, ffn_w_out, a_w_in, a_w_out, a_lb,
               a_out_norm, kv_norm, kv_mod_w, kv_mod_b, kv_w, b_w_q, b_w_o, b_rel_bias, final_norm, mem_2,
               norm_mix_2, w_in_2, q_norm_2, k_norm_2, attn_sinks_2, sgu_norm_2, sgu_w_2, sgu_b_2,
               out_norm_attn_2, out_norm_sgu_2, w_out_2, norm_cross_2, norm_mem_2, w_cq_2, w_ck_2, w_cv_2,
               cq_norm_2, ck_norm_2, w_co_2, norm_ffn_2, w_router_group_2, w_router_expert_2, w1_2, w3_2,
               w2_2, out):
    slots, pieces, jobs = plan()
    matrices = {"mod0": mod_w[0], "mod1": mod_w[1], "modkv": kv_mod_w, "a_in": a_w_in[0], "a_out": a_w_out[0],
                "ffn_in0": ffn_w_in[0], "ffn_in1": ffn_w_in[1], "ffn_out0": ffn_w_out[0],
                "ffn_out1": ffn_w_out[1], "kv": kv_w, "b_q": b_w_q[0], "b_o": b_w_o[0], "in2": w_in_2,
                "out2": w_out_2, "ck": w_ck_2, "cv": w_cv_2, "cq": w_cq_2, "co": w_co_2}
    gemv_of = {}
    for s in slots:
        if s["kind"] == "gemv":
            gemv_of[s["n"]] = len(gemv_of)
    NG = len(gemv_of)

    with ExitStack() as ctx:
        def sb(name, shape, dt=F32):
            return ctx.enter_context(nc.sbuf_tensor(name, shape, dt))

        def sem(name):
            return ctx.enter_context(nc.semaphore(name))

        ARENA = RING * SLOT + 19456
        arena = sb("arena", [P, ARENA])

        def part(at, *shape, base=RING * SLOT, rows=P):
            n = 1
            for k in shape:
                n *= k
            assert base + at + n <= ARENA
            flat = arena[0:rows, base + at:base + at + n]
            if len(shape) == 1:
                return flat
            names = "abcd"[:len(shape)]
            return flat.rearrange(f"p ({' '.join(names)}) -> p {' '.join(names)}",
                                  **{k: v for k, v in zip(names, shape)})

        ring = [arena[:, SLOT * n:SLOT * (n + 1)] for n in range(RING)]
        wsplit = sb("wsplit", [P, NBUF, 2, 1024], F32R)
        u = sb("u", [P, 2, DC, T], F32R)
        hid = sb("hid", [P, 2, 2, 2, T], F32R)
        h = sb("h", [P, DC, T])
        sq = sb("sq", [P, DC, T])
        vec1 = sb("vec1", [P, 112])
        vec2 = sb("vec2", [P, ROWS2])
        ident = sb("ident", [P, P])
        ones = sb("ones", [P, P])
        mod = sb("mod", [P, 112])
        gain = sb("gain", [P, 5, DC])
        lbs = sb("lbs", [P, 4, HA])
        gsb = sb("gsb", [P, 2, 256])
        cact = sb("cact", [P, DC, 32])
        stat = sb("stat", [P, 64])
        diag = sb("diag", [P, 4, P])
        small = sb("small", [P, 3, 64])

        def vec(name, i=0):
            return vec2[:, VEC[name] + i:VEC[name] + i + 1]

        FP, GS, qA, kA, qd, kd = (part(2048 * i, HA, T) for i in range(6))
        vA = part(12288, TB, D)
        gA = part(14336, HA, T)
        attA = part(16384, HA, 3, P)
        silu_g = part(0, 2, 2, T)
        hidden = part(1024, 2, 2, T)
        qB, kB = part(0, DC, T), part(2048, DC, T)
        vB = part(4096, TB, D)
        biasB = part(6144, HB, 3 * P)
        sc_sb, pr_sb, pt_sb = (part(12288 + 1024 * i, 2, 512) for i in range(3))
        rel_rows = part(15360, 3, HB)
        relT = part(15488, 384)
        k_raw = part(1024, T)
        qW = part(1280, 4, T)
        kW = part(2304, T)
        vW = part(2560, TB, P)
        uW = part(2816, 4, T)
        gW = part(3840, TB, 512)
        gn = part(4864, TB, 512)
        wT = part(5888, 8, P)
        wRow = part(6912, 8, P)
        mix = part(7936, DC, T)
        gain_bc = part(9984, 512)
        sgb = part(10496, 1024, rows=1)
        winmask = part(11520, 3, P)
        causal_f = part(11904, P)
        sinks = part(12032, HW)
        memT = part(0, DC, T)
        kX, qX = part(2048, DC, T), part(4096, DC, T)
        vX = part(6144, TB, D)
        raw = part(8192, DC, T)
        x_tok = part(0, TB, D)
        c_row = part(2304, P, rows=DC)
        rows1, rows2 = part(2048, P), part(2176, P)
        mem_tok = part(10240, TB, D)

        ps = ctx.enter_context(nc.psum_tensor("ps", [P, 8, 512], F32))
        lin = [ps[:, n, :].rearrange("p (c t) -> p c t", c=2) for n in range(2)]
        acc = ps[:, 2:6, :].rearrange("p b (c t) -> p (b c) t", t=T)
        gps = lambda g: ps[:, 6 + g % 2, 0:256]
        modps = ps[:, 6, 256:368]
        rbc = ps[:, 7, 0:256]
        stps = ps[:, 7, 256:320]

        slot_in = [sem(f"slot_in{n}") for n in range(RING)]
        hi_done = sem("hi_done")
        lo_done = sem("lo_done")
        piece_done = sem("piece_done")
        lin_out = {"act": sem("lin_out_act"), "dve": sem("lin_out_dve")}
        gemv_mm = sem("gemv_mm")
        gemv_sb = sem("gemv_sb")
        gemv_col = sem("gemv_col")
        mod_done = sem("mod_done")
        ld_x, ld_vec, ld_mem = sem("ld_x"), sem("ld_vec"), sem("ld_mem")
        const_done = sem("const_done")
        setup_t = sem("setup_t")
        setup_c = sem("setup_c")
        act_order = sem("act_order")
        sq_done = sem("sq_done")
        sum_done = sem("sum_done")
        std_done = sem("std_done")
        rstd_done = sem("rstd_done")
        diag_done = sem("diag_done")
        bc_done = sem("bc_done")
        scaled = sem("scaled")
        u_hi, u_lo = sem("u_hi"), sem("u_lo")

        block = ctx.enter_context(nc.Block())

        def slot_use(n):
            return 16 * (n // RING + 1)

        def slot_src(s):
            w = matrices[s["matrix"]]
            if s["kind"] == "out":
                return w[s["at"]:s["at"] + 256, :].rearrange("(k p) n -> p k n", p=P)
            return w.rearrange("(k p) n -> p k n", p=P)[:, :, s["at"]:s["at"] + 256]

        def slot_dst(s):
            return ring[s["n"] % RING].rearrange("p (k n) -> p k n", k=2 if s["kind"] == "out" else DC)

        def piece_src(p):
            s = slots[p["slot"]]
            if s["kind"] == "out":
                return slot_dst(s)[:, :, 512 * p["half"]:512 * (p["half"] + 1)]
            return slot_dst(s)[:, :, P * p["half"]:P * (p["half"] + 1)]

        def piece_buf(p, lo):
            b = wsplit[:, p["w"] % NBUF, lo, :]
            return b.rearrange("p (k n) -> p k n", k=2 if slots[p["slot"]]["kind"] == "out" else DC)

        def wait_out(eng, p):
            eng.wait_ge(lin_out[p["engine"]], p["turn"])

        STATS = {name: i for i, name in enumerate(
            ("mix0", "ffn0", "kv", "ffn1", "mix_2", "mem", "cross", "moe"))}
        OPERANDS = {name: i for i, name in enumerate(
            ("mix0", "ffn0", "kv", "mix1", "ffn1", "mix_2", "mixed", "mem", "cross"))}
        SCALED_BEFORE = {"ffn0": 1, "kv": 2, "ffn1": 4, "mix_2": 5, "mem": 7, "cross": 8, "moe": 9}
        SQ_FREE = {"mix0": [], "ffn0": [], "kv": [(u_lo, 16)], "ffn1": [(u_lo, 32)],
                   "mix_2": [(u_lo, 40)], "mem": [(u_lo, 56)], "cross": [(u_lo, 64)],
                   "moe": [(u_lo, 72)]}


        ld_c = sem("ld_c")
        c_t = sem("c_t")
        f_hi, f_lo = sem("f_hi"), sem("f_lo")
        acc_done = sem("acc_done")
        res_done = sem("res_done")
        a_prep = sem("a_prep")
        a_init = sem("a_init")
        a_dec = sem("a_dec")
        a_fg = sem("a_fg")
        a_mm = sem("a_mm")
        a_cp = sem("a_cp")
        a_x = sem("a_x")
        a_o = sem("a_o")
        a_sq = sem("a_sq")
        a_ss = sem("a_ss")
        a_var, a_std, a_rs = sem("a_var"), sem("a_std"), sem("a_rs")
        a_diag = sem("a_diag")
        a_bc = sem("a_bc")
        a_t = sem("a_t")
        a_og = sem("a_og")
        a_g = sem("a_g")
        a_hi, a_lo = sem("a_hi"), sem("a_lo")
        out_done = sem("out_done")

        LAST = {job: ps_[-1]["w"] for job, ps_ in jobs.items() if "w" in ps_[-1]}
        masks = sb("masks", [P, 8, P], U8)
        xor_i = part(12288, 3, P)

        def pairs(job):
            return [jobs[job][n:n + 2] for n in range(0, len(jobs[job]), 2)]

        def bank(pair):
            return lin[pair[0]["out"] % 2]

        LEVELS = [1, 2, 4, 8, 16, 32, 64]

        def halves(m, H, upper):
            v = m.rearrange("p h (b two j) -> p (h b) two j", two=2, j=H)
            return v[:, :, 1 if upper else 0, :]

        HEADS = [("B", n) for n in range(HB)] + [("W", n) for n in range(HW)] + [("X", n) for n in range(HX)]
        FIRST = {"B": 0, "W": HB, "X": HB + HW}
        COUNT = {"B": HB, "W": HW, "X": HX}
        at_s = sem("at_s")
        at_b = sem("at_b")
        at_e = sem("at_e")
        at_p = sem("at_p")
        at_t = sem("at_t")
        at_pt = sem("at_pt")
        at_o = sem("at_o")
        at_hi = sem("at_hi")
        at_lo = sem("at_lo")

        def before_b(a):
            return (2 * min(a, HB) + 5 * min(max(a - FIRST["W"], 0), HW) + 3 * max(a - FIRST["X"], 0))

        def runs(kind):
            if kind == "X":
                return slice(0, 256), slice(256, 512), slice(0, 512)
            if kind == "W":
                return slice(0, 129), slice(129, 386), slice(1, 385)
            return slice(0, 128), slice(128, 384), slice(0, 384)

        def blocks(kind):
            if kind == "X":
                return [(0, 0), (128, 2), (256, 1), (384, 3)]
            off = 1 if kind == "W" else 0
            return [(off, 0), (off + 128, 1), (off + 256, 2)]

        def drains(kind, i):
            if kind == "X":
                return 12 + i
            return {"B": 0, "W": 8}[kind] + i // 2 if i % 2 == 1 else None

        def o_bank(kind, i):
            k = 12 + i if kind == "X" else {"B": 0, "W": 8}[kind] + i // 2
            return k, ps[:, 6 + k % 2, :]

        def lo_before(k):
            return k if k <= 8 else 8 + max(k - 12, 0)

        fin = sem("fin")
        fin_sq = sem("fin_sq")
        sq_final = mix
        b_rel = sem("b_rel")
        b_relt = sem("b_relt")
        b_zero = sem("b_zero")
        b_bias = sem("b_bias")
        scratch = nc.dram_tensor("rel_by_head", [HB, 3 * P], F32).ap()
        w_ld = sem("w_ld")
        w_ms = sem("w_ms")
        w_tp = sem("w_tp")
        w_tc = sem("w_tc")
        w_sq = sem("w_sq")
        w_ss = sem("w_ss")
        w_std = sem("w_std")
        w_rs = sem("w_rs")
        w_n = sem("w_n")
        w_dup = sem("w_dup")
        w_dc = sem("w_dc")
        w_s = sem("w_s")
        w_sg = sem("w_sg")
        x_tp, x_tc = sem("x_tp"), sem("x_tc")
        x_sq, x_ss, x_std, x_rs, x_n = (sem("x_" + n) for n in ("sq", "ss", "std", "rs", "n"))
        flip = sb("flip", [P, P])
        pair_ones = sb("pair_ones", [P, P])
        q_rstd = stat[:, 32:48]
        kdup = part(15360, 2, T)
        gst = part(15872, 8)
        k_std = part(12288, T)
        half_std = part(12288, 2, T)
        x_rstd = part(12288, 4, T)
        mem_tok = part(17024, TB, D)
        m_hn = sem("m_hn")
        m_tok = sem("m_tok")
        m_tokc = sem("m_tokc")
        m_const = sem("m_const")
        m_wr = sem("m_wr")
        m_log = sem("m_log")
        m_acc = sem("m_acc")
        route = sem("route")
        route_e = sem("route_e")
        m_rank = sem("m_rank")
        m_flag = sem("m_flag")
        w13_in = [sem("w13_in0"), sem("w13_in1")]
        w2_in = [sem("w2_in0"), sem("w2_in1")]
        m_s = sem("m_s")
        m_g = sem("m_g")
        m_x = sem("m_x")
        m_h = sem("m_h")
        m_si = sem("m_si")
        m_hd = sem("m_hd")
        m_t = sem("m_t")
        m_tc = sem("m_tc")
        m_y = sem("m_y")
        m_yc = sem("m_yc")
        m_all = sem("m_all")
        m_out = sem("m_out")
        wbuf = [arena[:, RING * SLOT:2 * RING * SLOT], arena[:, 0:RING * SLOT]]
        w13 = [b_[:, 0:8192].rearrange("p (m k n) -> p m k n", m=2, k=DC) for b_ in wbuf]
        w2b = [b_[:, 8192:12288].rearrange("p (k n) -> p k n", k=4) for b_ in wbuf]
        hn_tok = part(12288, TB, D)
        xe = part(14336, DC, CAP)
        tt = part(14848, 512)
        y_sb = part(15360, 512)
        silu_e = part(15872, 256)
        hid_e = part(16128, 256)
        sel = part(16384, 2, TB, CAP)
        gate_sel = part(16640, 2, TB, 2 * CAP)
        slot_no = part(17152, 4, 2 * CAP)
        wr = part(17664, DC, NGROUP + NE)
        logits = part(17952, TB, NGROUP + NE)
        tri = part(18048, P)
        M1, M2, R, G = (part(18176 + 64 * i, TB, NE) for i in range(4))
        prod = part(18432, TB, NE)
        og, og_t = part(18496, TB, NGROUP), part(18504, TB, NGROUP)
        o1, o2, loc, loc2, eq8, eq_t = (part(18512 + 16 * i, TB, PER) for i in range(6))
        rs = part(18608, 16, TB)
        flag = part(18640, 4)
        slot_i = part(18688, 4 * 2 * CAP)
        CROSS_DONE = jobs["co"][-1]["turn"]

        def w_expert(w, n):
            return w[bass.ds(n, 1)].rearrange("o (k p) n -> p (o k) n", p=P)
        ROUTED = 39
        @block.sync
        def _(sp):
            sp.dma_start(x_tok, x[0].rearrange("(b p) d -> p b d", p=P)).then_inc(ld_x, 16)
            for s in slots:
                n = s["n"]
                if n >= RING:
                    old = slots[n - RING]
                    if old["kind"] == "gemv":
                        sp.wait_ge(gemv_mm, gemv_of[old["n"]] + 1)
                    else:
                        sp.wait_ge(lo_done, old["pieces"][-1] + 1)
                sp.dma_start(slot_dst(s), slot_src(s)).then_inc(slot_in[n % RING], 16)
            sp.wait_ge(at_lo, 12)
            for n in range(2):
                if n == 1:
                    sp.wait_ge(lo_done, LAST["co"] + 1)
                sp.dma_start(w13[n][:, 0], w_expert(w1_2, n)).then_inc(w13_in[n], 16)
                sp.dma_start(w13[n][:, 1], w_expert(w3_2, n)).then_inc(w13_in[n], 16)
                sp.dma_start(w2b[n], w_expert(w2_2, n)).then_inc(w2_in[n], 16)
            with sp.Fori(0, NE // 2 - 1) as i:
                for b in range(2):
                    sp.wait_ge(m_h, 2 * i + b + 1)
                    sp.dma_start(w13[b][:, 0], w_expert(w1_2, 2 * i + 2 + b)).then_inc(w13_in[b], 16)
                    sp.dma_start(w13[b][:, 1], w_expert(w3_2, 2 * i + 2 + b)).then_inc(w13_in[b], 16)
                    sp.wait_ge(m_y, 2 * i + b + 1)
                    sp.dma_start(w2b[b], w_expert(w2_2, 2 * i + 2 + b)).then_inc(w2_in[b], 16)
            sp.wait_ge(m_flag, 1)
            more = sp.value_load(flag[0:1, 1:2].bitcast(I32), min_val=0, max_val=1)
            with sp.If(more > 0):
                sp.wait_ge(m_y, NE)
                with sp.Fori(0, NE) as e:
                    sp.wait_ge(m_y, 3 * e + NE)
                    sp.dma_start(w13[0][:, 0], w_expert(w1_2, e)).then_inc(w13_in[0], 16)
                    sp.dma_start(w13[0][:, 1], w_expert(w3_2, e)).then_inc(w13_in[0], 16)
                    sp.dma_start(w2b[0], w_expert(w2_2, e)).then_inc(w2_in[0], 16)
            for b in range(TB):
                sp.wait_ge(m_out, 2 * b + 2)
                sp.dma_start(out[0][P * b:P * (b + 1), :], hn_tok[:, b, :]).then_inc(out_done, 16)
            sp.wait_ge(out_done, 32)

        @block.gpsimd
        def _(pool):
            pool.memset(ones[:], 1.0).then_inc(const_done, 1)
            pool.memset(ident[:], 0.0).then_inc(const_done, 1)
            pool.memset(cact[:], 0.0).then_inc(const_done, 1)
            pool.wait_ge(const_done, 3)
            pool.affine_select(out=ident[:], in_=ident[:], compare_op=ALU.not_equal, fill=1.0, base=0,
                               pattern=[[-1, P]], channel_multiplier=1).then_inc(const_done, 1)
            pool.iota(xor_i[:, 0, :].bitcast(I32), pattern=[[0, P]], base=0, channel_multiplier=1).then_inc(const_done, 1)
            pool.iota(xor_i[:, 1, :].bitcast(I32), pattern=[[1, P]], base=0, channel_multiplier=0).then_inc(const_done, 1)
            pool.wait_ge(setup_c, 4)
            pool.memset(GS, 1.0).then_inc(a_init, 1)
            pool.memset(qd, 0.0).then_inc(a_init, 1)
            pool.memset(attA, 0.0).then_inc(a_init, 1)
            pool.memset(pair_ones[:], 0.0).then_inc(w_ms, 1)
            pool.memset(flip[:], 0.0).then_inc(b_zero, 1)
            pool.wait_ge(w_ms, 1)
            pool.wait_ge(b_zero, 1)
            pool.affine_select(out=flip[:], in_=flip[:], compare_op=ALU.not_equal, fill=1.0, base=1 - P,
                               pattern=[[1, P]], channel_multiplier=1).then_inc(b_zero, 1)
            pool.wait_ge(b_zero, 2)
            pool.memset(pair_ones[0:64, 0:64], 1.0).then_inc(w_ms, 1)
            pool.memset(pair_ones[64:128, 64:128], 1.0).then_inc(w_ms, 1)
            pool.wait_ge(a_lo, 2)
            for r, n in enumerate((P, P, NREL - 2 * P)):
                pool.dma_start(rel_rows[0:n, r, :], b_rel_bias[0][P * r:P * r + n, :]).then_inc(b_rel, 16)
            pool.memset(relT[0:HB, :], 0.0).then_inc(b_zero, 1)
            pool.wait_ge(b_relt, 2)
            pool.dma_start(scratch, relT[0:HB, :]).then_inc(b_rel, 16)
            pool.wait_ge(b_rel, 64)
            pool.dma_start(biasB[:, :, 0:P], bass.AP(scratch.tensor, 129, [[1, P], [3 * P, HB], [1, P]]))\
                .then_inc(b_rel, 16)
            pool.dma_start(biasB[:, :, P:3 * P], bass.AP(scratch.tensor, 1, [[1, P], [3 * P, HB], [1, 2 * P]]))\
                .then_inc(b_rel, 16)
            pool.wait_ge(b_rel, 96)
            pool.memset(biasB[64:128, :, 64:128], MASKED).then_inc(b_bias, 1)
            pool.memset(biasB[64:128, :, P + 192:3 * P], MASKED).then_inc(b_bias, 1)
            pool.wait_ge(at_lo, HB // 2)
            pool.dma_start(wRow, sgu_w_2.rearrange("g i j -> i g j")).then_inc(w_ld, 16)
            pool.dma_start(gain_bc, bass.AP(sgu_norm_2.tensor, 0, [[0, P], [1, 512]])).then_inc(w_ld, 16)
            pool.dma_start(sinks, bass.AP(attn_sinks_2.tensor, 0, [[0, P], [1, HW]])).then_inc(w_ld, 16)
            pool.dma_start(sgb, bass.AP(sgu_b_2.tensor, 0, [[0, 1], [1, 8 * P]])).then_inc(w_ld, 16)
            pool.dma_start(mem_tok, mem_2[0].rearrange("(b p) d -> p b d", p=P)).then_inc(ld_mem, 16)
            pool.memset(winmask, 0.0).then_inc(w_ms, 1)
            pool.wait_ge(w_ms, 4)
            for n, sign in ((0, 1), (1, -1), (2, 1)):
                pool.affine_select(out=winmask[:, n, :], in_=winmask[:, n, :],
                                   compare_op=ALU.is_ge if sign > 0 else ALU.is_ge, fill=MASKED,
                                   base=0 if sign > 0 else -1, pattern=[[-sign, P]],
                                   channel_multiplier=sign).then_inc(w_ms, 1)
            pool.wait_ge(w_ld, 64)
            pool.affine_select(out=wRow, in_=wRow, compare_op=ALU.is_ge, fill=0.0, base=0,
                               pattern=[[0, 8], [-1, P]], channel_multiplier=1).then_inc(w_ms, 1)
            pool.wait_ge(x_tc, 2)
            pool.wait_ge(at_lo, 12)
            pool.iota(slot_i.bitcast(I32).rearrange("p (a b c) -> p a b c", a=4, b=2),
                      pattern=[[CAP, 4], [0, 2], [1, CAP]], base=0, channel_multiplier=0).then_inc(m_const, 1)
            pool.memset(tri, 1.0).then_inc(m_const, 1)
            pool.wait_ge(m_const, 2)
            pool.affine_select(out=tri, in_=tri, compare_op=ALU.is_gt, fill=0.0, base=0, pattern=[[1, P]],
                               channel_multiplier=-1).then_inc(m_const, 1)
            pool.dma_start(wr[:, :, 0:NGROUP], w_router_group_2.rearrange("(k p) g -> p k g", p=P)).then_inc(m_wr, 16)
            for g in range(NGROUP):
                pool.dma_start(wr[:, :, NGROUP + PER * g:NGROUP + PER * (g + 1)],
                               w_router_expert_2[g].rearrange("(k p) e -> p k e", p=P)).then_inc(m_wr, 16)

        @block.scalar
        def _(act):
            split = [0]

            def hi_upto(w):
                while split[0] <= min(w, len(pieces) - 1):
                    p = pieces[split[0]]
                    act.wait_ge(slot_in[p["slot"] % RING], slot_use(p["slot"]))
                    if p["w"] >= NBUF:
                        act.wait_ge(piece_done, p["w"] - NBUF + 1)
                    act.activation(piece_buf(p, 0), piece_src(p), ACT.Copy).then_inc(hi_done, 1)
                    split[0] += 1

            def result(pair):
                for p in pair:
                    hi_upto(p["w"] + LOOKAHEAD)
                act.wait_ge(piece_done, pair[1]["w"] + 1)

            def gemv_rows(s):
                g = gemv_of[s["n"]]
                act.wait_ge(gemv_mm, g + 1)
                act.activation(gsb[:, g % 2, :], gps(g), ACT.Copy).then_inc(gemv_sb, 1)

            def root(name):
                act.wait_ge(sum_done, STATS[name] + 1)
                act.activation(stat[:, 2:4], stps[:, 0:2], ACT.Sqrt, scale=1.0 / D, bias=EPS).then_inc(std_done, 1)

            def squares(name, src, written, job=None):
                for n in range(4):
                    if job:
                        hi_upto(jobs[job][2 * n + 1]["w"] + LOOKAHEAD)
                    act.wait_ge(*written(n))
                    if n == 0:
                        for w in SQ_FREE[name]:
                            act.wait_ge(*w)
                    two = slice(2 * n, 2 * n + 2)
                    act.activation(sq[:, two, :], src[:, two, :], ACT.Square).then_inc(sq_done, 1)

            def added(job):
                return lambda n: (lin_out["dve"], jobs[job][2 * n]["turn"])

            def operand_hi(name, shift, after):
                i = OPERANDS[name]
                if after is not None:
                    act.wait_ge(piece_done, after + 1)
                for c_ in range(DC):
                    act.wait_ge(scaled, 8 * i + c_ + 1)
                    bias = shift(c_) if shift else 0.0
                    act.activation(u[:, 0, c_, :], sq[:, c_, :], ACT.Identity, bias=bias).then_inc(u_hi, 1)

            act.dma_start(c_row, c[0].rearrange("(r p) -> r p", p=P)).then_inc(ld_c, 16)
            for i, (row, n, src) in enumerate(((0, 48, mod_b[0]), (48, 16, kv_mod_b), (64, 48, mod_b[1]))):
                act.dma_start(rows1[row:row + n, :], src.rearrange("(r p) -> r p", p=P)).then_inc(ld_vec, 16)
            act.wait_ge(c_t, 1)
            act.wait_ge(const_done, 3)
            act.activation(cact[:, :, 0:1], ps[:, 1, 384:384 + DC].rearrange("p (c o) -> p c o", o=1),
                           ACT.Silu).then_inc(act_order, 1)
            for name, src in (("norm_mix", norm_mix.rearrange("l (r p) -> (l r) p", p=P)),
                              ("norm_ffn", norm_ffn.rearrange("l (r p) -> (l r) p", p=P)),
                              ("a_lb", a_lb[0].rearrange("(r p) -> r p", p=P)),
                              ("kv_norm", kv_norm.rearrange("(r p) -> r p", p=P)),
                              ("final_norm", final_norm.rearrange("(r p) -> r p", p=P)),
                              ("norm_mix_2", norm_mix_2.rearrange("(r p) -> r p", p=P)),
                              ("norm_cross_2", norm_cross_2.rearrange("(r p) -> r p", p=P)),
                              ("norm_mem_2", norm_mem_2.rearrange("(r p) -> r p", p=P)),
                              ("norm_ffn_2", norm_ffn_2.rearrange("(r p) -> r p", p=P)),
                              ("a_out_norm", a_out_norm),
                              ("out_norm_attn_2", out_norm_attn_2.rearrange("(r p) -> r p", p=P)),
                              ("out_norm_sgu_2", out_norm_sgu_2.rearrange("(r p) -> r p", p=P)),
                              ("cq_norm_2", cq_norm_2.rearrange("(r p) -> r p", p=P)),
                              ("ck_norm_2", ck_norm_2.rearrange("(r p) -> r p", p=P))):
                r0 = VEC[name]
                act.dma_start(rows2[r0:r0 + src.shape[0], :], src).then_inc(ld_vec, 16)
            for name, src in (("q_norm_2", q_norm_2), ("k_norm_2", k_norm_2)):
                r0 = VEC[name]
                for twice in range(2):
                    act.dma_start(rows2[r0:r0 + 1, 64 * twice:64 * twice + 64],
                                  src.rearrange("(r p) -> r p", r=1)).then_inc(ld_vec, 16)
            for s in jobs["gemv_first"][:4]:
                gemv_rows(s)
            act.wait_ge(setup_c, 5)
            act.activation(lbs[:, 3, :], lbs[:, 0, :], ACT.Exp).then_inc(act_order, 1)
            squares("mix0", h, lambda n: (setup_c, 3 + n // 2))
            for s in jobs["gemv_first"][4:]:
                gemv_rows(s)
            root("mix0")
            hi_upto(LOOKAHEAD)
            operand_hi("mix0", lambda c_: mod[:, c_:c_ + 1], None)
            for n, pair in enumerate(pairs("zf")):
                result(pair)
                act.activation(kd[:, 2 * n:2 * n + 2, :], bank(pair), ACT.Sigmoid).then_inc(lin_out["act"], 1)
            for n, pair in enumerate(pairs("q")):
                result(pair)
                act.activation(qA[:, 2 * n:2 * n + 2, :], bank(pair), ACT.Silu).then_inc(lin_out["act"], 1)
            for r in range(8):
                pair = jobs[("v" if r < 4 else "g") + str(r)]
                n = r % 4
                gemv_rows(jobs[f"gemv_round{r}"][0])
                result(pair)
                if r < 4:
                    act.activation(vA[:, :, 256 * n:256 * (n + 1)], bank(pair), ACT.Copy).then_inc(lin_out["act"], 1)
                else:
                    act.activation(gA[:, 2 * n:2 * n + 2, :], bank(pair), ACT.Silu).then_inc(lin_out["act"], 1)
                gemv_rows(jobs[f"gemv_round{r}"][1])
            for b in range(2):
                act.wait_ge(a_mm, 4 * 8 + b + 1)
                act.activation(attA[:, 4 * b:4 * b + 4, 1, :],
                               ps[:, 2 + b, :].rearrange("p (h t) -> p h t", h=4), ACT.Copy).then_inc(a_x, 1)
            act.wait_ge(u_lo, 8)
            for n in range(4):
                act.wait_ge(a_o, 2 * n + 2)
                act.activation(sq[:, 2 * n:2 * n + 2, :], acc[:, 2 * n:2 * n + 2, :], ACT.Square).then_inc(a_sq, 1)
            for n in range(2):
                act.activation(qA[:, 4 * n:4 * n + 4, :], acc[:, 4 * n:4 * n + 4, :], ACT.Copy,
                               scale=vec("a_out_norm")).then_inc(a_og, 1)
            act.wait_ge(a_var, 1)
            act.activation(stat[:, 16:32], stat[:, 0:16], ACT.Sqrt).then_inc(a_std, 1)
            for b in range(2):
                act.wait_ge(a_g, b + 1)
                act.activation(u[:, 0, 4 * b:4 * b + 4, :], sq[:, 4 * b:4 * b + 4, :], ACT.Copy).then_inc(a_hi, 1)
            hi_upto(jobs["a_out"][0]["w"] + LOOKAHEAD)

            def ffn_act(layer, name, shift, before):
                squares(name, h, added(before), before)
                root(name)
                operand_hi(name, shift, LAST[before])
                for i in range(FFI):
                    fi = layer * FFI + i
                    pair = jobs[f"gate{layer}_{i}"]
                    result(pair)
                    if i >= 2:
                        wait_out(act, jobs[f"up{layer}_{i - 2}"][1])
                    act.activation(silu_g[:, i % 2, :, :], bank(pair), ACT.Silu).then_inc(lin_out["act"], 1)
                    for p in jobs[f"up{layer}_{i}"]:
                        hi_upto(p["w"] + LOOKAHEAD)
                    if i > 0:
                        for p in jobs[f"down{layer}_{i - 1}"]:
                            hi_upto(p["w"] + LOOKAHEAD - 1)
                    wait_out(act, jobs[f"up{layer}_{i}"][1])
                    if fi >= 2:
                        act.wait_ge(piece_done, jobs[f"down{(fi - 2) // FFI}_{(fi - 2) % FFI}"][1]["w"] + 1)
                    act.activation(hid[:, fi % 2, 0, :, :], hidden[:, i % 2, :, :], ACT.Copy).then_inc(f_hi, 1)
                    if layer == 0:
                        for s in jobs[f"gemv_ffn{i}"]:
                            gemv_rows(s)
                for p in jobs[f"down{layer}_{FFI - 1}"]:
                    hi_upto(p["w"] + LOOKAHEAD)
                if layer == 0:
                    for s in jobs[f"gemv_ffn{FFI}"]:
                        gemv_rows(s)

            ffn_act(0, "ffn0", lambda c_: mod[:, 24 + c_:25 + c_], "a_out")
            def attention_act(kind, hi_out):
                first, n = FIRST[kind], COUNT[kind]
                r0, r1, every = runs(kind)

                def exps(i):
                    a = first + i
                    act.wait_ge(at_b, before_b(a + 1))
                    if i >= 2:
                        act.wait_ge(at_t, a - 1)
                    for m, r in enumerate((r0, r1)):
                        src = sc_sb[:, i % 2, r] if kind == "W" else ps[:, 2 + i % 2, r]
                        act.activation(pr_sb[:, i % 2, r], src, ACT.Exp,
                                       scale=q_rstd[:, 2 * i + m:2 * i + m + 1] if kind == "X" else 1.0,
                                       bias=small[:, 0, 2 * a + m:2 * a + m + 1],
                                       accum_out=small[:, 1, 2 * a + m:2 * a + m + 1]).then_inc(at_e, 1)

                def copy(i):
                    a = first + i
                    act.wait_ge(at_t, a + 1)
                    if i >= 2:
                        act.wait_ge(at_o, a - 1)
                    w = 128 * len(blocks(kind))
                    act.activation(pt_sb[:, i % 2, 0:w], ps[:, 4 + i % 2, 0:w], ACT.Copy).then_inc(at_pt, 1)

                def drain(i):
                    if drains(kind, i) is not None:
                        act.wait_ge(at_o, first + i + 1)
                        k, bank_ = o_bank(kind, i)
                        hi_out(i, bank_).then_inc(at_hi, 1)

                for i in range(n + 2):
                    if i < n:
                        exps(i)
                    if 1 <= i <= n:
                        copy(i - 1)
                    if i >= 2:
                        drain(i - 2)

            def kv_act():
                squares("kv", h, lambda n: (acc_done, 2 * n + 2))
                root("kv")
                operand_hi("kv", lambda c_: mod[:, 48 + c_:49 + c_], LAST["up0_10"])
                for n, pair in enumerate(pairs("kv_k")):
                    result(pair)
                    act.activation(kB[:, 2 * n:2 * n + 2, :], bank(pair), ACT.Copy).then_inc(lin_out["act"], 1)
                for n, pair in enumerate(pairs("kv_v")):
                    result(pair)
                    act.activation(vB[:, :, 256 * n:256 * (n + 1)], bank(pair), ACT.Copy).then_inc(lin_out["act"], 1)

            kv_act()
            operand_hi("mix1", lambda c_: mod[:, 64 + c_:65 + c_], LAST["kv_v"])
            for n, pair in enumerate(pairs("b_q")):
                result(pair)
                act.activation(qB[:, 2 * n:2 * n + 2, :], bank(pair), ACT.Copy, scale=0.125).then_inc(lin_out["act"], 1)
            act.wait_ge(piece_done, LAST["b_q"] + 1)
            attention_act("B", lambda i, o: act.activation(
                u[:, 0, i // 2, :], o[:, 0:T], ACT.Copy))
            hi_upto(jobs["b_o"][0]["w"] + LOOKAHEAD)
            ffn_act(1, "ffn1", lambda c_: mod[:, 88 + c_:89 + c_], "b_o")

            for c_ in range(DC):
                act.wait_ge(acc_done, 9 + c_)
                act.activation(sq_final[:, c_, :], h[:, c_, :], ACT.Square, scale=vec("final_norm", c_))\
                    .then_inc(fin_sq, 1)
            squares("mix_2", h, lambda n: (acc_done, 8 + 2 * n + 2))
            root("mix_2")
            act.wait_ge(fin, 3)
            act.activation(stat[:, 14:16], stat[:, 12:14], ACT.Sqrt, scale=1.0 / D, bias=EPS).then_inc(fin, 1)
            operand_hi("mix_2", None, LAST["up1_10"])
            def in2_act():
                for n, pair in enumerate(pairs("in2")):
                    result(pair)
                    if n == 0:
                        act.wait_ge(u_lo, 48)
                    if n == 4:
                        act.wait_ge(w_ss, 1)
                        act.activation(stat[:, 16:32], stps[:, 0:16], ACT.Sqrt, bias=64 * EPS).then_inc(w_std, 1)
                        act.activation(k_std, acc[:, 0, :], ACT.Sqrt, scale=1.0 / 64, bias=EPS).then_inc(w_std, 1)
                    if n < 2:
                        act.activation(sq[:, 2 * n:2 * n + 2, :], bank(pair), ACT.Square).then_inc(w_sq, 1)
                        act.activation(qW[:, 2 * n:2 * n + 2, :], bank(pair), ACT.Copy,
                                       scale=vec("q_norm_2")).then_inc(lin_out["act"], 1)
                    elif n == 2:
                        act.activation(sq[:, 4, :], bank(pair)[:, 0, :], ACT.Square).then_inc(w_sq, 1)
                        act.activation(k_raw, bank(pair)[:, 0, :], ACT.Copy)
                        act.activation(vW, bank(pair)[:, 1, :].rearrange("p (b n) -> p b n", b=TB),
                                       ACT.Copy).then_inc(lin_out["act"], 1)
                    elif n < 5:
                        act.activation(uW[:, 2 * n - 6:2 * n - 4, :], bank(pair), ACT.Gelu_apprx_tanh)\
                            .then_inc(lin_out["act"], 1)
                    else:
                        m = n - 5
                        act.activation(gW[:, :, 256 * m:256 * (m + 1)], bank(pair), ACT.Gelu_apprx_tanh).then_inc(lin_out["act"], 1)

            in2_act()
            wait_out(act, jobs["in2"][-1])
            for b in range(TB):
                act.activation(gn[:, b, :], gW[:, b, :], ACT.Square, accum_out=gst[:, b:b + 1]).then_inc(w_sq, 1)
            act.wait_ge(w_sq, 5)
            act.activation(gst[:, 2:4], gst[:, 0:2], ACT.Sqrt, scale=1.0 / 512, bias=EPS).then_inc(w_std, 1)
            act.wait_ge(w_dup, 1)
            act.activation(kdup, acc[:, 0:2, :], ACT.Copy).then_inc(w_dc, 1)
            attention_act("W", lambda i, o: act.activation(mix[:, i // 2, :], o[:, 0:T], ACT.Copy))
            act.wait_ge(w_sg, 2)
            act.wait_ge(at_hi, 12)
            act.wait_ge(w_ss, 1)
            act.activation(sq[:], mix, ACT.Square).then_inc(w_sq, 1)
            act.wait_ge(w_ss, 2)
            act.activation(half_std, ps[:, 6, :].rearrange("p (c t) -> p c t", c=2), ACT.Sqrt, scale=1.0 / 512,
                           bias=EPS).then_inc(w_std, 1)
            operand_hi("mixed", None, LAST["in2"])
            for n in range(4):
                hi_upto(jobs["out2"][2 * n + 1]["w"] + LOOKAHEAD)

            act.wait_ge(x_tc, 1)
            squares("mem", memT, lambda n: (x_tc, 1 + n // 2))
            root("mem")
            operand_hi("mem", None, LAST["out2"])
            for n, pair in enumerate(pairs("ck")):
                result(pair)
                act.activation(raw[:, 2 * n:2 * n + 2, :], bank(pair), ACT.Square).then_inc(x_sq, 1)
                act.activation(kX[:, 2 * n:2 * n + 2, :], bank(pair), ACT.Copy).then_inc(lin_out["act"], 1)
            for n, pair in enumerate(pairs("cv")):
                result(pair)
                act.activation(vX[:, :, 256 * n:256 * (n + 1)], bank(pair), ACT.Copy).then_inc(lin_out["act"], 1)
                if n == 0:
                    act.wait_ge(x_ss, 1)
                    act.activation(x_rstd, acc[:, 0:4, :], ACT.Sqrt, scale=1.0 / 256, bias=EPS).then_inc(x_std, 1)
            squares("cross", h, added("out2"))
            root("cross")
            operand_hi("cross", None, LAST["cv"])
            for n, pair in enumerate(pairs("cq")):
                result(pair)
                if n == 0:
                    act.wait_ge(u_lo, 72)
                act.activation(sq[:, 2 * n:2 * n + 2, :], bank(pair), ACT.Square).then_inc(x_sq, 1)
                for m in range(2):
                    ins = act.activation(qX[:, 2 * n + m, :], bank(pair)[:, m, :], ACT.Copy,
                                         scale=vec("cq_norm_2", m))
                ins.then_inc(lin_out["act"], 1)
            act.wait_ge(x_ss, 2)
            act.activation(stat[:, 16:24], stps[:, 0:8], ACT.Sqrt, bias=256 * EPS).then_inc(x_std, 1)
            act.wait_ge(piece_done, LAST["cq"] + 1)
            act.wait_ge(x_rs, 5)
            act.wait_ge(x_n, 2)
            attention_act("X", lambda i, o: act.activation(
                u[:, 0, 2 * i:2 * i + 2, :], o.rearrange("p (c t) -> p c t", c=2), ACT.Copy))
            squares("moe", h, added("co"), "co")
            root("moe")
            act.wait_ge(route, 2)
            for b in range(TB):
                act.activation(og_t[:, b, :], logits[:, b, 0:NGROUP], ACT.Exp, bias=rs[:, 0, b:b + 1],
                               accum_out=rs[:, 1, b:b + 1]).then_inc(route_e, 1)
            act.wait_ge(route, 20)
            act.activation(rs[:, 8, :], rs[:, 7, :], ACT.Exp).then_inc(route_e, 1)

            def expert_act(n):
                act.wait_ge(m_h, n + 1)
                act.activation(silu_e, ps[:, 0, 0:256], ACT.Silu).then_inc(m_si, 1)
                act.wait_ge(m_t, n + 1)
                act.activation(tt, ps[:, 1, :], ACT.Copy).then_inc(m_tc, 1)
                act.wait_ge(m_y, n + 1)
                act.activation(y_sb, ps[:, 6, :], ACT.Copy).then_inc(m_yc, 1)

            with act.Fori(0, NE // 2) as i:
                for b in range(2):
                    expert_act(2 * i + b)
            act.wait_ge(m_flag, 1)
            more = act.value_load(flag[0:1, 1:2].bitcast(I32), min_val=0, max_val=1)
            with act.If(more > 0):
                with act.Fori(0, NE) as e:
                    for p_ in range(3):
                        expert_act(3 * e + NE + p_)
                act.wait_ge(m_all, 1 + 3 * NE)
            act.wait_ge(m_all, 1)
            act.activation(hn_tok[:, 0, 0:512], ps[:, 2, :], ACT.Copy).then_inc(m_out, 1)
            act.wait_ge(m_out, 2)
            act.activation(hn_tok[:, 1, 0:512], ps[:, 4, :], ACT.Copy).then_inc(m_out, 1)

        @block.vector
        def _(dve):
            split = [0]

            def lo_upto(w):
                while split[0] <= min(w, len(pieces) - 1):
                    p = pieces[split[0]]
                    dve.wait_ge(hi_done, p["w"] + 1)
                    dve.tensor_tensor(piece_buf(p, 1), piece_src(p), piece_buf(p, 0).bitcast(F32),
                                      ALU.subtract).then_inc(lo_done, 1)
                    split[0] += 1

            def result(pair):
                for p in pair:
                    lo_upto(p["w"] + LOOKAHEAD)
                dve.wait_ge(piece_done, pair[1]["w"] + 1)

            def second_root():
                r1, r1_sq, mean, r2 = (stat[:, n:n + 2] for n in (8, 10, 12, 14))
                dve.reciprocal(r1, stat[:, 2:4]).then_inc(fin, 1)
                dve.wait_ge(fin, 1)
                dve.tensor_tensor(r1_sq, r1, r1, ALU.mult).then_inc(fin, 1)
                dve.wait_ge(fin, 2)
                dve.tensor_tensor(mean, stps[:, 2:4], r1_sq, ALU.mult).then_inc(fin, 1)
                dve.wait_ge(fin, 4)
                dve.reciprocal(r2, r2).then_inc(fin, 1)
                dve.wait_ge(fin, 5)
                dve.tensor_tensor(stat[:, 4:6], r1, r2, ALU.mult).then_inc(rstd_done, 1)

            def norm_rstd(name):
                i = STATS[name]
                dve.wait_ge(std_done, i + 1)
                if name == "mix_2":
                    second_root()
                else:
                    dve.reciprocal(stat[:, 4:6], stat[:, 2:4]).then_inc(rstd_done, 1)
                dve.wait_ge(rstd_done, i + 1)
                if i > 0:
                    dve.wait_ge(bc_done, i)
                for b in range(TB):
                    dve.tensor_scalar(diag[:, b, :], ident[:], stat[:, 4 + b:5 + b], None, ALU.mult)\
                       .then_inc(diag_done, 1)
                dve.wait_ge(bc_done, i + 1)

            def operand(name, src, gains, shift, by=lambda c_: rbc):
                i = OPERANDS[name]
                if i > 0:
                    dve.wait_ge(u_lo, 8 * i)
                for c_ in range(DC + 2):
                    if c_ < DC:
                        dve.scalar_tensor_tensor(out=sq[:, c_, :], in0=src[:, c_, :], scalar=gains(c_), in1=by(c_),
                                                 op0=ALU.mult, op1=ALU.mult).then_inc(scaled, 1)
                    c_ -= 2
                    if c_ < 0:
                        continue
                    dve.wait_ge(u_hi, 8 * i + c_ + 1)
                    s_ = shift(c_) if shift else 0.0
                    dve.scalar_tensor_tensor(out=u[:, 1, c_, :], in0=sq[:, c_, :], scalar=s_,
                                             in1=u[:, 0, c_, :].bitcast(F32), op0=ALU.add, op1=ALU.subtract)\
                       .then_inc(u_lo, 1)

            def add_gated(job, gate):
                for n, pair in enumerate(pairs(job)):
                    result(pair)
                    for m in range(2):
                        c_ = 2 * n + m
                        ins = dve.scalar_tensor_tensor(out=h[:, c_, :], in0=bank(pair)[:, m, :],
                                                       scalar=gate(c_) if gate else 1.0, in1=h[:, c_, :],
                                                       op0=ALU.mult, op1=ALU.add)
                    ins.then_inc(lin_out["dve"], 1)

            dve.wait_ge(setup_t, 1)
            dve.tensor_copy(vec1[:], ps[:, 0, 0:112]).then_inc(setup_c, 1)
            dve.wait_ge(setup_t, 2)
            dve.tensor_copy(vec2[:], ps[:, 1, 0:ROWS2]).then_inc(setup_c, 1)
            for b in range(2):
                dve.wait_ge(setup_t, 3 + b)
                dve.tensor_copy(h[:, 4 * b:4 * b + 4, :], acc[:, 4 * b:4 * b + 4, :]).then_inc(setup_c, 1)
            lb_col = vec2[:, VEC["a_lb"]:VEC["a_lb"] + HA]
            dve.wait_ge(setup_c, 4)
            dve.tensor_tensor(lbs[:, 0, :], lb_col, lb_col, ALU.subtract).then_inc(setup_c, 1)
            dve.wait_ge(act_order, 2)
            dve.reciprocal(lbs[:, 1, :], lbs[:, 3, :]).then_inc(setup_c, 1)
            dve.wait_ge(setup_c, 6)
            dve.tensor_tensor(lbs[:, 2, :], lbs[:, 3, :], lbs[:, 1, :], ALU.mult).then_inc(setup_c, 1)
            dve.wait_ge(setup_c, 7)
            dve.tensor_tensor(lbs[:, 0, :], lbs[:, 2, :], lbs[:, 2, :], ALU.subtract).then_inc(setup_c, 1)
            dve.wait_ge(setup_c, 8)
            dve.tensor_scalar(lbs[:, 1, :], lbs[:, 0, :], -1.0, 1.0, ALU.mult, ALU.add).then_inc(setup_c, 1)
            dve.tensor_scalar(lbs[:, 2, :], lbs[:, 0, :], 1.0, -1.0, ALU.mult, ALU.add).then_inc(setup_c, 1)
            dve.wait_ge(const_done, 6)
            si, ti, xi = (xor_i[:, n, :] for n in range(3))
            dve.tensor_tensor(xi.bitcast(I32), si.bitcast(I32), ti.bitcast(I32), ALU.bitwise_xor).then_inc(setup_c, 1)
            dve.tensor_tensor(si, ti.bitcast(I32), si.bitcast(I32), ALU.is_lt).then_inc(setup_c, 1)
            dve.wait_ge(setup_c, 12)
            dve.tensor_copy(ti, xi.bitcast(I32)).then_inc(setup_c, 1)
            dve.wait_ge(setup_c, 13)
            dve.scalar_tensor_tensor(out=xi, in0=si, scalar=1000.0, in1=ti, op0=ALU.mult, op1=ALU.add).then_inc(setup_c, 1)
            dve.wait_ge(setup_c, 14)
            dve.tensor_scalar(masks[:, 0, :], xi, 0.0, None, ALU.is_equal).then_inc(setup_c, 1)
            for n, H in enumerate(LEVELS):
                dve.wait_ge(setup_c, 15 + 2 * n)
                dve.tensor_scalar(ti, xi, float(H), None, ALU.is_ge).then_inc(setup_c, 1)
                dve.wait_ge(setup_c, 16 + 2 * n)
                dve.scalar_tensor_tensor(out=masks[:, n + 1, :], in0=xi, scalar=float(2 * H), in1=ti,
                                         op0=ALU.is_lt, op1=ALU.mult).then_inc(setup_c, 1)
            dve.wait_ge(gemv_col, 1)
            dve.tensor_tensor(mod[:, 0:16], modps[:, 0:16], vec1[:, 0:16], ALU.add).then_inc(mod_done, 1)
            dve.wait_ge(mod_done, 1)
            dve.scalar_tensor_tensor(out=gain[:, 0, :], in0=mod[:, 8:16], scalar=1.0,
                                     in1=vec2[:, VEC["norm_mix"]:VEC["norm_mix"] + DC],
                                     op0=ALU.add, op1=ALU.mult).then_inc(mod_done, 1)
            dve.wait_ge(mod_done, 2)
            norm_rstd("mix0")
            lo_upto(LOOKAHEAD)
            operand("mix0", h, lambda c_: gain[:, 0, c_:c_ + 1], lambda c_: mod[:, c_:c_ + 1])
            for n, p in enumerate(jobs["zf"]):
                lo_upto(p["w"] + LOOKAHEAD)
                wait_out(dve, p)
                dve.tensor_scalar(FP[:, n, :], kd[:, n, :], lbs[:, 1, n:n + 1], lbs[:, 0, n:n + 1],
                                  ALU.mult, ALU.add).then_inc(a_prep, 1)
                dve.tensor_scalar(kA[:, n, :], kd[:, n, :], lbs[:, 2, n:n + 1], lbs[:, 1, n:n + 1],
                                  ALU.mult, ALU.add).then_inc(a_prep, 1)
            dve.wait_ge(a_prep, 16)
            dve.tensor_scalar(FP, FP, MIN_FORGET, None, ALU.max).then_inc(a_prep, 1)
            for p in jobs["q"]:
                lo_upto(p["w"] + LOOKAHEAD)
            wait_out(dve, jobs["q"][-1])
            dve.wait_ge(a_prep, 17)
            dve.wait_ge(a_init, 3)

            def decayed(n):
                H = (LEVELS + [128])[n]
                if n > 0:
                    dve.wait_ge(a_mm, 4 * (n + 1))
                    dve.wait_ge(a_fg, 2 * n)
                dve.tensor_tensor(halves(qd, H, True), halves(qA, H, True), halves(FP, H, True), ALU.mult)\
                   .then_inc(a_dec, 1)
                dve.tensor_tensor(halves(kd, H, False), halves(kA, H, False), halves(GS, H, False), ALU.mult)\
                   .then_inc(a_dec, 1)

            def products(n):
                H = LEVELS[n]
                last = lambda upper: halves(FP, H, upper)[:, :, H - 1:H].to_broadcast([P, HA * T // (2 * H), H])
                dve.wait_ge(a_dec, 2 * n + 2)
                dve.tensor_tensor(halves(GS, H, False), halves(GS, H, False), last(True), ALU.mult)\
                   .then_inc(a_fg, 1)
                dve.wait_ge(a_fg, 2 * n + 1)
                dve.tensor_tensor(halves(FP, H, True), halves(FP, H, True), last(False), ALU.mult)\
                   .then_inc(a_fg, 1)

            def select(r):
                m = masks[:, r, :].rearrange("p (o t) -> p o t", o=1).to_broadcast([P, 4, P])
                for b in range(4):
                    dve.wait_ge(a_mm, 4 * r + b + 1)
                    dve.copy_predicated(out=attA[:, 2 * b:2 * b + 2, 0:3:2, :],
                                        mask=m.rearrange("p (h b) t -> p h b t", h=2),
                                        data=ps[:, 2 + b, :].rearrange("p (h b t) -> p h b t", h=2, b=2))\
                       .then_inc(a_cp, 1)

            decayed(0)
            products(0)
            for r in range(8):
                for p in jobs[("v" if r < 4 else "g") + str(r)]:
                    lo_upto(p["w"] + LOOKAHEAD)
                select(r)
                if r < 7:
                    decayed(r + 1)
                    if r + 1 < 7:
                        products(r + 1)
            dve.wait_ge(a_ss, 1)
            dve.tensor_scalar(stat[:, 0:16], stps[:, 0:16], 1.0 / P, EPS, ALU.mult, ALU.add).then_inc(a_var, 1)
            dve.wait_ge(a_std, 1)
            dve.reciprocal(stat[:, 32:48], stat[:, 16:32]).then_inc(a_rs, 1)
            dve.wait_ge(a_rs, 1)
            for n in range(16):
                if n >= 4:
                    dve.wait_ge(a_bc, n - 3)
                else:
                    dve.wait_ge(bc_done, 1)
                dve.tensor_scalar(diag[:, n % 4, :], ident[:], stat[:, 32 + n:33 + n], None, ALU.mult)\
                   .then_inc(a_diag, 1)
                if n % 8 == 7:
                    b = n // 8
                    four = slice(4 * b, 4 * b + 4)
                    dve.wait_ge(a_og, b + 1)
                    wait_out(dve, jobs["g7"][-1])
                    dve.tensor_tensor(qA[:, four, :], qA[:, four, :], gA[:, four, :], ALU.mult).then_inc(a_t, 1)
                    dve.wait_ge(a_t, b + 1)
                    dve.wait_ge(a_bc, n + 1)
                    dve.tensor_tensor(sq[:, four, :], qA[:, four, :],
                                      ps[:, 0:2, :].rearrange("p b (c t) -> p (b c) t", t=T), ALU.mult)\
                       .then_inc(a_g, 1)
            for b in range(2):
                dve.wait_ge(a_hi, b + 1)
                dve.tensor_tensor(u[:, 1, 4 * b:4 * b + 4, :], sq[:, 4 * b:4 * b + 4, :],
                                  u[:, 0, 4 * b:4 * b + 4, :].bitcast(F32), ALU.subtract).then_inc(a_lo, 1)
            dve.wait_ge(gemv_col, 2)
            dve.tensor_tensor(mod[:, 16:48], modps[:, 16:48], vec1[:, 16:48], ALU.add).then_inc(mod_done, 1)
            dve.wait_ge(mod_done, 3)
            dve.scalar_tensor_tensor(out=gain[:, 1, :], in0=mod[:, 32:40], scalar=1.0,
                                     in1=vec2[:, VEC["norm_ffn"]:VEC["norm_ffn"] + DC],
                                     op0=ALU.add, op1=ALU.mult).then_inc(mod_done, 1)
            add_gated("a_out", lambda c_: mod[:, 16 + c_:17 + c_])

            def ffn_dve(layer, name, gains, shift, gate):
                norm_rstd(name)
                lo_upto(jobs[f"gate{layer}_0"][0]["w"] + LOOKAHEAD - 1)
                operand(name, h, gains, shift)
                for i in range(FFI):
                    fi = layer * FFI + i
                    for p in jobs[f"gate{layer}_{i}"]:
                        lo_upto(p["w"] + LOOKAHEAD)
                    pair = jobs[f"up{layer}_{i}"]
                    result(pair)
                    wait_out(dve, jobs[f"gate{layer}_{i}"][0])
                    if fi >= 2:
                        dve.wait_ge(f_lo, fi - 1)
                    dve.tensor_tensor(hidden[:, i % 2, :, :], silu_g[:, i % 2, :, :], bank(pair),
                                      ALU.mult).then_inc(lin_out["dve"], 1)
                    if i > 0:
                        for p in jobs[f"down{layer}_{i - 1}"]:
                            lo_upto(p["w"] + LOOKAHEAD - 1)
                    dve.wait_ge(f_hi, fi + 1)
                    dve.tensor_tensor(hid[:, fi % 2, 1, :, :], hidden[:, i % 2, :, :],
                                      hid[:, fi % 2, 0, :, :].bitcast(F32), ALU.subtract).then_inc(f_lo, 1)
                lo_upto(LAST[f"down{layer}_{FFI - 1}"] + LOOKAHEAD - 1)
                for c_ in range(DC):
                    dve.wait_ge(piece_done, jobs[f"down{layer}_{FFI - 1}"][c_ // 4]["w"] + 1)
                    dve.scalar_tensor_tensor(out=h[:, c_, :], in0=acc[:, c_, :], scalar=gate(c_), in1=h[:, c_, :],
                                             op0=ALU.mult, op1=ALU.add).then_inc(acc_done, 1)

            dve.wait_ge(mod_done, 4)
            ffn_dve(0, "ffn0", lambda c_: gain[:, 1, c_:c_ + 1], lambda c_: mod[:, 24 + c_:25 + c_],
                    lambda c_: mod[:, 40 + c_:41 + c_])
            def attention_dve(kind, lo_out):
                first, n = FIRST[kind], COUNT[kind]
                r0, r1, every = runs(kind)

                def scores(i):
                    a, at = first + i, before_b(first + i)
                    if i >= 2:
                        dve.wait_ge(at_e, 2 * (a - 1))
                    src, maxima = ps[:, 2 + i % 2, :], small[:, 0, 2 * a:2 * a + 2]
                    if kind == "W":
                        dve.tensor_copy(sc_sb[:, i % 2, 0:386:385],
                                        sinks[:, i:i + 1].to_broadcast([P, 2])).then_inc(at_b, 1)
                    dve.wait_ge(at_s, a + 1)
                    if kind == "W":
                        for m, (c0, c1) in enumerate(((0, P), (P, 3 * P))):
                            dve.scalar_tensor_tensor(out=sc_sb[:, i % 2, 1 + c0:1 + c1], in0=src[:, c0:c1],
                                                     scalar=q_rstd[:, 2 * i + m:2 * i + m + 1],
                                                     in1=winmask[:, c0 // P:c1 // P, :].rearrange("p b k -> p (b k)"),
                                                     op0=ALU.mult, op1=ALU.add).then_inc(at_b, 1)
                        dve.wait_ge(at_b, at + 3)
                        src = sc_sb[:, i % 2, :]
                    for m, r in enumerate((r0, r1)):
                        dve.tensor_reduce(out=maxima[:, m:m + 1], in_=src[:, r], axis=AX, op=ALU.max,
                                          negate=True).then_inc(at_b, 1)
                    if kind == "X":
                        dve.wait_ge(at_b, at + 2)
                        dve.tensor_tensor(maxima, maxima, q_rstd[:, 2 * i:2 * i + 2], ALU.mult).then_inc(at_b, 1)

                def probs(i):
                    a = first + i
                    dve.wait_ge(at_e, 2 * a + 2)
                    dve.reciprocal(small[:, 2, 2 * a:2 * a + 2], small[:, 1, 2 * a:2 * a + 2]).then_inc(at_p, 1)
                    dve.wait_ge(at_p, 3 * a + 1)
                    for m, r in enumerate((r0, r1)):
                        dve.tensor_scalar(pr_sb[:, i % 2, r], pr_sb[:, i % 2, r],
                                          small[:, 2, 2 * a + m:2 * a + m + 1], None, ALU.mult).then_inc(at_p, 1)

                def drain(i):
                    if lo_out and drains(kind, i) is not None:
                        k, bank_ = o_bank(kind, i)
                        dve.wait_ge(at_hi, k + 1)
                        lo_out(i, bank_).then_inc(at_lo, 1)

                scores(0)
                for i in range(n + 3):
                    if i + 1 < n:
                        scores(i + 1)
                    if i < n:
                        probs(i)
                    if i >= 3:
                        drain(i - 3)

            def new_gains():
                dve.wait_ge(gemv_col, 3)
                dve.tensor_tensor(mod[:, 48:112], modps[:, 48:112], vec1[:, 48:112], ALU.add).then_inc(mod_done, 1)
                dve.wait_ge(mod_done, 5)
                for g, at, gain_of in ((2, 56, vec2[:, VEC["kv_norm"]:VEC["kv_norm"] + DC]),
                                       (3, 72, vec2[:, VEC["norm_mix"] + DC:VEC["norm_mix"] + 2 * DC]),
                                       (4, 96, vec2[:, VEC["norm_ffn"] + DC:VEC["norm_ffn"] + 2 * DC])):
                    dve.scalar_tensor_tensor(out=gain[:, g, :], in0=mod[:, at:at + DC], scalar=1.0, in1=gain_of,
                                             op0=ALU.add, op1=ALU.mult).then_inc(mod_done, 1)
                dve.tensor_tensor(gain[:, 0, :], vec2[:, VEC["final_norm"]:VEC["final_norm"] + DC],
                                  vec2[:, VEC["norm_mix_2"]:VEC["norm_mix_2"] + DC], ALU.mult).then_inc(mod_done, 1)
                dve.wait_ge(mod_done, 9)

            new_gains()
            norm_rstd("kv")
            lo_upto(jobs["kv_k"][0]["w"] + LOOKAHEAD - 1)
            operand("kv", h, lambda c_: gain[:, 2, c_:c_ + 1], lambda c_: mod[:, 48 + c_:49 + c_])
            lo_upto(LAST["kv_k"])
            dve.wait_ge(b_relt, 1)
            dve.wait_ge(b_zero, 3)
            dve.tensor_copy(relT[0:HB, 0:NREL], ps[0:HB, 2, 0:NREL]).then_inc(b_relt, 1)
            lo_upto(LAST["kv_v"] + LOOKAHEAD)
            operand("mix1", h, lambda c_: gain[:, 3, c_:c_ + 1], lambda c_: mod[:, 64 + c_:65 + c_])
            lo_upto(LAST["b_q"] + LOOKAHEAD)
            attention_dve("B", lambda i, o: dve.tensor_tensor(
                u[:, 1, i // 2, :], o[:, 0:T], u[:, 0, i // 2, :].bitcast(F32), ALU.subtract))
            add_gated("b_o", lambda c_: mod[:, 80 + c_:81 + c_])
            ffn_dve(1, "ffn1", lambda c_: gain[:, 4, c_:c_ + 1], lambda c_: mod[:, 88 + c_:89 + c_],
                    lambda c_: mod[:, 104 + c_:105 + c_])

            norm_rstd("mix_2")
            lo_upto(jobs["in2"][0]["w"] + LOOKAHEAD - 1)
            operand("mix_2", h, lambda c_: gain[:, 0, c_:c_ + 1], None)
            for b in range(TB):
                dve.tensor_scalar(diag[:, 2 + b, :], ident[:], stat[:, 8 + b:9 + b], None, ALU.mult).then_inc(fin, 1)
            dve.wait_ge(fin, 8)
            for c_ in range(DC):
                dve.scalar_tensor_tensor(out=h[:, c_, :], in0=h[:, c_, :], scalar=vec("final_norm", c_),
                                         in1=ps[:, 4, 0:T], op0=ALU.mult, op1=ALU.mult).then_inc(res_done, 1)
            lo_upto(jobs["in2"][7]["w"])
            for b in range(2):
                dve.wait_ge(w_tp, b + 1)
                dve.tensor_copy(wT[:, 4 * b:4 * b + 4, :], ps[:, 2 + b, :].rearrange("p (g i) -> p g i", g=4))\
                    .then_inc(w_tc, 1)
            lo_upto(jobs["in2"][9]["w"] + LOOKAHEAD)
            dve.wait_ge(w_std, 1)
            dve.reciprocal(q_rstd, stat[:, 16:32]).then_inc(w_n, 1)
            dve.wait_ge(w_std, 2)
            dve.reciprocal(k_std, k_std).then_inc(w_rs, 1)
            wait_out(dve, jobs["in2"][5])
            dve.wait_ge(w_rs, 1)
            dve.scalar_tensor_tensor(out=kW, in0=k_raw, scalar=vec("k_norm_2"), in1=k_std,
                                     op0=ALU.mult, op1=ALU.mult).then_inc(w_n, 1)
            lo_upto(LAST["in2"] + LOOKAHEAD)
            wait_out(dve, jobs["in2"][-1])
            dve.wait_ge(w_std, 3)
            dve.reciprocal(gst[:, 4:6], gst[:, 2:4]).then_inc(w_rs, 1)
            dve.wait_ge(w_rs, 2)
            dve.wait_ge(w_ld, 64)
            for b in range(TB):
                dve.scalar_tensor_tensor(out=gn[:, b, :], in0=gW[:, b, :], scalar=gst[:, 4 + b:5 + b], in1=gain_bc,
                                         op0=ALU.mult, op1=ALU.mult).then_inc(w_n, 1)
            for b in range(2):
                dve.wait_ge(w_s, b + 1)
                dve.tensor_tensor(mix[:, 4 + 2 * b:6 + 2 * b, :], acc[:, 4 + 2 * b:6 + 2 * b, :],
                                  uW[:, 2 * b:2 * b + 2, :], ALU.mult).then_inc(w_sg, 1)
            dve.wait_ge(w_ms, 8)
            dve.wait_ge(w_n, 2)
            attention_dve("W", None)
            dve.wait_ge(w_std, 4)
            dve.reciprocal(half_std, half_std).then_inc(w_rs, 1)
            dve.wait_ge(w_rs, 3)
            dve.wait_ge(at_hi, 12)
            operand("mixed", mix, lambda c_: vec("out_norm_attn_2", c_) if c_ < 4 else vec("out_norm_sgu_2", c_ - 4),
                    None, lambda c_: half_std[:, c_ // 4, :])
            add_gated("out2", None)

            for b in range(2):
                dve.wait_ge(x_tp, b + 1)
                dve.tensor_copy(memT[:, 4 * b:4 * b + 4, :], acc[:, 4 * b:4 * b + 4, :]).then_inc(x_tc, 1)
            norm_rstd("mem")
            lo_upto(jobs["ck"][0]["w"] + LOOKAHEAD - 1)
            dve.wait_ge(x_tc, 2)
            operand("mem", memT, lambda c_: vec("norm_mem_2", c_), None)
            lo_upto(jobs["cv"][1]["w"] + LOOKAHEAD)
            dve.wait_ge(x_std, 1)
            for hh in range(HX):
                dve.reciprocal(x_rstd[:, hh, :], x_rstd[:, hh, :]).then_inc(x_rs, 1)
                lo_upto(jobs["cv"][2 * hh + 1]["w"] + LOOKAHEAD)
            dve.wait_ge(x_rs, 4)
            wait_out(dve, jobs["ck"][-1])
            for m in range(2):
                dve.scalar_tensor_tensor(out=kX[:, m::2, :], in0=kX[:, m::2, :], scalar=vec("ck_norm_2", m),
                                         in1=x_rstd, op0=ALU.mult, op1=ALU.mult).then_inc(x_n, 1)
            norm_rstd("cross")
            operand("cross", h, lambda c_: vec("norm_cross_2", c_), None)
            lo_upto(LAST["cq"] + LOOKAHEAD)
            dve.wait_ge(x_std, 2)
            dve.reciprocal(q_rstd[:, 0:8], stat[:, 16:24]).then_inc(x_rs, 1)
            dve.wait_ge(x_rs, 5)
            attention_dve("X", lambda i, o: dve.tensor_tensor(
                u[:, 1, 2 * i:2 * i + 2, :], o.rearrange("p (c t) -> p c t", c=2),
                u[:, 0, 2 * i:2 * i + 2, :].bitcast(F32), ALU.subtract))
            add_gated("co", None)
            norm_rstd("moe")
            for c_ in range(DC):
                dve.scalar_tensor_tensor(out=sq[:, c_, :], in0=h[:, c_, :], scalar=vec("norm_ffn_2", c_), in1=rbc,
                                         op0=ALU.mult, op1=ALU.mult).then_inc(m_hn, 1)
            steps = [0]

            def step(ins):
                ins.then_inc(route, 1)
                steps[0] += 1
                dve.wait_ge(route, steps[0])

            def first_max(values, width, one_hot, t_, at):
                wide = lambda a: a.rearrange("p (b o) -> p b o", o=1).to_broadcast([P, TB, width])
                numbers = slot_no[:, 0:1, 0:width].to_broadcast([P, TB, width])
                step(dve.tensor_reduce(out=rs[:, at, :], in_=values, axis=AX, op=ALU.max))
                step(dve.tensor_tensor(t_, values, wide(rs[:, at, :]), ALU.is_equal))
                step(dve.scalar_tensor_tensor(out=t_, in0=numbers, scalar=-100.0, in1=t_, op0=ALU.add, op1=ALU.mult))
                step(dve.tensor_reduce(out=rs[:, at + 1, :], in_=t_, axis=AX, op=ALU.min))
                step(dve.tensor_scalar(rs[:, at + 1, :], rs[:, at + 1, :], 100.0, None, ALU.add))
                step(dve.tensor_tensor(one_hot, numbers, wide(rs[:, at + 1, :]), ALU.is_equal))

            dve.wait_ge(m_const, 3)
            dve.wait_ge(m_tok, 2)
            dve.tensor_copy(hn_tok, ps[:, 2:6, :].rearrange("p (b j) n -> p b (j n)", b=TB)).then_inc(m_tokc, 1)
            dve.wait_ge(m_log, 1)
            step(dve.tensor_copy(logits, ps[:, 6, 0:72].rearrange("p (b e) -> p b e", b=TB)))
            step(dve.tensor_reduce(out=rs[:, 0, :], in_=logits[:, :, 0:NGROUP], axis=AX, op=ALU.max, negate=True))
            step(dve.tensor_copy(slot_no.rearrange("p a b -> p (a b)"), slot_i.bitcast(I32)))
            dve.wait_ge(route_e, 2)
            first_max(logits[:, :, 0:NGROUP], NGROUP, og, og_t, 2)
            step(dve.tensor_tensor(prod.rearrange("p b (g e) -> p b g e", g=NGROUP),
                                   logits[:, :, NGROUP:].rearrange("p b (g e) -> p b g e", g=NGROUP),
                                   og.rearrange("p b (g o) -> p b g o", o=1).to_broadcast([P, TB, NGROUP, PER]),
                                   ALU.mult))
            step(dve.tensor_reduce(out=loc, in_=prod.rearrange("p b (g e) -> p b e g", g=NGROUP), axis=AX,
                                   op=ALU.add))
            first_max(loc, PER, o1, eq8, 4)
            step(dve.scalar_tensor_tensor(out=loc2, in0=o1, scalar=-3e38, in1=loc, op0=ALU.mult, op1=ALU.add))
            assert steps[0] == 18
            step(dve.tensor_reduce(out=rs[:, 6, :], in_=loc2, axis=AX, op=ALU.max))
            step(dve.tensor_tensor(rs[:, 7, :], rs[:, 6, :], rs[:, 4, :], ALU.subtract))
            first_max(loc2, PER, o2, eq8, 9)
            dve.wait_ge(route_e, 3)
            step(dve.tensor_scalar(rs[:, 11, :], rs[:, 8, :], 1.0, None, ALU.add))
            step(dve.tensor_tensor(rs[:, 11, :], rs[:, 11, :], rs[:, 1, :], ALU.mult))
            step(dve.reciprocal(rs[:, 12, :], rs[:, 11, :]))
            step(dve.tensor_tensor(rs[:, 13, :], rs[:, 12, :], rs[:, 8, :], ALU.mult))
            four = lambda a: a.rearrange("p b (g e) -> p b g e", g=NGROUP)
            for o_, m_ in ((o1, M1), (o2, M2)):
                for b in range(TB):
                    step(dve.tensor_tensor(
                        m_[:, b, :].rearrange("p (g e) -> p g e", g=NGROUP),
                        o_[:, b:b + 1, :].to_broadcast([P, NGROUP, PER]),
                        og[:, b, :].rearrange("p (g o) -> p g o", o=1).to_broadcast([P, NGROUP, PER]), ALU.mult))
            for b in range(TB):
                step(dve.tensor_scalar(G[:, b, :], M2[:, b, :], rs[:, 13, b:b + 1], None, ALU.mult))
                step(dve.scalar_tensor_tensor(out=G[:, b, :], in0=M1[:, b, :], scalar=rs[:, 12, b:b + 1],
                                              in1=G[:, b, :], op0=ALU.mult, op1=ALU.add))
            step(dve.tensor_tensor(M1, M1, M2, ALU.add))
            assert steps[0] == ROUTED
            dve.wait_ge(m_rank, 1)
            step(dve.scalar_tensor_tensor(out=R, in0=ps[:, 6, 128:192].rearrange("p (b e) -> p b e", b=TB),
                                          scalar=1.0, in1=M1, op0=ALU.add, op1=ALU.mult))
            step(dve.tensor_scalar(R, R, -1.0, None, ALU.add))
            step(dve.tensor_reduce(out=rs[:, 14, 0:1], in_=ps[:, 6, 192:224], axis=AX, op=ALU.max))
            step(dve.tensor_scalar(flag[:, 0:1], rs[:, 14, 0:1], float(CAP), None, ALU.is_gt))
            dve.tensor_copy(flag[:, 1:2].bitcast(I32), flag[:, 0:1]).then_inc(m_flag, 1)

            def select_e(e, k, pass_=0):
                for b in range(TB):
                    r_ = R[:, b, bass.ds(e, 1)]
                    dve.tensor_scalar(sel[:, k, b, :], slot_no[:, pass_, 0:CAP], r_, None, ALU.is_equal)\
                        .then_inc(m_s, 1)
                    dve.tensor_scalar(gate_sel[:, k, b, :], slot_no[:, pass_, :], r_, G[:, b, bass.ds(e, 1)],
                                      ALU.is_equal, ALU.mult).then_inc(m_s, 1)

            def tokens(n):
                dve.wait_ge(m_g, n + 1)
                dve.tensor_copy(xe.rearrange("p k s -> p (k s)"), ps[:, 7, :]).then_inc(m_x, 1)

            def hidden_e(n):
                dve.wait_ge(m_si, n + 1)
                dve.tensor_tensor(hid_e, silu_e, ps[:, 0, 256:512], ALU.mult).then_inc(m_hd, 1)

            select_e(0, 0)
            select_e(1, 1)
            tokens(0)
            with dve.Fori(0, NE // 2 - 1) as i:
                for b in range(2):
                    hidden_e(2 * i + b)
                    dve.wait_ge(m_t, 2 * i + b + 1)
                    select_e(2 * i + b + 2, b)
                    tokens(2 * i + b + 1)
            hidden_e(NE - 2)
            tokens(NE - 1)
            hidden_e(NE - 1)
            dve.wait_ge(m_flag, 1)
            more = dve.value_load(flag[0:1, 1:2].bitcast(I32), min_val=0, max_val=1)
            with dve.If(more > 0):
                with dve.Fori(0, NE) as e:
                    for p_ in range(3):
                        dve.wait_ge(m_t, 3 * e + NE + p_)
                        select_e(e, 0, p_ + 1)
                        tokens(3 * e + NE + p_)
                        hidden_e(3 * e + NE + p_)
                dve.wait_ge(m_all, 1 + 3 * NE)
            dve.wait_ge(m_all, 1)
            dve.wait_ge(m_out, 1)
            dve.tensor_copy(hn_tok[:, 0, 512:1024], ps[:, 3, :]).then_inc(m_out, 1)
            dve.wait_ge(m_out, 3)
            dve.tensor_copy(hn_tok[:, 1, 512:1024], ps[:, 5, :]).then_inc(m_out, 1)

        @block.tensor
        def _(pe):
            col = [0]

            def linear(p, by_token=False, arriving=None):
                pe.wait_ge(lo_done, p["w"] + 1)
                if p["half"] == 0 and p["engine_before"]:
                    pe.wait_ge(lin_out[p["engine_before"]], p["turn_before"])
                o, hi, lo = lin[p["out"] % 2][:, p["half"], :], piece_buf(p, 0), piece_buf(p, 1)
                blocks = range(TB) if by_token else range(1)
                for b in blocks:
                    for k in range(DC):
                        if arriving:
                            pe.wait_ge(arriving[0], arriving[1] + k + 1)
                        for n, (w_, x_) in enumerate(((hi, 0), (hi, 1), (lo, 0))):
                            first, last = k == 0 and n == 0, k == DC - 1 and n == 2
                            if by_token:
                                mm = pe.matmul(o[:, P * b:P * (b + 1)], u[:, x_, k, P * b:P * (b + 1)],
                                               w_[:, k, :], start=first, stop=last)
                            else:
                                mm = pe.matmul(o, w_[:, k, :], u[:, x_, k, :], start=first, stop=last)
                mm.then_inc(piece_done, 1)

            def linear_tokens(pair):
                p = pair[0]
                pe.wait_ge(lo_done, pair[1]["w"] + 1)
                if p["engine_before"]:
                    pe.wait_ge(lin_out[p["engine_before"]], p["turn_before"])
                first_buf = p["w"] % NBUF
                for b in range(TB):
                    for k in range(DC):
                        for n, (w_, x_) in enumerate(((0, 0), (0, 1), (1, 0))):
                            mm = pe.matmul(lin[p["out"] % 2][:, b, :].rearrange("p (c n) -> p c n", c=2),
                                           u[:, x_, k, P * b:P * (b + 1)],
                                           wsplit[:, first_buf:first_buf + 2, w_, P * k:P * (k + 1)],
                                           start=(k == 0 and n == 0), stop=(k == DC - 1 and n == 2))
                mm.then_inc(piece_done, 2)

            def column(g, signal=gemv_col):
                assert col[0] == g
                pe.wait_ge(gemv_sb, g + 1)
                for m in range(2):
                    mm = pe.matmul(modps[:, 2 * g + m:2 * g + m + 1], gsb[:, g % 2, P * m:P * (m + 1)],
                                   ones[:, 0:1], start=True, stop=True)
                mm.then_inc(signal, 1)
                col[0] += 1

            def gemv(some):
                for s in some:
                    g = gemv_of[s["n"]]
                    if g in (8, 24):
                        pe.wait_ge(mod_done, {8: 1, 24: 3}[g])
                    if g >= 2:
                        pe.wait_ge(gemv_sb, g - 1)
                    pe.wait_ge(slot_in[s["n"] % RING], slot_use(s["n"]))
                    w_ = slot_dst(s)
                    for k in range(DC):
                        j = k % 4
                        mm = pe.matmul(gps(g)[32 * j:32 * j + 32, :], cact[:, k, :], w_[:, k, :],
                                       start=(k < 4), stop=(k >= 4))
                    if col[0] < g:
                        column(g - 1, gemv_mm)
                    else:
                        mm.then_inc(gemv_mm, 1)

            def sums(name, some=range(4)):
                for n in some:
                    pe.wait_ge(sq_done, 4 * STATS[name] + n + 1)
                    if n == 0 and STATS[name] > 0:
                        pe.wait_ge(std_done, STATS[name])
                    for k in (2 * n, 2 * n + 1):
                        for b in range(TB):
                            mm = pe.matmul(stps[:, b:b + 1], sq[:, k, P * b:P * (b + 1)], ones[:, 0:1],
                                           start=(k == 0 and b == 0), stop=(k == DC - 1), skip_group_check=True)
                            if name == "mix_2":
                                mm = pe.matmul(stps[:, 2 + b:3 + b], sq_final[:, k, P * b:P * (b + 1)],
                                               ones[:, 0:1], start=False, stop=(k == DC - 1),
                                               skip_group_check=True)
                    if n == 3:
                        mm.then_inc(sum_done, 1)

            def project(job, name, arriving):
                for n, pair in enumerate(pairs(job)):
                    linear(pair[0], arriving=arriving if n == 0 else None)
                    linear(pair[1])
                    if n > 0:
                        sums(name, [n - 1])
                sums(name, [3])

            def spread(name):
                i = STATS[name]
                pe.wait_ge(diag_done, 2 * i + 2)
                if i > 0:
                    pe.wait_ge(scaled, 8 * SCALED_BEFORE[name])
                for b in range(TB):
                    mm = pe.matmul(rbc[:, P * b:P * (b + 1)], ones[:], diag[:, b, :], start=True, stop=True)
                mm.then_inc(bc_done, 1)

            pe.wait_ge(const_done, 4)
            pe.wait_ge(ld_c, 16)
            pe.transpose(ps[:, 1, 384:384 + DC], c_row, ident[0:DC, 0:DC]).then_inc(c_t, 1)
            pe.wait_ge(act_order, 1)
            gemv(jobs["gemv_first"][:4])
            pe.wait_ge(ld_vec, 16 * 21)
            pe.transpose(ps[:, 0, 0:112], rows1[0:112, :], ident[0:112, 0:112]).then_inc(setup_t, 1)
            pe.transpose(ps[:, 1, 0:ROWS2], rows2[0:ROWS2, :], ident[0:ROWS2, 0:ROWS2]).then_inc(setup_t, 1)
            pe.wait_ge(ld_x, 16)
            for c_ in range(DC):
                for b in range(TB):
                    mm = pe.transpose(acc[:, c_, P * b:P * (b + 1)], x_tok[:, b, P * c_:P * (c_ + 1)], ident[:])
                if c_ % 4 == 3:
                    mm.then_inc(setup_t, 1)
            gemv(jobs["gemv_first"][4:])
            column(7)
            sums("mix0")
            spread("mix0")
            pe.wait_ge(setup_c, 2)
            for n, p in enumerate(jobs["zf"] + jobs["q"]):
                linear(p, arriving=(u_lo, 0) if n == 0 else None)

            def round_(r):
                q_, k_ = (qA, kA) if r == 0 else (qd, kd)
                if r == 0:
                    pe.wait_ge(a_prep, 17)
                    wait_out(pe, jobs["q"][-1])
                    pe.wait_ge(setup_c, 4)
                else:
                    pe.wait_ge(a_dec, 2 * r)
                for b in range(4):
                    if r > 0:
                        pe.wait_ge(a_cp, 4 * (r - 1) + b + 1)
                    for n in range(4):
                        hh, tb = 2 * b + n // 2, n % 2
                        mm = pe.matmul(ps[:, 2 + b, P * n:P * (n + 1)], k_[:, hh, P * tb:P * (tb + 1)],
                                       q_[:, hh, P * tb:P * (tb + 1)], start=True, stop=True)
                    mm.then_inc(a_mm, 1)

            for r in range(8):
                pair = jobs[("v" if r < 4 else "g") + str(r)]
                gemv(jobs[f"gemv_round{r}"][0:1])
                if r < 4:
                    linear_tokens(pair)
                else:
                    linear(pair[0])
                gemv(jobs[f"gemv_round{r}"][1:2])
                if r >= 4:
                    linear(pair[1])
                round_(r)
            column(23)
            pe.wait_ge(a_dec, 16)
            for b in range(2):
                pe.wait_ge(a_cp, 28 + b + 1)
                for n in range(4):
                    mm = pe.matmul(ps[:, 2 + b, P * n:P * (n + 1)], kd[:, 4 * b + n, 0:P], qd[:, 4 * b + n, P:T],
                                   start=True, stop=True)
                mm.then_inc(a_mm, 1)
            pe.wait_ge(a_x, 2)
            pe.wait_ge(a_cp, 32)
            for hh in range(HA):
                pe.matmul(acc[:, hh, :], vA[:, 0, P * hh:P * (hh + 1)], attA[:, hh, 0:2, :], start=True, stop=False)
                pe.matmul(acc[:, hh, P:T], vA[:, 1, P * hh:P * (hh + 1)], attA[:, hh, 2, :], start=False,
                          stop=True).then_inc(a_o, 1)
            for hh in range(HA):
                pe.wait_ge(a_sq, hh // 2 + 1)
                for b in range(TB):
                    mm = pe.matmul(stps[:, 2 * hh + b:2 * hh + b + 1], sq[:, hh, P * b:P * (b + 1)], ones[:, 0:1],
                                   start=True, stop=True)
            mm.then_inc(a_ss, 1)
            wait_out(pe, jobs["g7"][-1])
            for hh in range(HA):
                if hh >= 4:
                    pe.wait_ge(a_g, 1)
                for b in range(TB):
                    pe.wait_ge(a_diag, 2 * hh + b + 1)
                    pe.matmul(lin[hh % 4 // 2][:, hh % 2, P * b:P * (b + 1)], ones[:], diag[:, (2 * hh + b) % 4, :],
                              start=True, stop=True).then_inc(a_bc, 1)
            pe.wait_ge(a_g, 2)
            pe.wait_ge(a_lo, 2)
            project("a_out", "ffn0", None)

            def ffn_pe(layer, name):
                spread(name)
                for i in range(FFI + 1):
                    if i < FFI:
                        for n, p in enumerate(jobs[f"gate{layer}_{i}"] + jobs[f"up{layer}_{i}"]):
                            linear(p, arriving=(u_lo, 8 * OPERANDS[name]) if i == 0 and n == 0 else None)
                    if i > 0:
                        fi = layer * FFI + i - 1
                        pe.wait_ge(f_lo, fi + 1)
                        for p in jobs[f"down{layer}_{i - 1}"]:
                            pe.wait_ge(lo_done, p["w"] + 1)
                            for jj in range(4):
                                c_ = 4 * p["half"] + jj
                                for k in range(2):
                                    for n, (lo, x_) in enumerate(((0, 0), (0, 1), (1, 0))):
                                        mm = pe.matmul(acc[:, c_, :], piece_buf(p, lo)[:, k, P * jj:P * (jj + 1)],
                                                       hid[:, fi % 2, x_, k, :],
                                                       start=(i == 1 and c_ % 2 == 0 and k == 0 and n == 0),
                                                       stop=(i == FFI and k == 1 and n == 2),
                                                       skip_group_check=True)
                            mm.then_inc(piece_done, 1)
                    if layer == 0:
                        gemv(jobs[f"gemv_ffn{i}"])

            ffn_pe(0, "ffn0")
            column(NG - 1)
            def attention_pe(kind, keys, queries, values, chunks, bias=None):
                first, n = FIRST[kind], COUNT[kind]

                def scores(i):
                    a = first + i
                    if i >= 2 and kind == "W":
                        pe.wait_ge(at_b, before_b(a - 1))
                    elif i >= 2:
                        pe.wait_ge(at_e, 2 * (a - 1))
                    o = ps[:, 2 + i % 2, :]
                    if bias:
                        pe.matmul(o[:, 0:3 * P], flip[:], bias(i), start=True, stop=False)
                    for block_ in range(TB):
                        at, w = ((0, 256), (256, 256))[block_] if kind == "X" else ((0, 128), (128, 256))[block_]
                        for k in range(chunks):
                            mm = pe.matmul(o[:, at:at + w], queries(i, k)[:, P * block_:P * (block_ + 1)],
                                           keys(i, k)[:, 0:w], start=(k == 0 and not bias),
                                           stop=(k == chunks - 1 and not (bias and block_ == 0)))
                    mm.then_inc(at_s, 1)

                def turn_(i):
                    a = first + i
                    pe.wait_ge(at_p, 3 * a + 3)
                    if i >= 2:
                        pe.wait_ge(at_pt, a - 1)
                    for at, place in blocks(kind):
                        mm = pe.transpose(ps[:, 4 + i % 2, P * place:P * (place + 1)],
                                          pr_sb[:, i % 2, at:at + P], ident[:])
                    mm.then_inc(at_t, 1)

                def outputs(i):
                    a = first + i
                    k, bank_ = o_bank(kind, i)
                    pe.wait_ge(at_pt, a + 1)
                    if k - {"B": 0, "W": 8, "X": 12}[kind] >= 2:
                        pe.wait_ge(at_hi, k - 1)
                        if kind != "W":
                            pe.wait_ge(at_lo, lo_before(k - 1))
                    pt = pt_sb[:, i % 2, :]
                    if kind == "X":
                        for m in range(2):
                            for b in range(TB):
                                mm = pe.matmul(bank_[:, T * m:T * (m + 1)], values(i, b, m), pt[:, T * b:T * (b + 1)],
                                               start=(b == 0), stop=(b == 1))
                    else:
                        rows = slice(64 * (i % 2), 64 * (i % 2) + 64)
                        pe.matmul(bank_[rows, 0:T], values(i, 0, 0), pt[:, 0:T], start=True, stop=False)
                        mm = pe.matmul(bank_[rows, P:T], values(i, 1, 0), pt[:, T:T + P], start=False, stop=True)
                    mm.then_inc(at_o, 1)

                scores(0)
                scores(1)
                for i in range(n + 1):
                    if i < n:
                        turn_(i)
                    if i + 2 < n:
                        scores(i + 2)
                    if i >= 1:
                        outputs(i - 1)

            sums("kv")
            pe.wait_ge(b_rel, 48)
            pe.wait_ge(acc_done, 8)
            for r, n in enumerate((P, P, NREL - 2 * P)):
                mm = pe.transpose(ps[0:HB, 2, P * r:P * r + n], rel_rows[0:n, r, :], ident[0:n, 0:n])
            mm.then_inc(b_relt, 1)
            spread("kv")
            for n, p in enumerate(jobs["kv_k"]):
                linear(p, arriving=(u_lo, 16) if n == 0 else None)
            for pair in pairs("kv_v"):
                linear_tokens(pair)
            for n, p in enumerate(jobs["b_q"]):
                linear(p, arriving=(u_lo, 24) if n == 0 else None)
            wait_out(pe, jobs["b_q"][-1])
            pe.wait_ge(b_rel, 96)
            pe.wait_ge(b_bias, 2)
            half = lambda t_, i: t_[64 * (i % 2):64 * (i % 2) + 64, i // 2, :]
            attention_pe("B", lambda i, k: half(kB, i), lambda i, k: half(qB, i),
                         lambda i, b, m: vB[:, b, 64 * i:64 * i + 64], 1, lambda i: biasB[:, i, :])
            pe.wait_ge(at_lo, HB // 2)
            project("b_o", "ffn1", None)
            ffn_pe(1, "ffn1")

            pe.wait_ge(fin_sq, 8)
            sums("mix_2")
            spread("mix_2")
            pe.wait_ge(w_ms, 8)
            pe.wait_ge(acc_done, 16)
            for g in range(8):
                mm = pe.transpose(ps[:, 2 + g // 4, P * (g % 4):P * (g % 4 + 1)], wRow[:, g, :], ident[:])
                if g % 4 == 3:
                    mm.then_inc(w_tp, 1)
            for n, p in enumerate(jobs["in2"][:8]):
                linear(p, by_token=(n == 5), arriving=(u_lo, 40) if n == 0 else None)
                if n == 0:
                    pe.wait_ge(fin, 7)
                    for b in range(TB):
                        mm = pe.matmul(ps[:, 4, P * b:P * (b + 1)], ones[:], diag[:, 2 + b, :], start=True,
                                       stop=True)
                    mm.then_inc(fin, 1)
            pe.wait_ge(w_sq, 3)
            pe.wait_ge(w_tc, 2)
            for c_ in range(4):
                for b in range(TB):
                    pe.matmul(stps[:, 4 * c_ + b:4 * c_ + b + 3:2], sq[:, c_, P * b:P * (b + 1)],
                              pair_ones[:, 0:P:64], start=True, stop=True)
            pe.matmul(acc[:, 0, :], pair_ones[:], sq[:, 4, :], start=True, stop=True).then_inc(w_ss, 1)
            for p in jobs["in2"][8:10]:
                linear(p)
            linear_tokens(pairs("in2")[5])
            pe.wait_ge(w_std, 2)
            pe.wait_ge(w_n, 2)
            for kv in range(2):
                for hf in range(2):
                    mm = pe.matmul(acc[64 * hf:64 * hf + 64, kv, :], ident[:, 64 * kv:64 * kv + 64], kW,
                                   start=True, stop=True)
            mm.then_inc(w_dup, 1)
            linear_tokens(pairs("in2")[6])
            pe.wait_ge(w_n, 4)
            for g in range(8):
                for b in range(TB):
                    o = acc[64 * (g % 2):64 * (g % 2) + 64, 4 + g // 2, P * b:P * (b + 1)]
                    pe.matmul(o, gn[:, b, 64 * g:64 * g + 64], wT[:, g, :], start=True, stop=False)
                    mm = pe.matmul(o, ones[0:1, 0:64], sgb[:, P * g:P * (g + 1)], start=False, stop=True)
                if g % 4 == 3:
                    mm.then_inc(w_s, 1)
            pe.wait_ge(w_dc, 1)
            pe.wait_ge(w_sg, 2)
            attention_pe("W", lambda i, k: kdup[64 * (i % 2):64 * (i % 2) + 64, i // 4, :],
                         lambda i, k: half(qW, i), lambda i, b, m: vW[:, b, 64 * (i // 4):64 * (i // 4) + 64], 1)
            pe.wait_ge(w_sq, 6)
            for b in range(2):
                for k in range(4):
                    mm = pe.matmul(ps[:, 6, T * b:T * (b + 1)], ones[:], sq[:, 4 * b + k, :], start=(k == 0),
                                   stop=(k == 3))
            mm.then_inc(w_ss, 1)
            for n, p in enumerate(jobs["out2"]):
                linear(p, arriving=(u_lo, 48) if n == 0 else None)

            pe.wait_ge(ld_mem, 16)
            for c_ in range(DC):
                for b in range(TB):
                    mm = pe.transpose(acc[:, c_, P * b:P * (b + 1)], mem_tok[:, b, P * c_:P * (c_ + 1)], ident[:])
                if c_ % 4 == 3:
                    mm.then_inc(x_tp, 1)
            sums("mem")
            spread("mem")
            for n, p in enumerate(jobs["ck"]):
                linear(p, arriving=(u_lo, 56) if n == 0 else None)
            for n, pair in enumerate(pairs("cv")):
                linear_tokens(pair)
                if n == 0:
                    pe.wait_ge(x_sq, 4)
                    for hh in range(HX):
                        for k in range(2):
                            mm = pe.matmul(acc[:, hh, :], ones[:], raw[:, 2 * hh + k, :], start=(k == 0),
                                           stop=(k == 1))
                    mm.then_inc(x_ss, 1)
            sums("cross")
            spread("cross")
            for n, p in enumerate(jobs["cq"]):
                linear(p, arriving=(u_lo, 64) if n == 0 else None)
            pe.wait_ge(x_sq, 8)
            for hh in range(HX):
                for b in range(TB):
                    for k in range(2):
                        mm = pe.matmul(stps[:, 2 * hh + b:2 * hh + b + 1], sq[:, 2 * hh + k, P * b:P * (b + 1)],
                                       ones[:, 0:1], start=(k == 0), stop=(k == 1))
            mm.then_inc(x_ss, 1)
            pe.wait_ge(x_n, 2)
            wait_out(pe, jobs["cq"][-1])
            pe.wait_ge(x_std, 1)
            attention_pe("X", lambda i, k: kX[:, 2 * i + k, :], lambda i, k: qX[:, 2 * i + k, :],
                         lambda i, b, m: vX[:, b, T * i + P * m:T * i + P * (m + 1)], 2)
            pe.wait_ge(at_lo, 12)
            project("co", "moe", None)
            spread("moe")
            pe.wait_ge(m_hn, 8)
            for b in range(TB):
                for c_ in range(DC):
                    mm = pe.transpose(ps[:, 2 + 2 * b + c_ // 4, P * (c_ % 4):P * (c_ % 4 + 1)],
                                      sq[:, c_, P * b:P * (b + 1)], ident[:])
                mm.then_inc(m_tok, 1)
            pe.wait_ge(m_wr, 80)
            for b in range(TB):
                for k in range(DC):
                    mm = pe.matmul(ps[:, 6, 36 * b:36 * (b + 1)], sq[:, k, P * b:P * (b + 1)], wr[:, k, :],
                                   start=(k == 0), stop=(k == DC - 1))
            mm.then_inc(m_log, 1)
            pe.wait_ge(m_tokc, 1)
            for b in range(TB):
                for c_ in range(DC):
                    pe.matmul(ps[:, 2 + 2 * b + c_ // 4, P * (c_ % 4):P * (c_ % 4 + 1)],
                              h[:, c_, P * b:P * (b + 1)], ident[:], start=(c_ % 4 == 0), stop=False,
                              skip_group_check=True)
            pe.wait_ge(route, ROUTED)
            pe.matmul(ps[:, 6, 128:160], tri, M1[:, 0, :], start=True, stop=True)
            pe.matmul(ps[:, 6, 160:192], tri, M1[:, 1, :], start=True, stop=False)
            pe.matmul(ps[:, 6, 160:192], ones[:], M1[:, 0, :], start=False, stop=True)
            pe.matmul(ps[:, 6, 192:224], ones[:], M1[:, 0, :], start=True, stop=False)
            pe.matmul(ps[:, 6, 192:224], ones[:], M1[:, 1, :], start=False, stop=True).then_inc(m_rank, 1)

            def gather(n, k):
                pe.wait_ge(m_s, 4 * n + 4)
                for c_ in range(DC):
                    for b in range(TB):
                        mm = pe.matmul(ps[:, 7, CAP * c_:CAP * (c_ + 1)], hn_tok[:, b, P * c_:P * (c_ + 1)],
                                       sel[:, k, b, :], start=(b == 0), stop=(b == TB - 1))
                mm.then_inc(m_g, 1)

            def up(n, k, loaded):
                pe.wait_ge(m_x, n + 1)
                pe.wait_ge(w13_in[k], loaded)
                for m in range(2):
                    for c_ in range(DC):
                        for j in range(2):
                            mm = pe.matmul(ps[64 * j:64 * j + 64, 0, 256 * m:256 * (m + 1)], xe[:, c_, :],
                                           w13[k][:, m, c_, 256 * j:256 * (j + 1)], start=(c_ == 0),
                                           stop=(c_ == DC - 1))
                mm.then_inc(m_h, 1)

            def turn_e(n, k):
                pe.wait_ge(m_hd, n + 1)
                for m in range(2):
                    pe.transpose(ps[:, 1, P * m:P * (m + 1)], hid_e[:, P * m:P * (m + 1)], ident[:])
                for b in range(TB):
                    mm = pe.transpose(ps[:, 1, 256 + P * b:256 + P * (b + 1)], gate_sel[:, k, b, :], ident[:])
                mm.then_inc(m_t, 1)

            def down(n, k, loaded):
                pe.wait_ge(m_tc, n + 1)
                pe.wait_ge(w2_in[k], loaded)
                for m in range(2):
                    for jk in range(2):
                        for j in range(2):
                            mm = pe.matmul(ps[64 * j:64 * j + 64, 6, :], tt[:, P * m + 64 * jk:P * m + 64 * jk + 64],
                                           w2b[k][:, 2 * jk + m, 512 * j:512 * (j + 1)],
                                           start=(m == 0 and jk == 0), stop=(m == 1 and jk == 1))
                mm.then_inc(m_y, 1)

            def scatter(n):
                pe.wait_ge(m_yc, n)
                for b in range(TB):
                    for j in range(2):
                        mm = pe.matmul(ps[:, 2 + 2 * b + j, :], tt[64 * j:64 * j + 64, 256 + P * b:256 + P * (b + 1)],
                                       y_sb[64 * j:64 * j + 64, :], start=False, stop=False, skip_group_check=True)
                return mm

            def middle(n, k, loaded, last=False):
                up(n, k, loaded)
                scatter(n)
                turn_e(n, k)
                if not last:
                    gather(n + 1, 1 - k)
                down(n, k, loaded // 2)

            pe.wait_ge(route, ROUTED + 4)
            pe.wait_ge(m_tokc, 1)
            gather(0, 0)
            up(0, 0, 32)
            turn_e(0, 0)
            gather(1, 1)
            down(0, 0, 16)
            with pe.Fori(0, NE // 2 - 1) as i:
                middle(2 * i + 1, 1, 32 * i + 32)
                middle(2 * i + 2, 0, 32 * i + 64)
            middle(NE - 1, 1, 16 * NE, last=True)
            scatter(NE).then_inc(m_all, 1)
            pe.wait_ge(m_flag, 1)
            more = pe.value_load(flag[0:1, 1:2].bitcast(I32), min_val=0, max_val=1)
            with pe.If(more > 0):
                with pe.Fori(0, NE) as e:
                    for p_ in range(3):
                        n = 3 * e + NE + p_
                        gather(n, 0)
                        up(n, 0, 32 * e + 16 * NE + 32)
                        turn_e(n, 0)
                        down(n, 0, 16 * e + 8 * NE + 16)
                        scatter(n + 1).then_inc(m_all, 1)


_INPUTS = ["x", "c", "mod_w", "mod_b", "norm_mix", "norm_ffn", "ffn_w_in", "ffn_w_out", "a_w_in", "a_w_out",
           "a_lb", "a_out_norm", "kv_norm", "kv_mod_w", "kv_mod_b", "kv_w", "b_w_q", "b_w_o", "b_rel_bias",
           "final_norm", "mem_2", "norm_mix_2", "w_in_2", "q_norm_2", "k_norm_2", "attn_sinks_2",
           "sgu_norm_2", "sgu_w_2", "sgu_b_2", "out_norm_attn_2", "out_norm_sgu_2", "w_out_2",
           "norm_cross_2", "norm_mem_2", "w_cq_2", "w_ck_2", "w_cv_2", "cq_norm_2", "ck_norm_2", "w_co_2",
           "norm_ffn_2", "w_router_group_2", "w_router_expert_2", "w1_2", "w3_2", "w2_2"]


def kernel(**inputs):
    import numpy as np
    from concourse import bacc
    from concourse.bass_utils import run_bass_kernel_spmd

    nc = bacc.Bacc("TRN2", target_bir_lowering=False, num_devices=1)
    arrays, args = {}, []
    for name in _INPUTS:
        array = np.ascontiguousarray(inputs[name])
        arrays[f"in_{name}"] = array
        args.append(nc.dram_tensor(f"in_{name}", array.shape, mybir.dt.from_np(array.dtype),
                                   kind="ExternalInput").ap())
    out = nc.dram_tensor("out_0", (1, T, D), F32, kind="ExternalOutput")
    two_blocks(nc, *args, out.ap())
    result = run_bass_kernel_spmd(nc, [arrays], core_ids=[0])
    return result.results[0]["out_0"]
```
